# Optimizing a Trainium2 kernel written in Bass

```python
import jax
import jax.numpy as jnp
from jax import lax
import numpy as np

D_MODEL = 1024
BATCH = 1
SEQ = 512
DEPTH = 1
DEC_BATCH = 8
DEC_SEQ = 1
PAST_LEN = 1024
PAGE_SIZE = 128

HEAD_DIM = 64
POOL_WINDOWS = (2, 4, 8, 16)
POOL_WIDTH = D_MODEL // 4
POOL_GROUP = POOL_WIDTH // len(POOL_WINDOWS)
POOL_STATE = max(POOL_WINDOWS) - 1
NSA_WIDTH = D_MODEL // 2
NSA_HEADS = NSA_WIDTH // HEAD_DIM
NSA_KV_HEADS = 2
NSA_REP = NSA_HEADS // NSA_KV_HEADS
N_BRANCH = 3
CMP_BLOCK = 32
CMP_STRIDE = 16
CMP_HIDDEN = 2 * HEAD_DIM
SEL_BLOCK = 64
SEL_TOPK = 16
CMP_PER_SEL = SEL_BLOCK // CMP_STRIDE
WINDOW = 512
FORCE_BONUS = 1000.0
MEM_LEN = 256
MEM_WIDTH = D_MODEL - POOL_WIDTH - NSA_WIDTH
MEM_HEADS = 4
MEM_HEAD_DIM = MEM_WIDTH // MEM_HEADS
ROPE_DIM = HEAD_DIM // 4
ROPE_THETA = 500000.0
N_EXPERT_GROUPS = 4
EXPERTS_PER_GROUP = 8
TOP_K_INNER = 2
EXPERT_FF = 512
Q_BLOCK = 128
N_KV_SLOTS = 4
NSA_KV_WIDTH = N_BRANCH * 2 * NSA_KV_HEADS * HEAD_DIM
GATE_WIDTH = NSA_HEADS * N_BRANCH
IN_WIDTH = POOL_WIDTH + NSA_WIDTH + NSA_KV_WIDTH + GATE_WIDTH + MEM_WIDTH
EPS = 1e-6

kernel_name = 'hybrid_pool_nsa_hmoe_decode_step'

def rmsnorm(x, g):
    xf = x.astype(jnp.float32)
    y = xf * lax.rsqrt(jnp.mean(xf * xf, axis=-1, keepdims=True) + EPS)
    return (y * g.astype(jnp.float32)).astype(x.dtype)

def rope_partial(x, pos):
    half = ROPE_DIM // 2
    inv = jnp.power(ROPE_THETA, -jnp.arange(half, dtype=jnp.float32) * 2.0 / ROPE_DIM)
    ang = pos.astype(jnp.float32)[:, None] * inv[None, :]
    shape = (ang.shape[0],) + (1,) * (x.ndim - 3) + (half,)
    cos = jnp.cos(ang).reshape(shape)
    sin = jnp.sin(ang).reshape(shape)
    xf = x.astype(jnp.float32)
    x1 = xf[..., :half]
    x2 = xf[..., half:ROPE_DIM]
    out = jnp.concatenate([x1 * cos - x2 * sin, x2 * cos + x1 * sin, xf[..., ROPE_DIM:]], axis=-1)
    return out.astype(x.dtype)

def masked_softmax(s, mask):
    s = jnp.where(mask, s.astype(jnp.float32), -jnp.inf)
    m = jnp.max(s, axis=-1, keepdims=True)
    m = jnp.where(jnp.isfinite(m), m, 0.0)
    e = jnp.where(mask, jnp.exp(s - m), 0.0)
    return e / jnp.maximum(jnp.sum(e, axis=-1, keepdims=True), 1e-30)

def project(xn, pos, p):
    b, t, _ = xn.shape
    z = xn @ p['w_in']
    o1 = POOL_WIDTH
    o2 = o1 + NSA_WIDTH
    o3 = o2 + NSA_KV_WIDTH
    o4 = o3 + GATE_WIDTH
    u = z[..., :o1]
    q = rmsnorm(z[..., o1:o2].reshape(b, t, NSA_HEADS, HEAD_DIM), p['g_q'])
    q = rope_partial(q, pos).reshape(b, t, NSA_KV_HEADS, NSA_REP, HEAD_DIM)
    kv = z[..., o2:o3].reshape(b, t, N_BRANCH, 2, NSA_KV_HEADS, HEAD_DIM)
    k = rope_partial(rmsnorm(kv[:, :, :, 0], p['g_k'][:, None, :]), pos)
    v = kv[:, :, :, 1]
    rows4 = jnp.stack([k[:, :, 0], v[:, :, 0], k[:, :, 1], v[:, :, 1]], axis=2)
    rows_w = jnp.stack([k[:, :, 2], v[:, :, 2]], axis=2)
    gates = jax.nn.sigmoid(z[..., o3:o4].astype(jnp.float32)).astype(xn.dtype)
    gates = gates.reshape(b, t, NSA_KV_HEADS, NSA_REP, N_BRANCH)
    qm = rmsnorm(z[..., o4:].reshape(b, t, MEM_HEADS, MEM_HEAD_DIM), p['g_mq'])
    return u, q, rows4, rows_w, gates, qm

def pool_mix(u, prev, pos0, p):
    b, t, _ = u.shape
    ext = jnp.concatenate([prev, u], axis=1).astype(jnp.float32)
    cs = jnp.concatenate([jnp.zeros_like(ext[:, :1]), jnp.cumsum(ext, axis=1)], axis=1)
    pos = pos0 + jnp.arange(t, dtype=jnp.int32)
    means = []
    for gi, w in enumerate(POOL_WINDOWS):
        sl = slice(gi * POOL_GROUP, (gi + 1) * POOL_GROUP)
        hi = cs[:, POOL_STATE + 1:POOL_STATE + 1 + t, sl]
        lo = cs[:, POOL_STATE + 1 - w:POOL_STATE + 1 - w + t, sl]
        cnt = jnp.minimum(pos + 1, w).astype(jnp.float32)[None, :, None]
        means.append((hi - lo) / cnt)
    mean = jnp.concatenate(means, axis=-1).astype(u.dtype)
    r = (mean - u).reshape(b, t, len(POOL_WINDOWS), POOL_GROUP)
    y = jnp.einsum('btgc,gcd->btgd', r, p['w_pool']).reshape(b, t, POOL_WIDTH)
    return y * p['s_pool']

def compress_blocks(rows, pe, w1, w2):
    b, l, g, d = rows.shape
    n_chunk = -(-l // CMP_STRIDE)
    rows = jnp.pad(rows, ((0, 0), (0, n_chunk * CMP_STRIDE - l), (0, 0), (0, 0)))
    chunks = rows.reshape(b, n_chunk, CMP_STRIDE, g, d)
    blocks = jnp.concatenate([chunks[:, :-1], chunks[:, 1:]], axis=2)
    blocks = blocks + pe[None, None, :, None, :]
    flat = jnp.moveaxis(blocks, 3, 2).reshape(b, n_chunk - 1, g, CMP_BLOCK * d)
    return jax.nn.gelu(flat @ w1) @ w2

def sel_blocks(rows):
    b, l, g, d = rows.shape
    ns = -(-l // SEL_BLOCK)
    rows = jnp.pad(rows, ((0, 0), (0, ns * SEL_BLOCK - l), (0, 0), (0, 0)))
    return rows.reshape(b, ns, SEL_BLOCK, g, d).transpose(0, 3, 1, 2, 4).reshape(b, g, ns, SEL_BLOCK * d)

def nsa_context(rows4, p):
    kc = compress_blocks(rows4[:, :, 0], p['pe_cmp'][0], p['w_cmp1'][0], p['w_cmp2'][0])
    vc = compress_blocks(rows4[:, :, 1], p['pe_cmp'][1], p['w_cmp1'][1], p['w_cmp2'][1])
    kc_end = jnp.arange(kc.shape[1], dtype=jnp.int32) * CMP_STRIDE + (CMP_BLOCK - 1)
    return kc, vc, kc_end, sel_blocks(rows4[:, :, 2]), sel_blocks(rows4[:, :, 3])

def nsa_core(q, q_pos, gates, kc, vc, kc_end, ks_blk, vs_blk, kw, vw, kw_pos):
    b, tq = q.shape[0], q.shape[1]
    scale = HEAD_DIM ** -0.5
    t = q_pos
    s_c = jnp.einsum('bqgrd,bkgd->bgrqk', q, kc) * scale
    p_c = masked_softmax(s_c, kc_end[None, :] <= t[:, None])
    o_c = jnp.einsum('bgrqk,bkgd->bqgrd', p_c.astype(vc.dtype), vc)
    ns = ks_blk.shape[2]
    nc = kc.shape[1]
    imp = jnp.sum(p_c, axis=2)
    imp = jnp.pad(imp, ((0, 0), (0, 0), (0, 0), (0, ns * CMP_PER_SEL - nc)))
    imp = imp.reshape(b, NSA_KV_HEADS, tq, ns, CMP_PER_SEL).sum(-1)
    blk = jnp.arange(ns, dtype=jnp.int32)[None, :]
    cur = (t // SEL_BLOCK)[:, None]
    valid = blk * SEL_BLOCK <= t[:, None]
    forced = (blk == 0) | (blk == cur) | (blk == cur - 1)
    score = jnp.where(valid, imp + jnp.where(forced, FORCE_BONUS, 0.0), -jnp.inf)
    n_top = min(SEL_TOPK, ns)
    top_s, idx = lax.top_k(score, n_top)
    bi = jnp.arange(b)[:, None, None, None]
    gi = jnp.arange(NSA_KV_HEADS)[None, :, None, None]
    k_sel = ks_blk[bi, gi, idx].reshape(b, NSA_KV_HEADS, tq, n_top * SEL_BLOCK, HEAD_DIM)
    v_sel = vs_blk[bi, gi, idx].reshape(b, NSA_KV_HEADS, tq, n_top * SEL_BLOCK, HEAD_DIM)
    k_pos = (idx[..., None] * SEL_BLOCK + jnp.arange(SEL_BLOCK, dtype=jnp.int32)).reshape(b, NSA_KV_HEADS, tq, n_top * SEL_BLOCK)
    mask_s = jnp.repeat(jnp.isfinite(top_s), SEL_BLOCK, axis=-1) & (k_pos <= t[:, None])
    s_s = jnp.einsum('bqgrd,bgqkd->bgrqk', q, k_sel) * scale
    p_s = masked_softmax(s_s, mask_s[:, :, None])
    o_s = jnp.einsum('bgrqk,bgqkd->bqgrd', p_s.astype(v_sel.dtype), v_sel)
    dist = t[:, None] - kw_pos[None, :]
    mask_w = (dist >= 0) & (dist < WINDOW) & (kw_pos[None, :] >= 0)
    s_w = jnp.einsum('bqgrd,bkgd->bgrqk', q, kw) * scale
    p_w = masked_softmax(s_w, mask_w)
    o_w = jnp.einsum('bgrqk,bkgd->bqgrd', p_w.astype(vw.dtype), vw)
    return gates[..., 0:1] * o_c + gates[..., 1:2] * o_s + gates[..., 2:3] * o_w

def memory_kv(mem, p):
    b, m, _ = mem.shape
    kv = (rmsnorm(mem, p['g_mem']) @ p['w_mem_kv']).reshape(b, m, 2, MEM_HEADS, MEM_HEAD_DIM)
    return jnp.stack([rmsnorm(kv[:, :, 0], p['g_mk']), kv[:, :, 1]], axis=2)

def mem_attend(qm, mem_kv):
    b, t = qm.shape[0], qm.shape[1]
    s = jnp.einsum('bqhd,bkhd->bhqk', qm, mem_kv[:, :, 0]).astype(jnp.float32) * MEM_HEAD_DIM ** -0.5
    pr = jax.nn.softmax(s, axis=-1).astype(mem_kv.dtype)
    return jnp.einsum('bhqk,bkhd->bqhd', pr, mem_kv[:, :, 1]).reshape(b, t, MEM_WIDTH)

def hier_moe(x, p):
    n = x.shape[0]
    l1 = (x @ p['w_router1']).astype(jnp.float32) + p['b_router1']
    p1 = jax.nn.softmax(l1, axis=-1)
    top1_p, grp = lax.top_k(p1, 1)
    grp = grp[:, 0]
    l2 = jnp.einsum('nd,dge->nge', x, p['w_router2']).astype(jnp.float32) + p['b_router2']
    l2 = l2[jnp.arange(n), grp]
    top_v, top_i = lax.top_k(l2, TOP_K_INNER)
    top_w = jax.nn.softmax(top_v, axis=-1) * top1_p
    inner = jnp.sum(jax.nn.one_hot(top_i, EXPERTS_PER_GROUP, dtype=jnp.float32) * top_w[..., None], axis=1)
    combine = (jax.nn.one_hot(grp, N_EXPERT_GROUPS, dtype=jnp.float32)[:, :, None] * inner[:, None, :]).astype(x.dtype)
    y = jnp.zeros_like(x)
    for gi in range(N_EXPERT_GROUPS):
        hg = jnp.einsum('nd,edf->nef', x, p['w_gate'][gi])
        hu = jnp.einsum('nd,edf->nef', x, p['w_up'][gi])
        h = jax.nn.silu(hg) * hu * combine[:, gi, :, None]
        y = y + jnp.einsum('nef,efd->nd', h, p['w_down'][gi])
    return y

def finish(x, y_pool, o_nsa, o_mem, p):
    b, t, d = x.shape
    g = p['g_mix']
    mixed = jnp.concatenate([
        rmsnorm(y_pool, g[:POOL_WIDTH]),
        rmsnorm(o_nsa, g[POOL_WIDTH:POOL_WIDTH + NSA_WIDTH]),
        rmsnorm(o_mem, g[POOL_WIDTH + NSA_WIDTH:])], axis=-1)
    h = x + mixed @ p['w_out']
    hn = rmsnorm(h, p['g_ffn']).reshape(b * t, d)
    return h + hier_moe(hn, p).reshape(b, t, d)

def layer_prompt(x, mem, p):
    b, t, _ = x.shape
    pos = jnp.arange(t, dtype=jnp.int32)
    u, q, rows4, rows_w, gates, qm = project(rmsnorm(x, p['g_attn']), pos, p)
    y_pool = pool_mix(u, jnp.zeros((b, POOL_STATE, POOL_WIDTH), u.dtype), 0, p)
    kc, vc, kc_end, ks, vs = nsa_context(rows4, p)
    kw_pad = jnp.pad(rows_w, ((0, 0), (WINDOW, 0), (0, 0), (0, 0), (0, 0)))
    n_chunks = t // Q_BLOCK

    def chunk(args):
        qc, gc, c = args
        start = c * Q_BLOCK
        kw = lax.dynamic_slice_in_dim(kw_pad, start, WINDOW + Q_BLOCK, axis=1)
        kw_pos = start - WINDOW + jnp.arange(WINDOW + Q_BLOCK, dtype=jnp.int32)
        q_pos = start + jnp.arange(Q_BLOCK, dtype=jnp.int32)
        return nsa_core(qc, q_pos, gc, kc, vc, kc_end, ks, vs, kw[:, :, 0], kw[:, :, 1], kw_pos)

    qs = jnp.swapaxes(q.reshape(b, n_chunks, Q_BLOCK, NSA_KV_HEADS, NSA_REP, HEAD_DIM), 0, 1)
    gs = jnp.swapaxes(gates.reshape(b, n_chunks, Q_BLOCK, NSA_KV_HEADS, NSA_REP, N_BRANCH), 0, 1)
    o = lax.map(chunk, (qs, gs, jnp.arange(n_chunks, dtype=jnp.int32)))
    o_nsa = jnp.swapaxes(o, 0, 1).reshape(b, t, NSA_WIDTH)
    mem_kv = memory_kv(mem, p)
    y = finish(x, y_pool, o_nsa, mem_attend(qm, mem_kv), p)
    keep = min(WINDOW, t)
    return y, rows4, rows_w[:, t - keep:], u[:, t - POOL_STATE:], mem_kv

def layer_sample(x, pool_prev, kv_pool, page_table, win_buf, mem_kv, p):
    b, t, _ = x.shape
    pos = PAST_LEN + jnp.arange(t, dtype=jnp.int32)
    u, q, rows4, rows_w, gates, qm = project(rmsnorm(x, p['g_attn']), pos, p)
    y_pool = pool_mix(u, pool_prev, PAST_LEN, p)
    past = kv_pool[page_table].reshape(b, -1, N_KV_SLOTS, NSA_KV_HEADS, HEAD_DIM)
    kc, vc, kc_end, ks, vs = nsa_context(jnp.concatenate([past, rows4], axis=1), p)
    n_buf = win_buf.shape[1]
    kw = jnp.concatenate([win_buf, rows_w], axis=1)
    kw_pos = PAST_LEN - n_buf + jnp.arange(n_buf + t, dtype=jnp.int32)
    o = nsa_core(q, pos, gates, kc, vc, kc_end, ks, vs, kw[:, :, 0], kw[:, :, 1], kw_pos)
    y = finish(x, y_pool, o.reshape(b, t, NSA_WIDTH), mem_attend(qm, mem_kv), p)
    pool_ext = jnp.concatenate([pool_prev, u], axis=1)
    return y, rows4, kw[:, t:], pool_ext[:, t:]

def setup_inputs(seed: int = 0) -> dict:
    key = jax.random.key(seed)
    keys = iter(jax.random.split(key, 40))

    def nrm(shape, scale):
        return jax.random.normal(next(keys), shape, jnp.float32) * scale

    def gain(shape):
        return 1.0 + 0.02 * jax.random.normal(next(keys), shape, jnp.float32)

    n_pages = PAST_LEN // PAGE_SIZE
    n_used = DEC_BATCH * n_pages
    n_phys = n_used + max(1, n_used // 4)
    n_win = min(WINDOW, PAST_LEN)
    g = NSA_KV_HEADS
    x_prompt = nrm((BATCH, SEQ, D_MODEL), 1.0)
    x_sample = nrm((DEC_BATCH, DEC_SEQ, D_MODEL), 1.0)
    cache_kv = nrm((DEPTH, n_phys, PAGE_SIZE, N_KV_SLOTS, g, HEAD_DIM), 1.0)
    cache_win = nrm((DEPTH, DEC_BATCH, n_win, 2, g, HEAD_DIM), 1.0)
    state_pool = nrm((DEPTH, DEC_BATCH, POOL_STATE, POOL_WIDTH), 1.0)
    cache_mem_kv = nrm((DEPTH, DEC_BATCH, MEM_LEN, 2, MEM_HEADS, MEM_HEAD_DIM), 1.0)
    page_table = jax.random.permutation(next(keys), n_phys)[:n_used].reshape(DEC_BATCH, n_pages).astype(jnp.int32)
    mem_prompt = nrm((BATCH, MEM_LEN, D_MODEL), 1.0)
    return {
        'x_prompt': x_prompt,
        'x_sample': x_sample,
        'cache_kv': cache_kv,
        'cache_win': cache_win,
        'state_pool': state_pool,
        'cache_mem_kv': cache_mem_kv,
        'page_table': page_table,
        'mem_prompt': mem_prompt,
        'g_attn': gain((DEPTH, D_MODEL)),
        'w_in': nrm((DEPTH, D_MODEL, IN_WIDTH), D_MODEL ** -0.5),
        'g_q': gain((DEPTH, HEAD_DIM)),
        'g_k': gain((DEPTH, N_BRANCH, HEAD_DIM)),
        'pe_cmp': nrm((DEPTH, 2, CMP_BLOCK, HEAD_DIM), 0.1),
        'w_cmp1': nrm((DEPTH, 2, CMP_BLOCK * HEAD_DIM, CMP_HIDDEN), (CMP_BLOCK * HEAD_DIM) ** -0.5),
        'w_cmp2': nrm((DEPTH, 2, CMP_HIDDEN, HEAD_DIM), CMP_HIDDEN ** -0.5),
        'w_pool': nrm((DEPTH, len(POOL_WINDOWS), POOL_GROUP, POOL_GROUP), POOL_GROUP ** -0.5),
        's_pool': gain((DEPTH, POOL_WIDTH)),
        'g_mem': gain((DEPTH, D_MODEL)),
        'w_mem_kv': nrm((DEPTH, D_MODEL, 2 * MEM_WIDTH), D_MODEL ** -0.5),
        'g_mq': gain((DEPTH, MEM_HEAD_DIM)),
        'g_mk': gain((DEPTH, MEM_HEAD_DIM)),
        'g_mix': gain((DEPTH, D_MODEL)),
        'w_out': nrm((DEPTH, D_MODEL, D_MODEL), D_MODEL ** -0.5),
        'g_ffn': gain((DEPTH, D_MODEL)),
        'w_router1': nrm((DEPTH, D_MODEL, N_EXPERT_GROUPS), D_MODEL ** -0.5),
        'b_router1': nrm((DEPTH, N_EXPERT_GROUPS), 0.01),
        'w_router2': nrm((DEPTH, D_MODEL, N_EXPERT_GROUPS, EXPERTS_PER_GROUP), D_MODEL ** -0.5),
        'b_router2': nrm((DEPTH, N_EXPERT_GROUPS, EXPERTS_PER_GROUP), 0.01),
        'w_gate': nrm((DEPTH, N_EXPERT_GROUPS, EXPERTS_PER_GROUP, D_MODEL, EXPERT_FF), D_MODEL ** -0.5),
        'w_up': nrm((DEPTH, N_EXPERT_GROUPS, EXPERTS_PER_GROUP, D_MODEL, EXPERT_FF), D_MODEL ** -0.5),
        'w_down': nrm((DEPTH, N_EXPERT_GROUPS, EXPERTS_PER_GROUP, EXPERT_FF, D_MODEL), EXPERT_FF ** -0.5),
    }

def reference(x_prompt, x_sample, cache_kv, cache_win, state_pool, cache_mem_kv, page_table, mem_prompt,
              g_attn, w_in, g_q, g_k, pe_cmp, w_cmp1, w_cmp2, w_pool, s_pool, g_mem, w_mem_kv, g_mq, g_mk,
              g_mix, w_out, g_ffn, w_router1, b_router1, w_router2, b_router2, w_gate, w_up, w_down):
    hp = x_prompt
    hs = x_sample
    kv_p, kv_s, win_p, win_s, pool_p, pool_s, mem_p = [], [], [], [], [], [], []
    for l in range(DEPTH):
        p = {
            'g_attn': g_attn[l], 'w_in': w_in[l], 'g_q': g_q[l], 'g_k': g_k[l],
            'pe_cmp': pe_cmp[l], 'w_cmp1': w_cmp1[l], 'w_cmp2': w_cmp2[l],
            'w_pool': w_pool[l], 's_pool': s_pool[l],
            'g_mem': g_mem[l], 'w_mem_kv': w_mem_kv[l], 'g_mq': g_mq[l], 'g_mk': g_mk[l],
            'g_mix': g_mix[l], 'w_out': w_out[l], 'g_ffn': g_ffn[l],
            'w_router1': w_router1[l], 'b_router1': b_router1[l],
            'w_router2': w_router2[l], 'b_router2': b_router2[l],
            'w_gate': w_gate[l], 'w_up': w_up[l], 'w_down': w_down[l],
        }
        hp, r4p, rwp, plp, mkv = layer_prompt(hp, mem_prompt, p)
        hs, r4s, rws, pls = layer_sample(hs, state_pool[l], cache_kv[l], page_table, cache_win[l], cache_mem_kv[l], p)
        kv_p.append(r4p)
        kv_s.append(r4s)
        win_p.append(rwp)
        win_s.append(rws)
        pool_p.append(plp)
        pool_s.append(pls)
        mem_p.append(mkv)
    return (hp, hs, jnp.stack(kv_p), jnp.stack(kv_s), jnp.stack(win_p), jnp.stack(win_s),
            jnp.stack(pool_p), jnp.stack(pool_s), jnp.stack(mem_p))


_drawn_inputs = setup_inputs


def setup_inputs(seed=0):
    import zlib

    import numpy as np

    out = dict(_drawn_inputs(seed))
    spreads = {}
    factors = {'g_attn': 2.839,
     'g_q': 5.566,
     'g_k': 3.561,
     's_pool': 3.939,
     'g_mem': 2.871,
     'g_mq': 4.832,
     'g_mk': 4.179,
     'g_ffn': 3.15,
     'b_router1': 7.516,
     'b_router2': 5.682}
    for name, (base, spread) in spreads.items():
        noise = np.random.default_rng([zlib.crc32(name.encode()), seed]).standard_normal(out[name].shape)
        drawn = base * np.exp(spread * noise) if base else spread * noise
        out[name] = jnp.asarray(drawn.astype(out[name].dtype))
    for name, factor in factors.items():
        out[name] = (out[name] * factor).astype(out[name].dtype)
    return out
```

```python
from contextlib import ExitStack

import concourse.bass as bass
from concourse import mybir

F32 = mybir.dt.float32
BF16 = mybir.dt.bfloat16
I32 = mybir.dt.int32
U32 = mybir.dt.uint32
ALU = mybir.AluOpType
ACT = mybir.ActivationFunctionType
AX = mybir.AxisListType

P = 128
D = 1024
KD = D // P
T = 512
NB = 8
PAST = 1024
PAGE = 128
HD = 64
R, G = 4, 2
H = R * G
MEM = 256
MH = 4
EPS = 1e-6
SCALE = HD ** -0.5
NEG = -1e30
WINDOWS = (2, 4, 8, 16)
STATE = 15
TILES = T // P
ROWS = [P] * TILES + [NB]
NC_P = T // 16 - 1
NC_S = PAST // 16 - 1
NSEQ = NB + 1

U0, Q0, K0, M0, V0, G0 = 0, 256, 768, 1152, 1408, 1792
ZW = 1816
ZC = ZW // 4
NG = (V0 - Q0) // HD

NEXP = 32
FF = 512
KF = FF // P
CAP = 64
NTOK = T + NB
NOVER = (2 * NTOK) // (CAP + 1)
NTILE = NEXP + NOVER
QMAX = (NTOK - 1) // CAP

C_ID = 0
C_CAUS = C_ID + P
C_CADD = C_CAUS + P
C_CMUL = C_CADD + TILES * 32
C_COS = C_CMUL + TILES * 32
C_SIN = C_COS + 5 * 8
C_UP = C_SIN + 5 * 8
C_ONE = C_UP + P
C_RG = C_ONE + P
C_S8 = C_RG + 64
C_BLK = C_S8 + NB
C_G4 = C_BLK + 14
C_E8 = C_G4 + 4
C_EI = C_E8 + 8
C_MAIN = C_EI + 32
C_TOK = C_MAIN + NOVER
CW = C_TOK + TILES + 1

C_BAND = 0
C_PST = C_BAND + 12 * P
C_PDG = C_PST + 4 * NB
BW = C_PDG + 4 * NB

def constants():
    import numpy as np
    c = np.zeros((P, CW), np.float32)
    i = np.arange(P)
    c[:, C_ID:C_ID + P] = np.eye(P)
    c[:, C_CAUS:C_CAUS + P] = np.where(i[None, :] <= i[:, None], 0.0, NEG)
    for t in range(TILES):
        ok = (np.arange(32)[None, :] * 16 + 31 <= (t * P + i)[:, None]) & (np.arange(32) < NC_P)[None, :]
        c[:, C_CADD + 32 * t:C_CADD + 32 * t + 32] = np.where(ok, 0.0, NEG)
        c[:, C_CMUL + 32 * t:C_CMUL + 32 * t + 32] = ok
    inv = np.power(np.float32(500000.0), -np.arange(8, dtype=np.float32) * np.float32(2.0) / np.float32(16))
    for t in range(5):
        pos = (t * P + i if t < TILES else np.full(P, PAST)).astype(np.float32)
        ang = pos[:, None] * inv[None, :]
        c[:, C_COS + 8 * t:C_COS + 8 * t + 8] = np.cos(ang)
        c[:, C_SIN + 8 * t:C_SIN + 8 * t + 8] = np.sin(ang)
    bands = np.zeros((P, BW), np.float32)
    for w, win in enumerate(WINDOWS):
        tin, tout = i[:, None], i[None, :]
        eye = (tin == tout).astype(np.float32)
        own = ((tin <= tout) & (tout - tin < win)) / np.float32(win) - eye
        before = ((tout + P - tin < win) & (tout + P - tin > 0)) / np.float32(win)
        first = ((tin <= tout) & (tout - tin < win)) / np.minimum(tout + 1, win).astype(np.float32) - eye
        for j, m in enumerate((own, before, first)):
            o = C_BAND + (3 * w + j) * P
            bands[:, o:o + P] = m
        for b in range(NB):
            for s in range(STATE):
                if s >= STATE - (win - 1):
                    bands[b * STATE + s, C_PST + w * NB + b] = 1.0 / win
            bands[b, C_PDG + w * NB + b] = 1.0 / win - 1.0
    c[:, C_UP:C_UP + P] = i[:, None] < i[None, :]
    c[:, C_ONE:C_ONE + P] = 1.0
    j = np.arange(64)
    c[:64, C_RG:C_RG + 64] = (j[:, None] // 8 == j[None, :] // 8) & (j[:, None] % 2 == j[None, :] % 2)
    c[:64, C_S8:C_S8 + NB] = j[:, None] // 8 == np.arange(NB)[None, :]
    c[:, C_BLK:C_BLK + 14] = np.arange(1, 15)
    c[:, C_G4:C_G4 + 4] = [4, 3, 2, 1]
    c[:, C_E8:C_E8 + 8] = np.arange(8, 0, -1)
    c[:, C_EI:C_EI + 32] = np.arange(32)
    c[:, C_MAIN:C_MAIN + NOVER] = np.arange(NOVER)
    c[:, C_TOK:C_TOK + 5] = i[:, None] + P * np.arange(5)[None, :]
    return c, bands


class Chain:

    def __init__(self, eng, sem):
        self.eng, self.sem, self.n = eng, sem, 0

    def then(self, ins):
        self.n += 1
        ins.then_inc(self.sem, 1)
        self.eng.wait_ge(self.sem, self.n)


class Kernel:
    def __init__(self, nc, ins, outs):
        self.nc, self.ins, self.outs = nc, ins, outs
        self.stack = ExitStack()
        self.n_sems, self.stage_sems = 0, []

    def sb(self, name, shape, dt=F32, stack=None):
        return (stack or self.stack).enter_context(self.nc.sbuf_tensor(name, shape, dt))

    def sem(self, name, stack):
        self.n_sems += 1
        s = self.nc.alloc_semaphore(f"{name}_{self.n_sems}")
        if stack is not self.stack:
            self.stage_sems.append(s)
        return s

    def close(self, stage):
        stage.close()
        self.nc.clear_and_free_semaphores(self.stage_sems)
        self.nc.all_engine_barrier()
        self.stage_sems = []

    def c(self, at, n, rows=P):
        return self.consts[0:rows, at:at + n]

    def project(self):
        nc, I, O = self.nc, self.ins, self.outs
        st = ExitStack()
        n_items = 7
        rows = ROWS + [P, P]
        w_in = self.sb("w_in", [P, KD, ZW], stack=st)
        w_mem = self.sb("w_mem", [P, KD, 512], stack=st)
        g_rows = self.sb("g_rows", [P, 2, D], stack=st)
        g_head = self.sb("g_head", [P, V0 - Q0 + HD * MH], stack=st)
        xin = self.sb("xin", [P, 3, D], stack=st)
        xn = self.sb("xn", [P, 2, D], stack=st)
        xT = self.sb("xT", [P, 2, KD, P], stack=st)
        junk = self.sb("junk", [P, 2, V0 - Q0], stack=st)
        stat = self.sb("stat", [P, n_items, 4], stack=st)
        gstat = self.sb("gstat", [P, n_items, NG], stack=st)
        rot = self.sb("rot", [P, 4, 14, 8], stack=st)
        blank = self.sb("blank", [CAP, D], stack=st)
        blank_ready = self.sem("blank_ready", st)
        S = lambda n: self.sem(n, st)
        consts_in, gains_in, win_in, wmem_in = S("consts_in"), S("gains_in"), S("win_in"), S("wmem_in")
        x_in = [S(f"x_in{j}") for j in range(3)]
        dve_step, act_step = S("dve_step"), S("act_step")
        xn_ready, xT_in_psum, xT_ready, z_in_psum, z_ready = (S(n) for n in (
            "xn_ready", "xT_in_psum", "xT_ready", "z_in_psum", "z_ready"))
        ms_ready, rms_ready, sq_ready, gms_ready, grms_ready, z_done, stored = (S(n) for n in (
            "ms_ready", "rms_ready", "sq_ready", "gms_ready", "grms_ready", "z_done", "stored"))
        pz, pt = self.pz, self.pt
        z, memz = self.z, self.sb("memz", [P, 2, 512], stack=st)
        xs = [I["x"][t * P:t * P + rows[t], :] for t in range(5)] + [I["mem"][j * P:(j + 1) * P, :] for j in range(2)]

        def zt(t):
            return z[:, t, :] if t < 5 else memz[:, t - 5, :]

        def groups(t):
            return (Q0, NG) if t < 5 else (0, MH)

        block = st.enter_context(nc.Block("project"))

        @block.sync
        def _(sp):
            sp.dma_start(xin[0:rows[0], 0, :], xs[0]).then_inc(x_in[0], 16)
            sp.dma_start(self.consts[:, :], I["consts"]).then_inc(consts_in, 16)
            sp.dma_start(g_rows[:, :, :], I["g_rows"].partition_broadcast(P)).then_inc(gains_in, 16)
            sp.dma_start(w_in[:, 0:4, :], I["w_in"].rearrange("(p k) n -> p k n", k=KD)[:, 0:4, :]).then_inc(win_in, 16)
            sp.dma_start(w_in[:, 4:8, :], I["w_in"].rearrange("(p k) n -> p k n", k=KD)[:, 4:8, :]).then_inc(win_in, 16)
            for t in range(1, n_items):
                if t >= 3:
                    sp.wait_ge(xn_ready, t - 2)
                sp.dma_start(xin[0:rows[t], t % 3, :], xs[t]).then_inc(x_in[t % 3], 16)
                if t == 1:
                    sp.dma_start(g_head[:, :], I["g_head"].partition_broadcast(P)).then_inc(gains_in, 16)
                    sp.dma_start(w_mem[:, :, :], I["w_mem"].rearrange("(p k) n -> p k n", k=KD)).then_inc(wmem_in, 16)
            k3 = lambda t, r: z[0:r, t, K0:K0 + 384].rearrange("p (b c) -> p b c", b=3)
            v3 = lambda t, r: z[0:r, t, V0:V0 + 384].rearrange("p (b c) -> p b c", b=3)
            for t in range(5):
                r = rows[t]
                sp.wait_ge(z_done, t + 1)
                if t < TILES:
                    kv, win, at = O["kv_p"], O["win_p"], t * P
                else:
                    kv, win, at = O["kv_s"], None, 0
                dst = kv[at:at + r, :].rearrange("p (b s c) -> p b s c", b=2, s=2)
                sp.dma_start(dst[:, :, 0, :], k3(t, r)[:, 0:2, :]).then_inc(stored, 16)
                sp.dma_start(dst[:, :, 1, :], v3(t, r)[:, 0:2, :]).then_inc(stored, 16)
                if t < TILES:
                    sp.dma_start(win[at:at + r, 0:128], k3(t, r)[:, 2, :]).then_inc(stored, 16)
                    sp.dma_start(win[at:at + r, 128:256], v3(t, r)[:, 2, :]).then_inc(stored, 16)
                else:
                    dst = O["win_s"].rearrange("(b n) c -> b n c", b=NB)[:, T - 1, :]
                    sp.dma_start(dst[:, 0:128], k3(t, r)[:, 2, :]).then_inc(stored, 16)
                    sp.dma_start(dst[:, 128:256], v3(t, r)[:, 2, :]).then_inc(stored, 16)
                    sp.dma_start(O["pool_s"].rearrange("(b n) c -> b n c", b=NB)[:, STATE - 1, :],
                                 z[0:NB, t, U0:U0 + 256]).then_inc(stored, 16)
            sp.dma_start(O["pool_p"], z[P - STATE:P, TILES - 1, U0:U0 + 256]).then_inc(stored, 16)
            for j in range(2):
                sp.wait_ge(z_done, 6 + j)
                sp.dma_start(O["mem_p"][j * P:(j + 1) * P, :], memz[:, j, :]).then_inc(stored, 16)
            sp.wait_ge(stored, 16 * (4 * TILES + 5 + 1 + 2))

        @block.gpsimd
        def _(pool):
            nc.gpsimd.memset(blank[:, :], 0.0).then_inc(blank_ready, 1)
            pool.wait_ge(blank_ready, 1)
            pool.dma_start(self.ys_dram[NEXP * CAP:, :].rearrange("(a p) d -> p a d", p=CAP), blank[:, :].unsqueeze(1).broadcast_to([CAP, NOVER, D])).then_inc(self.blanked, 16)
            src = I["cache_win"].rearrange("(b n) c -> b (n c)", b=NB)
            dst = O["win_s"].rearrange("(b n) c -> b (n c)", b=NB)
            w = (T - 1) * 256
            pool.dma_start(dst[:, 0:w].rearrange("b (a n) -> b a n", a=7), src[:, 256:256 + w].rearrange("b (a n) -> b a n", a=7)).then_inc(self.moved, 16)
            src = I["state_pool"].rearrange("(b n) c -> b (n c)", b=NB)
            dst = O["pool_s"].rearrange("(b n) c -> b (n c)", b=NB)
            pool.dma_start(dst[:, 0:(STATE - 1) * 256], src[:, 256:STATE * 256]).then_inc(self.moved, 16)
            pool.wait_ge(self.blanked, 16)

        @block.vector
        def _(dve):
            ch = Chain(dve, dve_step)

            def norm(t):
                r = rows[t]
                dve.wait_ge(x_in[t % 3], 16 * (t // 3 + 1))
                if t >= 2:
                    dve.wait_ge(xT_in_psum, t - 1)
                ch.then(nc.vector.tensor_tensor_reduce(xn[0:r, t % 2, :], xin[0:r, t % 3, :], xin[0:r, t % 3, :], 1.0, 0.0,
                                                       ALU.mult, ALU.add, stat[0:r, t, 0:1]))
                nc.vector.tensor_scalar(stat[0:r, t, 1:2], stat[0:r, t, 0:1], 1.0 / D, EPS, ALU.mult, ALU.add).then_inc(ms_ready, 1)
                dve.wait_ge(rms_ready, t + 1)
                ch.then(nc.vector.reciprocal(stat[0:r, t, 3:4], stat[0:r, t, 2:3]))
                if t == 0:
                    dve.wait_ge(gains_in, 32)
                nc.vector.scalar_tensor_tensor(xn[0:r, t % 2, :], xin[0:r, t % 3, :], stat[0:r, t, 3:4],
                                               g_rows[0:r, 0 if t < 5 else 1, :], ALU.mult, ALU.mult).then_inc(xn_ready, 1)

            def heads(t):
                r = rows[t]
                at, n = groups(t)
                w = n * HD
                buf = zt(t)[0:r, at:at + w]
                b3 = buf.rearrange("p (n d) -> p n d", d=HD)
                dve.wait_ge(sq_ready, t + 1)
                ch.then(nc.vector.tensor_reduce(gstat[0:r, t, 0:n], junk[0:r, t % 2, 0:w].rearrange("p (n d) -> p n d", d=HD), AX.X, ALU.add))
                nc.vector.tensor_scalar(gstat[0:r, t, 0:n], gstat[0:r, t, 0:n], 1.0 / HD, EPS, ALU.mult, ALU.add).then_inc(gms_ready, 1)
                dve.wait_ge(grms_ready, t + 1)
                ch.then(nc.vector.reciprocal(gstat[0:r, t, 0:n], gstat[0:r, t, 0:n]))
                ch.then(nc.vector.tensor_tensor(b3, b3, gstat[0:r, t, 0:n].unsqueeze(2).broadcast_to([r, n, HD]), ALU.mult))
                last = nc.vector.tensor_tensor(buf, buf, g_head[0:r, 0:w] if t < 5 else g_head[0:r, V0 - Q0:V0 - Q0 + w], ALU.mult)
                if t >= 5:
                    last.then_inc(z_done, 1)
                    return
                ch.then(last)
                h3 = zt(t)[0:r, Q0:M0].rearrange("p (n d) -> p n d", d=HD)
                x1, x2 = h3[:, :, 0:8], h3[:, :, 8:16]
                cos = self.c(C_COS + 8 * t, 8, r).unsqueeze(1).broadcast_to([r, 14, 8])
                sin = self.c(C_SIN + 8 * t, 8, r).unsqueeze(1).broadcast_to([r, 14, 8])
                if t == 0:
                    dve.wait_ge(consts_in, 16)
                for j, (a, b) in enumerate(((x1, cos), (x2, sin), (x2, cos), (x1, sin))):
                    last = nc.vector.tensor_tensor(rot[0:r, j, :, :], a, b, ALU.mult)
                ch.then(last)
                nc.vector.tensor_tensor(x1, rot[0:r, 0, :, :], rot[0:r, 1, :, :], ALU.subtract)
                nc.vector.tensor_tensor(x2, rot[0:r, 2, :, :], rot[0:r, 3, :, :], ALU.add).then_inc(z_done, 1)

            norm(0)
            for t in range(n_items):
                if t + 1 < n_items:
                    norm(t + 1)
                heads(t)

        @block.scalar
        def _(act):
            def root(t):
                act.wait_ge(ms_ready, t + 1)
                nc.scalar.activation(stat[0:rows[t], t, 2:3], stat[0:rows[t], t, 1:2], ACT.Sqrt).then_inc(rms_ready, 1)

            def roots(t):
                n = groups(t)[1]
                act.wait_ge(gms_ready, t + 1)
                nc.scalar.activation(gstat[0:rows[t], t, 0:n], gstat[0:rows[t], t, 0:n], ACT.Sqrt).then_inc(grms_ready, 1)

            root(0)
            for t in range(n_items):
                r = rows[t]
                act.wait_ge(xT_in_psum, t + 1)
                if t >= 2:
                    act.wait_ge(z_in_psum, t - 1)
                nc.scalar.copy(xT[:, t % 2, :, 0:r], pt[:, :, 0:r]).then_inc(xT_ready, 1)
                if t + 1 < n_items:
                    root(t + 1)
                act.wait_ge(z_in_psum, t + 1)
                if t < 5:
                    ins = nc.scalar.copy(z[0:r, t, :].rearrange("p (a n) -> p a n", a=4), pz[0:r, :, 0:ZC])
                else:
                    ins = nc.scalar.copy(memz[:, t - 5, :], pz[:, 0, :])
                ins.then_inc(z_ready, 1)
                act.wait_ge(z_ready, t + 1)
                at, n = groups(t)
                if t >= 2:
                    act.wait_ge(gms_ready, t - 1)
                nc.scalar.activation(junk[0:r, t % 2, 0:n * HD], zt(t)[0:r, at:at + n * HD], ACT.Square).then_inc(sq_ready, 1)
                roots(t)

        @block.tensor
        def _(pe):
            pe.wait_ge(consts_in, 16)
            for t in range(n_items):
                r = rows[t]
                pe.wait_ge(xn_ready, t + 1)
                if t >= 1:
                    pe.wait_ge(xT_ready, t)
                for k in range(KD):
                    ins = nc.tensor.transpose(pt[:, k, 0:r], xn[0:r, t % 2, k:D:KD], self.c(C_ID, r, r))
                ins.then_inc(xT_in_psum, 1)
                pe.wait_ge(xT_ready, t + 1)
                if t >= 1:
                    pe.wait_ge(z_ready, t)
                if t == 0:
                    pe.wait_ge(win_in, 32)
                if t == 5:
                    pe.wait_ge(wmem_in, 16)
                for a in range(4 if t < 5 else 1):
                    for k in range(KD):
                        rhs = w_in[:, k, a * ZC:(a + 1) * ZC] if t < 5 else w_mem[:, k, :]
                        out = pz[0:r, a, 0:ZC] if t < 5 else pz[0:r, 0, :]
                        ins = nc.tensor.matmul(out, xT[:, t % 2, k, 0:r], rhs, start=(k == 0), stop=(k == KD - 1))
                ins.then_inc(z_in_psum, 1)

        self.close(st)

    def stream(self):
        nc, I, O = self.nc, self.ins, self.outs
        st = ExitStack()
        S = lambda n: self.sem(n, st)
        kvc = self.sb("kvc", [P, 2, 4, 4, 2, 64], stack=st)
        ksel = self.sb("ksel", [P, 2, 4, 2, 128], stack=st)
        winK = self.sb("winK", [P, 2, 4, 128], stack=st)
        memK = self.sb("memK", [P, 2, 2, 256], stack=st)
        XT = self.sb("XT", [P, 2, 2, G, 512], stack=st)
        KsT = self.sb("KsT", [P, 2, 1024], stack=st)
        KwT = self.sb("KwT", [P, 2, 512], stack=st)
        KmT = self.sb("KmT", [P, 2, 2, 256], stack=st)
        w1 = self.sb("w1", [P, 2, 16, 128], stack=st)
        w2 = self.sb("w2", [P, 2, 64], stack=st)
        w2pad = self.sb("w2pad", [P, G, 128], stack=st)
        pe_pos = self.sb("pe_pos", [P, 2, 16], stack=st)
        hbias = self.sb("hbias", [P, 2], stack=st)
        hx = self.sb("hx", [P, 2, 256], stack=st)
        ht = self.sb("ht", [P, 256], stack=st)
        gel = self.sb("gel", [P, 2, 256], stack=st)
        Vs = self.sb("Vs", [P, NB, 4, 2, 128], stack=st)
        Vw = self.sb("Vw", [P, NB, 4, 128], stack=st)
        Vm = self.sb("Vm", [P, NB, 2, 256], stack=st)
        Q = self.sb("Q", [P, NB * 72], stack=st)
        Qm = self.sb("Qm", [P, 2, NB * 36], stack=st)
        kTn = self.sb("kTn", [P, 2, NB], stack=st)
        zb = self.sb("zb", [1, 512], BF16, stack=st)
        pages = self.sb("pages", [1, NB * NB], I32, stack=st)
        gat = self.sb("gat", [NB, 24], stack=st)
        g64 = self.sb("g64", [64, 3], stack=st)
        kv_in, wk_in, mk_in = ([S(f"{n}_in{j}") for j in range(2)] for n in ("kv", "wk", "mk"))
        v_in, w_in_, pages_in, zeroed, made, steps_d, steps_a = (S(n) for n in (
            "v_in", "cmp_w_in", "pages_in", "zeroed", "made", "stream_dve", "stream_act"))
        small_in_psum, q_ready, turned, out_a, out_d = (S(n) for n in ("small_in_psum", "q_ready", "turned", "out_a", "out_d"))
        hid_in_psum, scored, hx_ready, he_ready, gel_ready, cmp_in_psum, cmp_ready = (S(n) for n in (
            "hid_in_psum", "scored", "hx_ready", "he_ready", "gel_ready", "cmp_in_psum", "cmp_ready"))
        gate_out, gate_in, gclamp, gexp, gsig = (S(n) for n in ("gate_out", "gate_in", "gclamp", "gexp", "gsig"))
        cs_in_psum, ec, pc, imp_in_psum, es, ps_ready, pT_in_psum, pT_ready, o_in_psum, oT_ready, os_in_psum = (S(n) for n in (
            "cs_in_psum", "ec", "pc", "imp_in_psum", "es", "ps_ready", "pT_in_psum", "pT_ready", "o_in_psum", "oT_ready", "os_in_psum"))
        ps, z = self.ps, self.z
        sel0, win0, misc, hid, cmp_ = ps[:, 0:2, :], ps[:, 2, :], ps[:, 3, :], ps[:, 6, :], ps[:, 7, :]
        kcT, vc = self.kcT, self.vc
        smp = TILES
        blocks = [NC_S] * NB + [NC_P]
        ntile = [4] * NB + [2]
        units = [8] * NB + [4]
        first = [8 * s for s in range(NSEQ)]
        hidv = hid.rearrange("p (q n) -> p q n", q=4)

        late = kvc[:, 1, :, :, :, :].rearrange("p a b c d -> p (a b c d)")
        more = ksel[:, 1, :, :, :].rearrange("p a b c -> p (a b c)")
        ssb, swb = late[0:64, 0:1040], late[0:64, 1040:1568]
        pTs = more[:, 0:512].rearrange("p (a b) -> p a b", a=8)
        pTw = late[:, 1568:1824].rearrange("p (a b) -> p a b", a=4)
        pTm = late[:, 1824:1888].rearrange("p (a b) -> p a b", a=2)
        oT, smb = late[:, 1888:2016], more[0:32, 512:768]
        dgn = more[0:64, 768:896].rearrange("p (a b) -> p a b", a=2)
        nw = more[0:NB, 896:1024].rearrange("p (a b) -> p a b", a=2)
        scb = self.sb("scb", [64, 64], stack=st)
        sst = self.sb("sst", [64, 4, 4], stack=st)
        imp = self.sb("imp", [64, 6, 16], stack=st)
        pTc = self.sb("pTc", [64, 64], stack=st)

        block = st.enter_context(nc.Block("stream"))

        marks = {}

        @block.vector
        def _(dve):
            ch = Chain(dve, steps_d)
            dve.wait_ge(zeroed, 6)
            dve.wait_ge(small_in_psum, 1)
            nc.vector.tensor_copy(hbias[:, :], hid[:, 0:2])
            nc.vector.tensor_copy(w2pad[:, 0, 0:64], w2[:, 0, :])
            nc.vector.tensor_copy(w2pad[:, 1, 64:128], w2[:, 0, :])
            nc.vector.tensor_copy(kTn[:, :, :], cmp_[:, 48:64].rearrange("p (a b) -> p a b", a=2))
            for g in range(G):
                half = slice(64 * g, 64 * g + 64)
                nc.vector.tensor_copy(Q[half, :].rearrange("p (b x) -> p b x", x=72)[:, :, g:g + 2 * R:2],
                                      cmp_[half, 0:32].rearrange("p (r b) -> p b r", r=R))
                for hp in range(2):
                    h = 2 * hp + g
                    ins = nc.vector.tensor_copy(Qm[half, hp, :].rearrange("p (b x) -> p b x", x=36)[:, :, h:h + 1],
                                                cmp_[half, 32 + 8 * hp:40 + 8 * hp].unsqueeze(2))
            ins.then_inc(q_ready, 1)
            nc.vector.tensor_scalar(gat[:, :], z[0:NB, smp, G0:G0 + 24], -80.0, None, ALU.max).then_inc(gclamp, 1)
            dve.wait_ge(gexp, 1)
            ch.then(nc.vector.tensor_scalar(gat[:, :], gat[:, :], 1.0, None, ALU.add))
            nc.vector.reciprocal(gat[:, :], gat[:, :]).then_inc(gsig, 1)

            def out(s):
                for u in range(1, units[s], 2):
                    dve.wait_ge(turned, first[s] + u + 1)
                    if s >= 2 and u == 1:
                        dve.wait_ge(scored, s - 1)
                    dst = (XT[:, s % 2, u // 2, 1, :] if u < 4 else KsT[:, s % 2, 512:1024] if u == 5
                           else KmT[:, s % 2, :, :].rearrange("p a n -> p (a n)"))
                    w = 128 * ntile[s]
                    nc.vector.tensor_copy(dst[:, 0:w], ps[:, 5, 0:w]).then_inc(out_d, 1)

            def gelu(s):
                n = blocks[s]
                dve.wait_ge(hid_in_psum, s + 1)
                x = hx[:, s % 2, :].rearrange("p (q n) -> p q n", q=4)[:, :, 0:n]
                t = ht[:, :].rearrange("p (q n) -> p q n", q=4)[:, :, 0:n]
                for q in range(2):
                    ins = nc.vector.tensor_scalar(x[:, 2 * q:2 * q + 2, :], hidv[:, 2 * q:2 * q + 2, 0:n], hbias[:, q:q + 1], None, ALU.add)
                ch.then(ins)
                ch.then(nc.vector.tensor_tensor(t, x, x, ALU.mult))
                ch.then(nc.vector.tensor_scalar(t, t, 0.044715, 1.0, ALU.mult, ALU.add))
                ch.then(nc.vector.tensor_tensor(t, t, x, ALU.mult))
                nc.vector.tensor_scalar(t, t, -50.0, None, ALU.max).then_inc(hx_ready, 1)
                dve.wait_ge(he_ready, s + 1)
                ch.then(nc.vector.tensor_scalar(t, t, 1.0, None, ALU.add))
                ch.then(nc.vector.reciprocal(t, t))
                if s >= 2:
                    dve.wait_ge(cmp_in_psum, s - 1)
                nc.vector.tensor_tensor(gel[:, s % 2, :].rearrange("p (q n) -> p q n", q=4)[:, :, 0:n], t, x, ALU.mult).then_inc(gel_ready, 1)

            def keep(s):
                n = blocks[s]
                dve.wait_ge(cmp_in_psum, s + 1)
                nc.vector.tensor_copy(kcT[:, s, 0:n], cmp_[:, 0:n])
                nc.vector.tensor_copy(vc[0:n, s, :], cmp_[0:n, 128:256]).then_inc(cmp_ready, 1)

            out(0)
            for s in range(NSEQ):
                if s + 1 < NSEQ:
                    out(s + 1)
                gelu(s)
                if s >= 1:
                    keep(s - 1)
            keep(NSEQ - 1)

            def peak(j, rows, src, mark):
                ch.then(nc.vector.tensor_reduce(sst[0:rows, j, 0:1], src, AX.X, ALU.max))
                ch.then(nc.vector.tensor_scalar(sst[0:rows, j, 1:2], sst[0:rows, j, 0:1], -SCALE, None, ALU.mult))
                marks[mark] = ch.n

            def weights(j, rows, probs, gate, mark):
                ch.then(nc.vector.reciprocal(sst[0:rows, j, 3:4], sst[0:rows, j, 2:3]))
                if gate is None:
                    ch.then(nc.vector.tensor_scalar(probs, probs, sst[0:rows, j, 3:4], None, ALU.mult))
                else:
                    ch.then(nc.vector.tensor_scalar(probs, probs, sst[0:rows, j, 3:4], gate, ALU.mult, ALU.mult))
                if mark:
                    marks[mark] = ch.n

            dve.wait_ge(cs_in_psum, 1)
            ch.then(nc.vector.tensor_copy(scb[:, 0:NC_S], misc[0:64, 0:NC_S]))
            peak(0, 64, scb[:, 0:NC_S], "cmax")
            ch.then(nc.vector.tensor_copy(smb[:, :], misc[0:32, 128:384]))
            peak(1, 32, smb[:, :], "mmax")
            nc.vector.memset(swb[:, 0:1], 0.0)
            nc.vector.tensor_copy(swb[:, 1:512], win0[0:64, 1:512])
            ch.then(nc.vector.tensor_copy(swb[:, 512:513], misc[0:64, 65:66]))
            peak(2, 64, swb[:, 1:513], "wmax")
            dve.wait_ge(es, 1)
            weights(0, 64, scb[:, 0:NC_S], None, "pc")
            dve.wait_ge(es, 2)
            weights(1, 32, smb[:, :], None, "mp")
            dve.wait_ge(imp_in_psum, 1)
            ch.then(nc.vector.tensor_reduce(imp[:, 0, :], hid[0:64, 0:64].rearrange("p (n k) -> p n k", k=4), AX.X, ALU.add))
            ch.then(nc.vector.tensor_reduce(sst[:, 0, 0:1], imp[:, 0, 1:15], AX.X, ALU.min))
            ch.then(nc.vector.scalar_tensor_tensor(imp[:, 1, 1:15], imp[:, 0, 1:15], sst[:, 0, 0:1], self.c(C_BLK, 14, 64), ALU.is_equal, ALU.mult))
            ch.then(nc.vector.tensor_reduce(sst[:, 0, 1:2], imp[:, 1, 1:15], AX.X, ALU.max))
            ch.then(nc.vector.tensor_scalar(imp[:, 2, 1:15], self.c(C_BLK, 14, 64), sst[:, 0, 1:2], NEG, ALU.is_equal, ALU.mult))
            for par in range(2):
                v = lambda a: a.rearrange("p (c t k j) -> p c t k j", c=4, t=2, k=4)[:, :, par, :, :]
                out4 = ssb[:, 0:1024].rearrange("p (c t k j) -> p c t k j", c=4, t=2, k=4)
                in4 = sel0[0:64, :, :].rearrange("p a (c t k j) -> p (a c) t k j", c=2, t=2, k=4)
                mask = imp[:, 2, :].rearrange("p (c k) -> p c k", c=4).unsqueeze(3).broadcast_to([64, 4, 4, 32])
                nc.vector.tensor_tensor(out4[:, :, par, :, :], in4[:, :, par, :, :], mask, ALU.add)
            ch.then(nc.vector.tensor_copy(ssb[:, 1024:1025], misc[0:64, 64:65]))
            peak(3, 64, ssb[:, 0:1025], "smax")
            dve.wait_ge(gate_in, 16 * NB)
            ch.then(nc.vector.tensor_scalar(scb[:, 0:NC_S], scb[:, 0:NC_S], g64[:, 0:1], None, ALU.mult))
            dve.wait_ge(es, 3)
            weights(2, 64, swb[:, 1:513], g64[:, 2:3], None)
            ch.then(nc.vector.tensor_scalar(dgn[:, 1, :], self.c(C_ID, 64, 64), swb[:, 512:513], None, ALU.mult))
            marks["wp"] = ch.n
            dve.wait_ge(es, 4)
            weights(3, 64, ssb[:, 0:1025], g64[:, 1:2], None)
            ch.then(nc.vector.tensor_scalar(dgn[:, 0, :], self.c(C_ID, 64, 64), ssb[:, 1024:1025], None, ALU.mult))
            marks["sp"] = ch.n
            dve.wait_ge(pT_in_psum, 1)
            nc.vector.tensor_copy(late[:, 1568:1824], ps[:, 5, 0:256])
            nc.vector.tensor_copy(pTc[0:NC_S, :], ps[0:NC_S, 5, 256:320])
            nc.vector.tensor_copy(late[:, 1824:1888], ps[:, 5, 448:512])
            nc.vector.tensor_copy(nw[:, 1, :], ps[0:NB, 5, 384:448]).then_inc(pT_ready, 1)
            dve.wait_ge(pT_in_psum, 2)
            nc.vector.tensor_copy(more[:, 0:512], ps[:, 4, :])
            nc.vector.tensor_copy(nw[:, 0, :], hid[0:NB, 256:320]).then_inc(pT_ready, 1)
            dve.wait_ge(o_in_psum, 1)
            nc.vector.tensor_copy(oT[:, :], cmp_[:, 0:128]).then_inc(oT_ready, 1)
            dve.wait_ge(os_in_psum, 1)
            for a in range(2):
                nc.vector.tensor_copy(self.o_s[:, :].rearrange("p (n a d) -> p n a d", a=2, d=64)[:, :, a, :],
                                      ps[0:NB, 4 + a, 0:384].rearrange("p (n d) -> p n d", d=64))

        @block.sync
        def _(sp):
            sp.dma_start(pages[:, :], I["page_table"]).then_inc(pages_in, 16)
            sp.dma_start(w1[:, :, :, :], I["w_cmp1"].rearrange("q (l p) n -> p q l n", p=P)).then_inc(w_in_, 16)
            sp.dma_start(w2[:, :, :], I["w_cmp2"].rearrange("q p n -> p q n")).then_inc(w_in_, 16)
            sp.dma_start(pe_pos[:, :, :], I["pe"]).then_inc(w_in_, 16)
            src = I["cache_kv"].rearrange("(g p t) c -> g p t c", p=64, t=2)
            sp.wait_ge(pages_in, 16)

            def load(b, slot):
                for pg in range(PAST // PAGE):
                    at = sp.value_load(pages[0:1, bass.ds(b * NB + pg, 1)], min_val=0, max_val=src.shape[0] - 1)
                    half = slice(64 * (pg % 2), 64 * (pg % 2) + 64)
                    rows = src[bass.ds(at, 1), :, :, :].rearrange("g p t c -> (g p) t c")
                    for t in range(2):
                        sp.dma_start(kvc[half, slot, pg // 2, :, t, :], rows[:, t, 0:256].rearrange("p (a d) -> p a d", a=4)).then_inc(kv_in[slot], 16)
                    sp.dma_start(ksel[half, slot, pg // 2, :, :], rows[:, :, 256:384]).then_inc(kv_in[slot], 16)
                    sp.dma_start(Vs[half, bass.ds(b, 1), pg // 2, :, :].rearrange("p o t c -> p (o t) c"),
                                 rows[:, :, 384:512]).then_inc(v_in, 16)

            load(0, 0)
            load(1, 1)
            with sp.Fori(1, NB // 2) as i:
                for slot in range(2):
                    sp.wait_ge(turned, i * 16 + (slot * 8 - 8))
                    load(i * 2 + slot, slot)
            sp.wait_ge(turned, 8 * (NSEQ - 2))
            for c in range(2):
                for t in range(2):
                    sp.dma_start(kvc[:, 0, c, :, t, :], O["kv_p"][256 * c + t:256 * c + 256:2, 0:256].rearrange("p (a d) -> p a d", a=4)).then_inc(kv_in[0], 16)

        @block.gpsimd
        def _(pool):
            nc.gpsimd.memset(Q[:, :], 0.0).then_inc(zeroed, 1)
            nc.gpsimd.memset(Qm[:, :, :], 0.0).then_inc(zeroed, 1)
            nc.gpsimd.memset(w2pad[:, :, :], 0.0).then_inc(zeroed, 1)
            nc.gpsimd.memset(zb[:, :], 0.0).then_inc(zeroed, 1)
            nc.gpsimd.memset(scb[:, :], 0.0).then_inc(zeroed, 1)
            nc.gpsimd.memset(imp[:, :, :], 0.0).then_inc(zeroed, 1)
            pool.wait_ge(gsig, 1)
            pool.dma_start(self.gate_dram, gat[:, :]).then_inc(gate_out, 16)
            pool.wait_ge(gate_out, 16)
            with nc.allow_non_contiguous_dma("192 gates"):
                for b in range(NB):
                    pool.dma_start(g64[H * b:H * b + H, :], self.gate_dram[b].rearrange("(q c) -> c q", q=3)).then_inc(gate_in, 16)

        @block.scalar
        def _(act):
            srcw = I["cache_win"].rearrange("(b p j) c -> b p j c", b=NB, j=4)
            srcm = I["cache_mem"].rearrange("(b p j) c -> b p j c", b=NB, j=2)

            def load(b):
                act.dma_start(winK[:, b % 2, :, :], srcw[b, :, :, 0:128]).then_inc(wk_in[b % 2], 16)
                act.dma_start(memK[:, b % 2, :, :], srcm[b, :, :, 0:256]).then_inc(mk_in[b % 2], 16)
                act.dma_start(Vw[:, b, :, :], srcw[b, :, :, 128:256]).then_inc(v_in, 16)
                act.dma_start(Vm[:, b, :, :], srcm[b, :, :, 256:512]).then_inc(v_in, 16)

            load(0)
            load(1)
            act.wait_ge(gclamp, 1)
            nc.scalar.activation(gat[:, :], gat[:, :], ACT.Exp, scale=-1.0).then_inc(gexp, 1)

            def out(s):
                for u in range(0, units[s], 2):
                    act.wait_ge(turned, first[s] + u + 1)
                    if s >= 2 and u == 0:
                        act.wait_ge(scored, s - 1)
                    src = ps[:, 4, :]
                    dst = (XT[:, s % 2, u // 2, 0, :] if u < 4 else KsT[:, s % 2, 0:512] if u == 4 else KwT[:, s % 2, :])
                    w = 128 * ntile[s]
                    nc.scalar.copy(dst[:, 0:w], src[:, 0:w]).then_inc(out_a, 1)
                if s + 2 < NB:
                    act.wait_ge(turned, first[s] + 8)
                    load(s + 2)

            out(0)
            for s in range(NSEQ):
                if s + 1 < NSEQ:
                    out(s + 1)
                n = blocks[s]
                act.wait_ge(hx_ready, s + 1)
                v = ht[:, :].rearrange("p (q n) -> p q n", q=4)[:, :, 0:n]
                nc.scalar.activation(v, v, ACT.Exp, scale=-2.0 * 0.7978845608028654).then_inc(he_ready, 1)
            act.wait_ge(steps_d, marks["cmax"])
            nc.scalar.activation(scb[:, 0:NC_S], scb[:, 0:NC_S], ACT.Exp, bias=sst[:, 0, 1:2], scale=SCALE,
                                 accum_out=sst[:, 0, 2:3]).then_inc(es, 1)
            act.wait_ge(steps_d, marks["mmax"])
            nc.scalar.activation(smb[:, :], smb[:, :], ACT.Exp, bias=sst[0:32, 1, 1:2], scale=SCALE,
                                 accum_out=sst[0:32, 1, 2:3]).then_inc(es, 1)
            act.wait_ge(steps_d, marks["wmax"])
            nc.scalar.activation(swb[:, 1:513], swb[:, 1:513], ACT.Exp, bias=sst[:, 2, 1:2], scale=SCALE,
                                 accum_out=sst[:, 2, 2:3]).then_inc(es, 1)
            act.wait_ge(steps_d, marks["smax"])
            nc.scalar.activation(ssb[:, 0:1025], ssb[:, 0:1025], ACT.Exp, bias=sst[:, 3, 1:2], scale=SCALE,
                                 accum_out=sst[:, 3, 2:3]).then_inc(es, 1)

        @block.tensor
        def _(pe):
            ident = lambda n, at=0: self.consts[at:at + n, C_ID + at:C_ID + at + n]
            pe.wait_ge(zeroed, 6)
            for a in range(4):
                nc.tensor.matmul(ps[0:64, a, :], zb[0:1, 0:64], zb[0:1, :], start=True, stop=False, skip_group_check=True)
            for r in range(R):
                nc.tensor.transpose(cmp_[:, 8 * r:8 * r + 8], z[0:NB, smp, Q0 + 128 * r:Q0 + 128 * r + 128], ident(NB))
            for j in range(2):
                nc.tensor.transpose(cmp_[:, 32 + 8 * j:40 + 8 * j], z[0:NB, smp, M0 + 128 * j:M0 + 128 * j + 128], ident(NB))
            for j in range(2):
                ins = nc.tensor.transpose(cmp_[:, 48 + 8 * j:56 + 8 * j], z[0:NB, smp, K0 + 128 * (j + 1):K0 + 128 * (j + 2)], ident(NB))
            pe.wait_ge(w_in_, 48)
            for q in range(2):
                for l in range(16):
                    ins = nc.tensor.matmul(hid[:, q:q + 1], w1[:, q, l, :], pe_pos[:, q, l:l + 1], start=(l == 0), stop=(l == 15))
            ins.then_inc(small_in_psum, 1)

            def turn(s):
                k, w, m = kvc[:, s % 2, :, :, :, :], winK[:, s % 2, :, :], memK[:, s % 2, :, :]
                pe.wait_ge(kv_in[s % 2], 384 * (s // 2 + 1) if s < NB else 384 * (NB // 2) + 64)
                for u in range(units[s]):
                    n = first[s] + u
                    if u == 6:
                        pe.wait_ge(wk_in[s % 2], 16 * (s // 2 + 1))
                    if u == 7:
                        pe.wait_ge(mk_in[s % 2], 16 * (s // 2 + 1))
                    if n >= 2:
                        pe.wait_ge(out_d if n % 2 else out_a, n // 2)
                    dst = ps[:, 4 + n % 2, :]
                    for c in range(ntile[s]):
                        if u < 4:
                            src = k[:, c, u, :, :].rearrange("p t d -> p (t d)")
                        elif u < 6:
                            src = ksel[:, s % 2, 2 * (u - 4) + c // 2, c % 2, :]
                        elif u == 6:
                            src = w[:, c, :]
                        else:
                            src = m[:, c % 2, 128 * (c // 2):128 * (c // 2) + 128]
                        ins = nc.tensor.transpose(dst[:, 128 * c:128 * c + 128], src, ident(P))
                    ins.then_inc(turned, 1)

            def compress(s):
                n = blocks[s]
                pe.wait_ge(out_a, first[s] // 2 + 2)
                pe.wait_ge(out_d, first[s] // 2 + 2)
                if s == 0:
                    pe.wait_ge(q_ready, 1)
                else:
                    pe.wait_ge(hx_ready, s)
                for q in range(2):
                    for l in range(16):
                        ins = nc.tensor.matmul(hidv[:, 2 * q:2 * q + 2, 0:n], w1[:, q, l, :],
                                               XT[:, s % 2, q, :, l:l + 8 * (n - 1) + 1:8], start=(l == 0), stop=(l == 15))
                ins.then_inc(hid_in_psum, 1)

            def score(s):
                if s == NB:
                    return
                pe.wait_ge(out_a, first[s] // 2 + 4)
                pe.wait_ge(out_d, first[s] // 2 + 4)
                add = dict(start=False, stop=False, skip_group_check=True)
                q = Q[:, 64 * s:64 * s + 64]
                for a in range(2):
                    nc.tensor.matmul(sel0[0:64, a, :], q, KsT[:, s % 2, 512 * a:512 * a + 512], **add)
                nc.tensor.matmul(win0[0:64, :], q, KwT[:, s % 2, :], **add)
                for a in range(2):
                    nc.tensor.matmul(misc[0:64, 64 + a:65 + a], q, kTn[:, a, s:s + 1], **add)
                for a in range(2):
                    ins = nc.tensor.matmul(misc[0:32, 128:384], Qm[:, a, 32 * s:32 * s + 32], KmT[:, s % 2, a, :], **add)
                ins.then_inc(scored, 1)

            def project_blocks(s):
                n = blocks[s]
                pe.wait_ge(gel_ready, s + 1)
                if s >= 1:
                    pe.wait_ge(cmp_ready, s)
                gk = gel[:, s % 2, :].rearrange("p (q n) -> p q n", q=4)
                for g in range(G):
                    nc.tensor.matmul(cmp_[:, 0:n], w2pad[:, g, :], gk[:, g, 0:n], start=(g == 0), stop=(g == 1))
                for g in range(G):
                    ins = nc.tensor.matmul(cmp_[0:n, 128 + 64 * g:192 + 64 * g], gk[:, 2 + g, 0:n], w2[:, 1, :], start=True, stop=True)
                ins.then_inc(cmp_in_psum, 1)

            turn(0)
            for s in range(NSEQ):
                if s + 1 < NSEQ:
                    turn(s + 1)
                compress(s)
                score(s)
                if s >= 1:
                    project_blocks(s - 1)
            project_blocks(NSEQ - 1)
            pe.wait_ge(cmp_ready, NSEQ)
            for b in range(NB):
                ins = nc.tensor.matmul(misc[0:64, 0:NC_S], Q[:, 64 * b:64 * b + 64], kcT[:, b, 0:NC_S], start=False, stop=False, skip_group_check=True)
            ins.then_inc(cs_in_psum, 1)
            pe.wait_ge(steps_d, marks["pc"])
            nc.tensor.matmul(hid[0:64, 0:64], self.c(C_RG, 64, 64), scb[:, :], start=True, stop=True).then_inc(imp_in_psum, 1)
            pe.wait_ge(steps_d, marks["wp"])
            for j in range(2):
                nc.tensor.transpose(ps[:, 5, 448 + 32 * j:480 + 32 * j], smb[:, 128 * j:128 * j + 128], ident(32))
            for j in range(4):
                nc.tensor.transpose(ps[:, 5, 64 * j:64 * j + 64], swb[:, 128 * j:128 * j + 128], ident(64))
            nc.tensor.transpose(ps[0:NC_S, 5, 256:320], scb[:, 0:NC_S], ident(64))
            nc.tensor.matmul(ps[0:NB, 5, 384:448], self.c(C_S8, NB, 64), dgn[:, 1, :], start=True, stop=True).then_inc(pT_in_psum, 1)
            pe.wait_ge(steps_d, marks["sp"])
            for j in range(8):
                nc.tensor.transpose(ps[:, 4, 64 * j:64 * j + 64], ssb[:, 128 * j:128 * j + 128], ident(64))
            nc.tensor.matmul(hid[0:NB, 256:320], self.c(C_S8, NB, 64), dgn[:, 0, :], start=True, stop=True).then_inc(pT_in_psum, 1)
            nc.tensor.matmul(cmp_, zb[0:1, 0:128], zb[0:1, :], start=True, stop=False, skip_group_check=True)
            add = dict(start=False, stop=False, skip_group_check=True)
            pe.wait_ge(v_in, 16 * (8 * NB + 2 * NB))
            pe.wait_ge(pT_ready, 1)
            for b in range(NB):
                o = cmp_[:, 8 * b:8 * b + 8]
                for j in range(4):
                    nc.tensor.matmul(o, Vw[:, b, j, :], pTw[:, j, 8 * b:8 * b + 8], **add)
                nc.tensor.matmul(o, vc[0:NC_S, b, :], pTc[0:NC_S, 8 * b:8 * b + 8], **add)
                for hp in range(2):
                    for j in range(2):
                        nc.tensor.matmul(cmp_[:, 64 + 32 * hp + 4 * b:68 + 32 * hp + 4 * b], Vm[:, b, j, 128 * hp:128 * hp + 128],
                                         pTm[:, j, 4 * b:4 * b + 4], **add)
            nc.tensor.matmul(cmp_[:, 0:64], z[0:NB, smp, V0 + 256:V0 + 384], nw[:, 1, :], **add)
            pe.wait_ge(pT_ready, 2)
            for b in range(NB):
                for j in range(8):
                    nc.tensor.matmul(cmp_[:, 8 * b:8 * b + 8], Vs[:, b, j // 2, j % 2, :], pTs[:, j, 8 * b:8 * b + 8], **add)
            nc.tensor.matmul(cmp_[:, 0:64], z[0:NB, smp, V0 + 128:V0 + 256], nw[:, 0, :], **add).then_inc(o_in_psum, 1)
            pe.wait_ge(oT_ready, 1)
            for c in range(H):
                at = 64 * (c % 2)
                nc.tensor.transpose(ps[0:NB, 4 + c % 2, 64 * (c // 2):64 * (c // 2) + 64], oT[at:at + 64, c:64:8], ident(64, at))
            for h in range(MH):
                at = 64 * (h % 2)
                ins = nc.tensor.transpose(ps[0:NB, 4 + h % 2, 256 + 64 * (h // 2):320 + 64 * (h // 2)], oT[at:at + 64, 64 + 32 * (h // 2) + h:96 + 32 * (h // 2):4], ident(64, at))
            ins.then_inc(os_in_psum, 1)

        self.close(st)

    def attend(self):
        nc, I, O = self.nc, self.ins, self.outs
        st = ExitStack()
        S = lambda n: self.sem(n, st)
        ps, z, o = self.ps, self.z, self.o
        qT = self.sb("qT", [P, R, T], stack=st)
        kT = self.sb("kT", [P, 2, T], stack=st)
        qmT = self.sb("qmT", [P, 2, T], stack=st)
        mz = self.sb("mz", [P, 2, 512], stack=st)
        mkT = self.sb("mkT", [P, 2, MEM], stack=st)
        gate = self.sb("gate", [P, TILES, 24], stack=st)
        prob = self.sb("prob", [P, 2, 2, 512], stack=st)
        pT = self.sb("pT", [P, 2, 512], stack=st)
        stt = self.sb("stt", [P, 2, 4, 8], stack=st)
        zb = self.sb("zb2", [1, 512], BF16, stack=st)
        mz_in, gclamp, gexp, steps, zeroed, turned, out_a, out_d = (S(n) for n in (
            "mz_in", "gate_clamped", "gate_exp", "attend_dve", "zb_zeroed", "qk_turned", "qk_out_a", "qk_out_d"))
        scores, peaks, exps, probs, p_turned, pT_a, pT_d, pv, o_in_psum, o_out = (S(n) for n in (
            "scores", "peaks", "exps", "probs", "p_turned", "pT_a", "pT_d", "pv", "o_in_psum", "o_out"))

        pre = []
        for r in range(R):
            pre.append(([z[:, t, Q0 + 128 * r:Q0 + 128 * r + 128] for t in range(TILES)], qT[:, r, :]))
        for a in range(2):
            pre.append(([z[:, t, K0 + 128 * (a + 1):K0 + 128 * (a + 2)] for t in range(TILES)], kT[:, a, :]))
        for a in range(2):
            pre.append(([z[:, t, M0 + 128 * a:M0 + 128 * a + 128] for t in range(TILES)], qmT[:, a, :]))
        pre.append(([mz[:, j, 128 * a:128 * a + 128] for a in range(2) for j in range(2)], mkT[:, :, :].rearrange("p a n -> p (a n)")))
        units = [(t, kind, g, rp) for t in range(TILES)
                 for kind, g, rp in [("cmp", 0, 0), ("mem", 0, 0)] + [(br, g, rp) for br in ("sel", "win") for rp in range(2) for g in range(G)]]
        NU = len(units)
        per = NU // TILES

        block = st.enter_context(nc.Block("attend"))

        @block.sync
        def _(sp):
            for j in range(2):
                sp.dma_start(mz[:, j, :], O["mem_p"][j * P:(j + 1) * P, :]).then_inc(mz_in, 16)

        @block.gpsimd
        def _(pool):
            nc.gpsimd.memset(zb[:, :], 0.0).then_inc(zeroed, 1)

        @block.tensor
        def _(pe):
            ident = self.consts[:, C_ID:C_ID + P]
            pe.wait_ge(zeroed, 1)
            for n, (srcs, _) in enumerate(pre):
                if n == len(pre) - 1:
                    pe.wait_ge(mz_in, 32)
                if n >= 2:
                    pe.wait_ge(out_d if n % 2 else out_a, n // 2)
                for c, src in enumerate(srcs):
                    ins = nc.tensor.transpose(ps[:, 4 + n % 2, 128 * c:128 * c + 128], src, ident)
                ins.then_inc(turned, 1)

            def score(u):
                t, kind, g, rp = units[u]
                q = slice(t * P, (t + 1) * P)
                if u >= 2:
                    pe.wait_ge(exps, u - 1)
                b = 2 * (u % 2)
                if kind == "cmp":
                    for g in range(G):
                        hs = slice(64 * g, 64 * g + 64)
                        for r in range(R):
                            ins = nc.tensor.matmul(ps[:, b + g, 32 * r:32 * r + NC_P], qT[hs, r, q], self.kcT[hs, NB, 0:NC_P], start=True, stop=True)
                elif kind == "mem":
                    for h in range(MH):
                        hs = slice(64 * (h % 2), 64 * (h % 2) + 64)
                        hp = h // 2
                        ins = nc.tensor.matmul(ps[:, b + h % 2, MEM * hp:MEM * hp + MEM], qmT[hs, hp, q], mkT[hs, hp, :], start=True, stop=True)
                else:
                    hs = slice(64 * g, 64 * g + 64)
                    for j in range(2):
                        ins = nc.tensor.matmul(ps[:, b + j, 0:(t + 1) * P], qT[hs, 2 * rp + j, q], kT[hs, int(kind == "win"), 0:(t + 1) * P], start=True, stop=True)
                ins.then_inc(scores, 1)

            def turn(u):
                t, kind, g, rp = units[u]
                pe.wait_ge(probs, u + 1)
                if u >= 1:
                    pe.wait_ge(pT_a, u)
                    pe.wait_ge(pT_d, u)
                p = prob[:, u % 2, :, :]
                for j in range(2):
                    for c in range(t + 1 if kind in ("sel", "win") else 4):
                        if kind == "cmp":
                            ins = nc.tensor.transpose(ps[0:NC_P, 4 + j, 128 * c:128 * c + 128], p[:, j, 32 * c:32 * c + NC_P], ident)
                        else:
                            ins = nc.tensor.transpose(ps[:, 4 + j, 128 * c:128 * c + 128], p[:, j, 128 * c:128 * c + 128], ident)
                ins.then_inc(p_turned, 1)

            def value(u):
                t, kind, g, rp = units[u]
                add = dict(start=False, stop=False, skip_group_check=True)
                if u % per == 0:
                    if t >= 1:
                        pe.wait_ge(o_out, t)
                    for a in range(2):
                        nc.tensor.matmul(ps[:, 6 + a, :], zb[0:1, 0:P], zb[0:1, :], start=True, stop=False, skip_group_check=True)
                pe.wait_ge(pT_a, u + 1)
                pe.wait_ge(pT_d, u + 1)
                for j in range(2):
                    if kind == "cmp":
                        for r in range(R):
                            c = 2 * r + j
                            ins = nc.tensor.matmul(ps[:, 6, 64 * c:64 * c + 64], pT[0:NC_P, j, 128 * r:128 * r + 128], self.vc[0:NC_P, NB, 64 * j:64 * j + 64], **add)
                    elif kind == "mem":
                        for hp in range(2):
                            h = 2 * hp + j
                            for k in range(2):
                                ins = nc.tensor.matmul(ps[:, 7, 64 * h:64 * h + 64], pT[:, j, 128 * (2 * hp + k):128 * (2 * hp + k) + 128],
                                                       mz[:, k, 256 + 64 * h:320 + 64 * h], **add)
                    else:
                        c = 2 * (2 * rp + j) + g
                        v = V0 + 128 * (1 if kind == "sel" else 2) + 64 * g
                        for k in range(t + 1):
                            ins = nc.tensor.matmul(ps[:, 6, 64 * c:64 * c + 64], pT[:, j, 128 * k:128 * k + 128], z[:, k, v:v + 64], **add)
                if u % per == per - 1:
                    ins.then_inc(o_in_psum, 1)

            pe.wait_ge(out_a, (len(pre) + 1) // 2)
            pe.wait_ge(out_d, len(pre) // 2)
            score(0)
            for u in range(NU):
                if u + 1 < NU:
                    score(u + 1)
                if u >= 1:
                    value(u - 1)
                turn(u)
            value(NU - 1)

        def shape(u):
            t, kind = units[u][0:2]
            return {"cmp": (4, NC_P, 32), "mem": (2, MEM, MEM)}.get(kind, (1, (t + 1) * P, 512))

        def view(a, u):
            n, w, s = shape(u)
            return a[:, :, 0:n * s].rearrange("p j (n s) -> p j n s", n=n)[:, :, :, 0:w]

        @block.vector
        def _(dve):
            ch = Chain(dve, steps)
            nc.vector.tensor_scalar(gate[:, :, :], z[:, 0:TILES, G0:G0 + 24], -80.0, None, ALU.max).then_inc(gclamp, 1)
            dve.wait_ge(gexp, 1)
            ch.then(nc.vector.tensor_scalar(gate[:, :, :], gate[:, :, :], 1.0, None, ALU.add))
            ch.then(nc.vector.reciprocal(gate[:, :, :], gate[:, :, :]))
            for n in range(1, len(pre), 2):
                dve.wait_ge(turned, n + 1)
                nc.vector.tensor_copy(pre[n][1], ps[:, 5, :]).then_inc(out_d, 1)

            def peak(u):
                t, kind = units[u][0:2]
                n, w, s = shape(u)
                b = 2 * (u % 2)
                dve.wait_ge(scores, u + 1)
                sc = view(ps[:, b:b + 2, :], u)
                st_ = stt[:, u % 2, 0:2, :]
                if kind == "cmp":
                    mask = self.c(C_CADD + 32 * t, NC_P).unsqueeze(1).broadcast_to([P, R, NC_P])
                    for j in range(2):
                        ins = nc.vector.tensor_tensor(sc[:, j, :, :], sc[:, j, :, :], mask, ALU.add)
                    ch.then(ins)
                elif kind != "mem":
                    d = sc[:, :, 0, t * P:(t + 1) * P]
                    ch.then(nc.vector.tensor_tensor(d, d, self.c(C_CAUS, P).unsqueeze(1).broadcast_to([P, 2, P]), ALU.add))
                top = stt[:, u % 2, 0, 0:2 * n]
                ch.then(nc.vector.tensor_reduce(top.rearrange("p (j n) -> p j n", j=2), sc, AX.X, ALU.max))
                if kind == "cmp":
                    pr = view(prob[:, u % 2, :, :], u)
                    if u >= 2:
                        dve.wait_ge(p_turned, u - 1)
                    for j in range(2):
                        ins = nc.vector.tensor_tensor(pr[:, j, :, :], sc[:, j, :, :], top[:, 4 * j:4 * j + 4].unsqueeze(2).broadcast_to([P, 4, NC_P]), ALU.subtract)
                    ins.then_inc(peaks, 1)
                else:
                    nc.vector.tensor_scalar(stt[:, u % 2, 1, 0:2 * n], top, -SCALE, None, ALU.mult).then_inc(peaks, 1)

            def weigh(u):
                t, kind, g, rp = units[u]
                n, w, s = shape(u)
                dve.wait_ge(exps, u + 1)
                pr = view(prob[:, u % 2, :, :], u)
                total, f = stt[:, u % 2, 2, 0:2 * n], stt[:, u % 2, 3, 0:2 * n]
                if kind == "cmp":
                    mask = self.c(C_CMUL + 32 * t, NC_P).unsqueeze(1).broadcast_to([P, R, NC_P])
                    for j in range(2):
                        ins = nc.vector.tensor_tensor(pr[:, j, :, :], pr[:, j, :, :], mask, ALU.mult)
                    ch.then(ins)
                    ch.then(nc.vector.tensor_reduce(total.rearrange("p (j n) -> p j n", j=2), pr, AX.X, ALU.add))
                    ch.then(nc.vector.tensor_scalar(total, total, 1e-30, None, ALU.max))
                ch.then(nc.vector.reciprocal(f, total))
                if kind == "cmp":
                    ch.then(nc.vector.tensor_tensor(f.rearrange("p (j r) -> p j r", j=2), f.rearrange("p (j r) -> p j r", j=2),
                                                    gate[:, t, 0:8].rearrange("p (r j) -> p j r", j=2), ALU.mult))
                    for j in range(2):
                        ins = nc.vector.tensor_tensor(pr[:, j, :, :], pr[:, j, :, :], f[:, 4 * j:4 * j + 4].unsqueeze(2).broadcast_to([P, 4, NC_P]), ALU.mult)
                elif kind == "mem":
                    for i in range(4):
                        ins = nc.vector.tensor_scalar(pr[:, i // 2, i % 2, :], pr[:, i // 2, i % 2, :], f[:, i:i + 1], None, ALU.mult)
                else:
                    for j in range(2):
                        c = 8 * (1 if kind == "sel" else 2) + 2 * (2 * rp + j) + g
                        ins = nc.vector.tensor_scalar(pr[:, j, 0, :], pr[:, j, 0, :], f[:, j:j + 1], gate[:, t, c:c + 1], ALU.mult, ALU.mult)
                ins.then_inc(probs, 1)

            peak(0)
            for u in range(NU):
                t, kind = units[u][0:2]
                if u + 1 < NU:
                    peak(u + 1)
                weigh(u)
                dve.wait_ge(p_turned, u + 1)
                rows = NC_P if kind == "cmp" else P
                w = 512 if kind in ("cmp", "mem") else (t + 1) * P
                nc.vector.tensor_copy(pT[0:rows, 1, 0:w], ps[0:rows, 5, 0:w]).then_inc(pT_d, 1)

        @block.scalar
        def _(act):
            act.wait_ge(gclamp, 1)
            nc.scalar.activation(gate[:, :, :], gate[:, :, :], ACT.Exp, scale=-1.0).then_inc(gexp, 1)
            for n in range(0, len(pre), 2):
                act.wait_ge(turned, n + 1)
                nc.scalar.copy(pre[n][1], ps[:, 4, :]).then_inc(out_a, 1)

            def exp(u):
                t, kind = units[u][0:2]
                b = 2 * (u % 2)
                act.wait_ge(peaks, u + 1)
                if u >= 2:
                    act.wait_ge(p_turned, u - 1)
                pr, sc = view(prob[:, u % 2, :, :], u), view(ps[:, b:b + 2, :], u)
                if kind == "cmp":
                    for j in range(2):
                        ins = nc.scalar.activation(pr[:, j, :, :], pr[:, j, :, :], ACT.Exp, scale=SCALE)
                else:
                    n = shape(u)[0]
                    for i in range(2 * n):
                        ins = nc.scalar.activation(pr[:, i // n, i % n, :], sc[:, i // n, i % n, :], ACT.Exp, bias=stt[:, u % 2, 1, i:i + 1],
                                                   scale=SCALE, accum_out=stt[:, u % 2, 2, i:i + 1])
                ins.then_inc(exps, 1)

            exp(0)
            for u in range(NU):
                t, kind = units[u][0:2]
                if u + 1 < NU:
                    exp(u + 1)
                act.wait_ge(p_turned, u + 1)
                rows = NC_P if kind == "cmp" else P
                w = 512 if kind in ("cmp", "mem") else (t + 1) * P
                nc.scalar.copy(pT[0:rows, 0, 0:w], ps[0:rows, 4, 0:w]).then_inc(pT_a, 1)
                if u >= 1 and u % per == 0:
                    act.wait_ge(o_in_psum, t)
                    nc.scalar.copy(o[:, t - 1, 0:512], ps[:, 6, :])
                    nc.scalar.copy(o[:, t - 1, 512:768], ps[:, 7, 0:256]).then_inc(o_out, 1)
            act.wait_ge(o_in_psum, TILES)
            nc.scalar.copy(o[:, TILES - 1, 0:512], ps[:, 6, :])
            nc.scalar.copy(o[:, TILES - 1, 512:768], ps[:, 7, 0:256]).then_inc(o_out, 1)

        self.close(st)

    def mix(self):
        nc, I, O = self.nc, self.ins, self.outs
        st = ExitStack()
        S = lambda n: self.sem(n, st)
        ps, z, o = self.ps, self.z, self.o
        NT = TILES + 1
        bands = self.sb("bands", [P, BW], stack=st)
        state = self.sb("state", [P, 256], stack=st)
        w_pool = self.sb("w_pool", [64, 4, 64], stack=st)
        w_out = self.sb("w_out", [P, KD, D], stack=st)
        rows_g = self.sb("rows_g", [P, 2 * D + 256 + 36], stack=st)
        w_router = self.sb("w_router", [P, KD, 36], stack=st)
        xin = self.sb("xin4", [P, 2, D], stack=st)
        rT = self.sb("rT", [64, 4, P], stack=st)
        mixed = self.sb("mixed", [P, D], stack=st)
        mT = self.sb("mT", [P, KD, P], stack=st)
        h = self.sb("h", [P, 2, D], stack=st)
        hn = self.sb("hn", [P, 2, D], stack=st)
        hT = self.sb("hT", [P, KD, P], stack=st)
        junk = self.sb("junk4", [P, 512], stack=st)
        sq = self.sb("sq", [P, 2, 8], stack=st)
        lg = self.sb("lg", [P, 36], stack=st)
        ro = self.sb("ro", [P, 160], stack=st)
        one = self.sb("one", [P, NT, 2, NEXP], stack=st)
        both = self.sb("both", [P, NT, NEXP], stack=st)
        cnt = self.sb("cnt", [P, NT + 1, NEXP], stack=st)
        scan = self.sb("scan", [P, 3, NEXP], stack=st)
        prod = self.sb("prod", [P, NT, 2, NEXP], stack=st)
        place = self.sb("place", [P, 8, NT * 2], stack=st)
        dest = self.sb("dest", [P, NT * 2], I32, stack=st)
        tok = self.sb("tok", [P, NT], I32, stack=st)
        zero_i = self.sb("zero_i", [CAP, NTILE], I32, stack=st)
        last = self.sb("last", [1, NOVER, NEXP], stack=st)
        consts_in, wout_in = S("mix_consts_in"), S("wout_in")
        stored = [S(f"h_stored{j}") for j in range(2)]
        x_in = [S(f"x4_in{j}") for j in range(2)]
        names = ("mix_dve", "cleared", "r_in_psum", "r_ready", "y_in_psum", "ss_ready", "ms_ready4", "root_ready", "mixed_ready",
                 "mT_in_psum", "mT_ready", "h_in_psum", "hms", "hroot", "hn_ready", "hT_in_psum", "hT_ready", "l_in_psum",
                 "lclear", "lexp", "pair_ready", "cnt_in_psum", "table_zero", "dest_ready", "scattered", "table_in")
        (steps, cleared, r_in_psum, r_ready, y_in_psum, ss_ready, ms_ready, root_ready, mixed_ready,
         mT_in_psum, mT_ready, h_in_psum, hms, hroot, hn_ready, hT_in_psum, hT_ready, l_in_psum,
         lclear, lexp, pair_ready, cnt_in_psum, table_zero, dest_ready, scattered, table_in) = (S(n) for n in names)
        gm, gf, sp_, br = rows_g[:, 0:D], rows_g[:, D:2 * D], rows_g[:, 2 * D:2 * D + 256], rows_g[:, 2 * D + 256:]

        block = st.enter_context(nc.Block("mix"))

        @block.sync
        def _(sp):
            sp.dma_start(bands[:, :], I["bands"]).then_inc(consts_in, 16)
            sp.dma_start(state[0:NB * STATE, :], I["state_pool"]).then_inc(consts_in, 16)
            sp.dma_start(w_pool[:, :, :], I["w_pool"].rearrange("(w c) d -> c w d", w=4)).then_inc(consts_in, 16)
            sp.dma_start(rows_g[:, :], I["mix_rows"].partition_broadcast(P)).then_inc(consts_in, 16)
            for t in range(2):
                sp.dma_start(xin[0:ROWS[t], t, :], I["x"][t * P:t * P + ROWS[t], :]).then_inc(x_in[t], 16)
            for j in range(2):
                sp.dma_start(w_out[:, 4 * j:4 * j + 4, :], I["w_out"].rearrange("(p k) n -> p k n", k=KD)[:, 4 * j:4 * j + 4, :]).then_inc(wout_in, 16)
            sp.dma_start(w_router[:, :, :], I["w_router"].rearrange("(p k) n -> p k n", k=KD)).then_inc(wout_in, 16)
            for t in range(NT):
                r = ROWS[t]
                sp.wait_ge(hn_ready, t + 1)
                sp.dma_start(self.hn_dram[t * P:t * P + r, :], hn[0:r, t % 2, :]).then_inc(stored[t % 2], 16)
                sp.dma_start(self.h_dram[t * P:t * P + r, :], h[0:r, t % 2, :]).then_inc(stored[t % 2], 16)
                if t + 2 < NT:
                    sp.dma_start(xin[0:ROWS[t + 2], t % 2, :], I["x"][(t + 2) * P:(t + 2) * P + ROWS[t + 2], :]).then_inc(x_in[t % 2], 16)
            sp.wait_ge(stored[0], 32 * ((NT + 1) // 2))
            sp.wait_ge(stored[1], 32 * (NT // 2))

        @block.gpsimd
        def _(pool):
            nc.gpsimd.memset(one[:, :, :, :], 0.0).then_inc(cleared, 1)
            nc.gpsimd.memset(cnt[:, :, :], 0.0).then_inc(cleared, 1)
            nc.gpsimd.memset(self.pair_w[:, :, :], 0.0).then_inc(cleared, 1)
            nc.gpsimd.memset(zero_i[:, :], 0).then_inc(cleared, 1)
            pool.wait_ge(cleared, 4)
            pool.dma_start(self.table_dram.rearrange("(s t) o -> s (t o)", t=NTILE), zero_i[:, :]).then_inc(table_zero, 16)
            pool.wait_ge(table_zero, 16)
            pool.wait_ge(dest_ready, 1)
            for t in range(NT):
                for k in range(2):
                    pool.indirect_dma_start(out=self.table_dram, out_offset=bass.IndirectOffsetOnAxis(ap=dest[0:ROWS[t], 2 * t + k:2 * t + k + 1].bitcast(U32), axis=0),
                                            in_=tok[0:ROWS[t], t:t + 1], in_offset=None).then_inc(scattered, 16)
            pool.wait_ge(scattered, 16 * 2 * NT)
            pool.dma_start(self.table[:, :], self.table_dram.rearrange("(s t) o -> s (t o)", t=NTILE)).then_inc(table_in, 16)
            pool.wait_ge(table_in, 16)

        @block.tensor
        def _(pe):
            ident = lambda n: self.consts[0:n, C_ID:C_ID + n]
            pe.wait_ge(consts_in, 64)

            def pool_mix(t):
                r = ROWS[t]
                if t >= 1:
                    pe.wait_ge(r_ready, t)
                band = lambda w, j: bands[:, C_BAND + (3 * w + j) * P:C_BAND + (3 * w + j + 1) * P]
                for w in range(4):
                    u = z[0:r, t, U0 + 64 * w:U0 + 64 * w + 64]
                    out = ps[0:64, 0, 128 * w:128 * w + r]
                    if t == 0:
                        ins = nc.tensor.matmul(out, u, band(w, 2), start=True, stop=True)
                    elif t < TILES:
                        nc.tensor.matmul(out, u, band(w, 0), start=True, stop=False)
                        ins = nc.tensor.matmul(out, z[:, t - 1, U0 + 64 * w:U0 + 64 * w + 64], band(w, 1), start=False, stop=True)
                    else:
                        n = NB * STATE
                        nc.tensor.matmul(out, state[0:n, 64 * w:64 * w + 64], bands[0:n, C_PST + NB * w:C_PST + NB * w + NB], start=True, stop=False)
                        ins = nc.tensor.matmul(out, z[0:NB, t, U0 + 64 * w:U0 + 64 * w + 64], bands[0:NB, C_PDG + NB * w:C_PDG + NB * w + NB], start=False, stop=True)
                ins.then_inc(r_in_psum, 1)
                pe.wait_ge(r_ready, t + 1)
                if t >= 1:
                    pe.wait_ge(ss_ready, t)
                for w in range(4):
                    ins = nc.tensor.matmul(ps[0:r, 1, 64 * w:64 * w + 64], rT[:, w, 0:r], w_pool[:, w, :], start=True, stop=True)
                ins.then_inc(y_in_psum, 1)

            def out_proj(t):
                r = ROWS[t]
                pe.wait_ge(mixed_ready, t + 1)
                if t >= 1:
                    pe.wait_ge(hT_ready, t)
                for k in range(KD):
                    ins = nc.tensor.transpose(ps[:, 2 + k // 4, 128 * (k % 4):128 * (k % 4) + r], mixed[0:r, k:D:KD], ident(r))
                ins.then_inc(mT_in_psum, 1)
                pe.wait_ge(mT_ready, t + 1)
                if t == 0:
                    pe.wait_ge(wout_in, 48)
                for a in range(2):
                    for k in range(KD):
                        ins = nc.tensor.matmul(ps[0:r, 4 + a, :], mT[:, k, 0:r], w_out[:, k, 512 * a:512 * a + 512], start=(k == 0), stop=(k == KD - 1))
                ins.then_inc(h_in_psum, 1)

            def route(t):
                r = ROWS[t]
                pe.wait_ge(hn_ready, t + 1)
                for k in range(KD):
                    ins = nc.tensor.transpose(ps[:, 2 + k // 4, 128 * (k % 4):128 * (k % 4) + r], hn[0:r, t % 2, k:D:KD], ident(r))
                ins.then_inc(hT_in_psum, 1)
                pe.wait_ge(hT_ready, t + 1)
                if t >= 1:
                    pe.wait_ge(lclear, t)
                for k in range(KD):
                    ins = nc.tensor.matmul(ps[0:r, 6, 0:36], hT[:, k, 0:r], w_router[:, k, :], start=(k == 0), stop=(k == KD - 1))
                ins.then_inc(l_in_psum, 1)

            pool_mix(0)
            for t in range(NT):
                if t + 1 < NT:
                    pool_mix(t + 1)
                out_proj(t)
                route(t)
            pe.wait_ge(pair_ready, NT)
            for t in range(NT + 1):
                r = ROWS[t] if t < NT else P
                out = ps[0:r, 7, NEXP * t:NEXP * t + NEXP]
                for s in range(min(t, NT)):
                    ins = nc.tensor.matmul(out, self.c(C_ONE, r, ROWS[s]), both[0:ROWS[s], s, :], start=(s == 0), stop=(t == NT and s == NT - 1))
                if t < NT:
                    ins = nc.tensor.matmul(out, self.c(C_UP, r, r), both[0:r, t, :], start=(t == 0), stop=True)
            ins.then_inc(cnt_in_psum, 1)

        @block.scalar
        def _(act):
            def mixed_T(t):
                r = ROWS[t]
                act.wait_ge(mT_in_psum, t + 1)
                nc.scalar.copy(mT[:, :, 0:r], ps[:, 2:4, :].rearrange("p a (k t) -> p (a k) t", t=P)[:, :, 0:r]).then_inc(mT_ready, 1)

            def root(t):
                act.wait_ge(ms_ready, t + 1)
                nc.scalar.activation(sq[0:ROWS[t], 0, 3:6], sq[0:ROWS[t], 0, 0:3], ACT.Sqrt).then_inc(root_ready, 1)

            root(0)
            for t in range(NT):
                r = ROWS[t]
                mixed_T(t)
                act.wait_ge(hms, t + 1)
                nc.scalar.activation(sq[0:r, 1, 1:2], sq[0:r, 1, 0:1], ACT.Sqrt).then_inc(hroot, 1)
                act.wait_ge(hT_in_psum, t + 1)
                nc.scalar.copy(hT[:, :, 0:r], ps[:, 2:4, :].rearrange("p a (k t) -> p (a k) t", t=P)[:, :, 0:r]).then_inc(hT_ready, 1)
                if t + 1 < NT:
                    root(t + 1)
                act.wait_ge(lclear, t + 1)
                nc.scalar.activation(ro[0:r, 0:5], ro[0:r, 0:5], ACT.Exp).then_inc(lexp, 1)

        @block.vector
        def _(dve):
            ch = Chain(dve, steps)
            dve.wait_ge(consts_in, 64)
            dve.wait_ge(cleared, 4)

            def first_top(dst, src, order, r, n, tmp):
                ch.then(nc.vector.tensor_reduce(tmp[:, 0:1], src, AX.X, ALU.max))
                ch.then(nc.vector.scalar_tensor_tensor(dst, src, tmp[:, 0:1], self.c(order, n, r), ALU.is_equal, ALU.mult))
                ch.then(nc.vector.tensor_reduce(tmp[:, 1:2], dst, AX.X, ALU.max))
                ch.then(nc.vector.tensor_scalar(dst, self.c(order, n, r), tmp[:, 1:2], None, ALU.is_equal))

            def pooled(t):
                r = ROWS[t]
                dve.wait_ge(r_in_psum, t + 1)
                nc.vector.tensor_copy(rT[:, :, 0:r], ps[0:64, 0, :].rearrange("p (w t) -> p w t", w=4)[:, :, 0:r]).then_inc(r_ready, 1)

            def norm_mix(t):
                r = ROWS[t]
                ot = o[:, t, :] if t < TILES else self.o_s[:, :]
                if t >= 1:
                    dve.wait_ge(mT_in_psum, t)
                dve.wait_ge(y_in_psum, t + 1)
                ins = nc.vector.tensor_tensor(mixed[0:r, 0:256], ps[0:r, 1, 0:256], sp_[0:r, :], ALU.mult)
                ins.then_inc(ss_ready, 1)
                dve.wait_ge(ss_ready, t + 1)
                s = sq[0:r, 0, :]
                parts = ((mixed[0:r, 0:256], 0, 256), (ot[0:r, 0:512], 256, 512), (ot[0:r, 512:768], 768, 256))
                for j, (a, at, n) in enumerate(parts):
                    ch.then(nc.vector.tensor_tensor_reduce(junk[0:r, 0:n], a, a, 1.0, 0.0, ALU.mult, ALU.add, s[:, j:j + 1]))
                for j, (a, at, n) in enumerate(parts):
                    ins = nc.vector.tensor_scalar(s[:, j:j + 1], s[:, j:j + 1], 1.0 / n, EPS, ALU.mult, ALU.add)
                ins.then_inc(ms_ready, 1)
                dve.wait_ge(root_ready, t + 1)
                ch.then(nc.vector.reciprocal(s[:, 3:6], s[:, 3:6]))
                for j, (a, at, n) in enumerate(parts):
                    ins = nc.vector.scalar_tensor_tensor(mixed[0:r, at:at + n], a, s[:, 3 + j:4 + j], gm[0:r, at:at + n], ALU.mult, ALU.mult)
                ins.then_inc(mixed_ready, 1)

            def norm_h(t):
                r = ROWS[t]
                dve.wait_ge(h_in_psum, t + 1)
                dve.wait_ge(x_in[t % 2], 16 * (t // 2 + 1))
                if t >= 2:
                    dve.wait_ge(stored[t % 2], 32 * (t // 2))
                ch.then(nc.vector.tensor_tensor(h[0:r, t % 2, :].rearrange("p (a n) -> p a n", a=2), ps[0:r, 4:6, :],
                                                xin[0:r, t % 2, :].rearrange("p (a n) -> p a n", a=2), ALU.add))
                ch.then(nc.vector.tensor_tensor_reduce(hn[0:r, t % 2, :], h[0:r, t % 2, :], h[0:r, t % 2, :], 1.0, 0.0, ALU.mult, ALU.add, sq[0:r, 1, 2:3]))
                nc.vector.tensor_scalar(sq[0:r, 1, 0:1], sq[0:r, 1, 2:3], 1.0 / D, EPS, ALU.mult, ALU.add).then_inc(hms, 1)
                dve.wait_ge(hroot, t + 1)
                ch.then(nc.vector.reciprocal(sq[0:r, 1, 3:4], sq[0:r, 1, 1:2]))
                nc.vector.scalar_tensor_tensor(hn[0:r, t % 2, :], h[0:r, t % 2, :], sq[0:r, 1, 3:4], gf[0:r, :], ALU.mult, ALU.mult).then_inc(hn_ready, 1)

            def choose(t):
                r = ROWS[t]
                dve.wait_ge(l_in_psum, t + 1)
                L = lg[0:r, :]
                ch.then(nc.vector.tensor_tensor(L, ps[0:r, 6, 0:36], br[0:r, :], ALU.add))
                f = lambda a, n: ro[0:r, a:a + n]
                first_top(f(8, 4), L[:, 0:4], C_G4, r, 4, f(72, 2))
                ch.then(nc.vector.tensor_scalar(f(0, 4), L[:, 0:4], f(72, 1), None, ALU.subtract))
                ch.then(nc.vector.tensor_tensor(f(16, 32).rearrange("p (g e) -> p g e", g=4), L[:, 4:36].rearrange("p (g e) -> p g e", g=4),
                                                f(8, 4).unsqueeze(2).broadcast_to([r, 4, 8]), ALU.mult))
                ch.then(nc.vector.tensor_reduce(f(48, 8), f(16, 32).rearrange("p (g e) -> p e g", g=4), AX.X, ALU.add))
                first_top(f(56, 8), f(48, 8), C_E8, r, 8, f(74, 2))
                ch.then(nc.vector.scalar_tensor_tensor(f(80, 8), f(56, 8), NEG, f(48, 8), ALU.mult, ALU.add))
                first_top(f(64, 8), f(80, 8), C_E8, r, 8, f(76, 2))
                nc.vector.tensor_tensor(f(4, 1), f(76, 1), f(74, 1), ALU.subtract).then_inc(lclear, 1)
                dve.wait_ge(lexp, t + 1)
                ch.then(nc.vector.tensor_reduce(f(90, 1), f(0, 4), AX.X, ALU.add))
                ch.then(nc.vector.tensor_scalar(f(91, 1), f(4, 1), 1.0, None, ALU.add))
                ch.then(nc.vector.tensor_tensor(f(92, 1), f(90, 1), f(91, 1), ALU.mult))
                ch.then(nc.vector.reciprocal(self.pair_w[0:r, t, 0:1], f(92, 1)))
                ch.then(nc.vector.tensor_tensor(self.pair_w[0:r, t, 1:2], self.pair_w[0:r, t, 0:1], f(4, 1), ALU.mult))
                for k in range(2):
                    ch.then(nc.vector.tensor_tensor(one[0:r, t, k, :].rearrange("p (g e) -> p g e", g=4), f(8, 4).unsqueeze(2).broadcast_to([r, 4, 8]),
                                                    f(56 + 8 * k, 8).unsqueeze(1).broadcast_to([r, 4, 8]), ALU.mult))
                nc.vector.tensor_tensor(both[0:r, t, :], one[0:r, t, 0, :], one[0:r, t, 1, :], ALU.add).then_inc(pair_ready, 1)

            pooled(0)
            norm_mix(0)
            for t in range(NT):
                if t + 1 < NT:
                    pooled(t + 1)
                norm_h(t)
                if t + 1 < NT:
                    norm_mix(t + 1)
                choose(t)

            dve.wait_ge(cnt_in_psum, 1)
            nc.vector.tensor_copy(cnt[:, 0:TILES, :], ps[:, 7, 0:TILES * NEXP].rearrange("p (t e) -> p t e", t=TILES))
            nc.vector.tensor_copy(cnt[0:NB, TILES, :], ps[0:NB, 7, TILES * NEXP:NT * NEXP])
            ch.then(nc.vector.tensor_copy(cnt[:, NT, :], ps[:, 7, NT * NEXP:(NT + 1) * NEXP]))
            over, a, b = scan[:, 0, :], scan[:, 1, :], scan[:, 2, :]
            ch.then(nc.vector.tensor_scalar(over, cnt[:, NT, :], float(CAP), None, ALU.is_gt))
            for i in range(2, QMAX + 1):
                ch.then(nc.vector.scalar_tensor_tensor(over, cnt[:, NT, :], float(CAP * i), over, ALU.is_gt, ALU.add))
            ch.then(nc.vector.tensor_copy(a, over))
            d = 1
            while d < NEXP:
                nc.vector.tensor_copy(b[:, 0:d], a[:, 0:d])
                ch.then(nc.vector.tensor_tensor(b[:, d:NEXP], a[:, d:NEXP], a[:, 0:NEXP - d], ALU.add))
                a, b = b, a
                d *= 2
            ch.then(nc.vector.tensor_copy(self.n_over[:, :], a[0:1, NEXP - 1:NEXP]))
            ch.then(nc.vector.tensor_tensor(last[:, :, :], a[0:1, :].unsqueeze(1).broadcast_to([1, NOVER, NEXP]),
                                            self.c(C_MAIN, NOVER, 1).unsqueeze(2).broadcast_to([1, NOVER, NEXP]), ALU.is_le))
            ch.then(nc.vector.tensor_reduce(prod[0:1, 0, 0, 0:NOVER], last[:, :, :], AX.X, ALU.add))
            ch.then(nc.vector.tensor_scalar(self.over_e[:, :], prod[0:1, 0, 0, 0:NOVER], float(NEXP - 1), None, ALU.min))
            ch.then(nc.vector.tensor_tensor(b, a, over, ALU.subtract))
            v = lambda j: place[:, j, :]
            one3 = one[:, :, :, :].rearrange("p t k e -> p (t k) e")
            prod3 = prod[:, :, :, :].rearrange("p t k e -> p (t k) e")
            RANK, EXP, BASE, QQ, SLOT, TILE, OV = range(7)
            for k in range(2):
                ins = nc.vector.tensor_tensor(prod[:, :, k, :], one[:, :, k, :], cnt[:, 0:NT, :], ALU.mult)
            ch.then(ins)
            ch.then(nc.vector.tensor_reduce(v(RANK), prod3, AX.X, ALU.add))
            ch.then(nc.vector.tensor_tensor(prod3, one3, self.c(C_EI, NEXP).unsqueeze(1).broadcast_to([P, 2 * NT, NEXP]), ALU.mult))
            ch.then(nc.vector.tensor_reduce(v(EXP), prod3, AX.X, ALU.add))
            ch.then(nc.vector.tensor_tensor(prod3, one3, b.unsqueeze(1).broadcast_to([P, 2 * NT, NEXP]), ALU.mult))
            ch.then(nc.vector.tensor_reduce(v(BASE), prod3, AX.X, ALU.add))
            ch.then(nc.vector.tensor_scalar(v(QQ), v(RANK), float(CAP), None, ALU.is_ge))
            for i in range(2, QMAX + 1):
                ch.then(nc.vector.scalar_tensor_tensor(v(QQ), v(RANK), float(CAP * i), v(QQ), ALU.is_ge, ALU.add))
            ch.then(nc.vector.scalar_tensor_tensor(v(SLOT), v(QQ), -float(CAP), v(RANK), ALU.mult, ALU.add))
            ch.then(nc.vector.tensor_scalar(v(OV), v(QQ), 0.0, None, ALU.is_gt))
            ch.then(nc.vector.scalar_tensor_tensor(v(TILE), v(QQ), float(NEXP - 1), v(BASE), ALU.add, ALU.add))
            ch.then(nc.vector.tensor_tensor(v(TILE), v(TILE), v(EXP), ALU.subtract))
            ch.then(nc.vector.tensor_tensor(v(TILE), v(TILE), v(OV), ALU.mult))
            ch.then(nc.vector.tensor_tensor(v(TILE), v(TILE), v(EXP), ALU.add))
            ch.then(nc.vector.scalar_tensor_tensor(v(RANK), v(SLOT), float(NTILE), v(TILE), ALU.mult, ALU.add))
            nc.vector.tensor_copy(dest[:, :], v(RANK))
            ch.then(nc.vector.tensor_copy(tok[:, :], self.c(C_TOK, NT)))
            ch.then(nc.vector.scalar_tensor_tensor(v(BASE), v(TILE), float(CAP), v(SLOT), ALU.mult, ALU.add))
            nc.vector.tensor_copy(self.pair_row[:, :], v(BASE)).then_inc(dest_ready, 1)

        self.close(st)

    def experts(self):
        nc, I = self.nc, self.ins
        st = ExitStack()
        S = lambda n: self.sem(n, st)
        ps = self.ps
        FH = FF // 2
        wg = self.sb("wg", [P, 2, KD, FF], stack=st)
        wu = self.sb("wu", [P, 2, KD, FF], stack=st)
        wd = self.sb("wd", [P, 2, 2, KF // 2, D], stack=st)
        xg = self.sb("xg", [CAP, 2, D], stack=st)
        xT = self.sb("xTe", [P, 2, KD, CAP], stack=st)
        gc = self.sb("gc", [2 * CAP, 2, FF // 2], stack=st)
        hh = self.sb("hh", [2 * CAP, 2, FF // 2], stack=st)
        hT = self.sb("hTe", [P, KF // 2, 2 * CAP], stack=st)
        yb = self.sb("yb", [2 * CAP, 2, D // 2], stack=st)
        g_in, u_in, d_in = ([S(f"{n}_in{j}") for j in range(2)] for n in ("wg", "wu", "wd"))
        xg_in, y_out = ([S(f"{n}{j}") for j in range(2)] for n in ("xg_in", "y_out"))
        (x_turned, xT_ready, gate_done, up_done, gc_ready, ge_ready, hh_ready, h_turned, hT_ready, y_in_psum, y_copied, steps) = (
            S(n) for n in ("x_turned", "xTe_ready", "gate_done", "up_done", "gc_ready", "ge_ready", "hh_ready",
                           "h_turned", "hTe_ready", "ye_in_psum", "y_copied", "experts_dve"))
        vg = I["w_gate"].rearrange("(e p k) f -> e p k f", p=P, k=KD)
        vu = I["w_up"].rearrange("(e p k) f -> e p k f", p=P, k=KD)
        vd = I["w_down"].rearrange("(e h p j) f -> e p h j f", h=2, p=P, j=KF // 2)
        ys = self.ys_dram.rearrange("(n s) d -> n s d", s=CAP)
        at = lambda v, n: v[bass.ds(n, 1), :, :, :].rearrange("e p k f -> (e p) k f")
        block = st.enter_context(nc.Block("experts"))

        @block.sync
        def _(sp):
            def load(n, slot):
                sp.dma_start(wg[:, slot, :, :], at(vg, n)).then_inc(g_in[slot], 16)
                sp.dma_start(wu[:, slot, :, :], at(vu, n)).then_inc(u_in[slot], 16)

            def load_down(n, slot):
                sp.dma_start(wd[:, slot, :, :, :], vd[bass.ds(n, 1), :, :, :, :].rearrange("e p h j f -> (e p) h j f")).then_inc(d_in[slot], 16)

            for n in range(2):
                load(n, n)
                load_down(n, n)
            with sp.Fori(1, NEXP // 2) as i:
                for slot in range(2):
                    sp.wait_ge(up_done, i * 4 + 2 * (slot - 1))
                    load(i * 2 + slot, slot)
                    sp.wait_ge(y_in_psum, i * 4 + 2 * (slot - 1))
                    load_down(i * 2 + slot, slot)

        @block.gpsimd
        def _(pool):

            for n in range(NEXP):
                if n >= 2:
                    pool.wait_ge(x_turned, n - 1)
                pool.indirect_dma_start(out=xg[:, n % 2, :], out_offset=None, in_=self.hn_dram,
                                        in_offset=bass.IndirectOffsetOnAxis(ap=self.table[:, n:n + 1].bitcast(U32), axis=0)).then_inc(xg_in[n % 2], 16)

        @block.tensor
        def _(pe):
            def turn(out, rows, chunks):
                m, w = rows.shape
                ident = self.consts[0:m, C_ID:C_ID + m]
                for k in range(chunks):
                    dst, src = ps[:, out, m * k:m * k + m], rows[:, k:w:chunks]
                    if k == 0:
                        ins = nc.tensor.matmul(dst, src, ident, start=True, stop=True)
                    else:
                        ins = nc.tensor.transpose(dst, src, ident)
                return ins

            def gate_up(n, slot, half):
                pe.wait_ge(xT_ready, n + 1)
                for w, sem, bank, done in ((wg, g_in, slot, gate_done), (wu, u_in, 2 + slot, up_done)):
                    pe.wait_ge(sem[slot], half * 16)
                    for k in range(KD):
                        for h in range(2):
                            ins = nc.tensor.matmul(ps[h * CAP:h * CAP + CAP, bank, 0:FH], xT[:, slot, k, :], w[:, slot, k, h * FH:h * FH + FH],
                                                   start=(k == 0), stop=(k == KD - 1))
                            if k == KD - 1:
                                ins.then_inc(done, 1)

            def turn_x(n, slot, half, first=False):
                pe.wait_ge(xg_in[slot], half * 16)
                if not first:
                    pe.wait_ge(xT_ready, n)
                turn(4, xg[:, slot, :], KD).then_inc(x_turned, 1)

            def down(n, slot, half, first=False):
                pe.wait_ge(hT_ready, n + 1)
                pe.wait_ge(d_in[slot], half * 16)
                if not first:
                    pe.wait_ge(y_copied, n)
                for k in range(KF):
                    h, j = k // (KF // 2), k % (KF // 2)
                    for a in range(2):
                        ins = nc.tensor.matmul(ps[a * CAP:a * CAP + CAP, 6 + slot, :], hT[:, j, h * CAP:h * CAP + CAP], wd[:, slot, h, j, 512 * a:512 * a + 512],
                                               start=(k == 0), stop=(k == KF - 1))
                        if k == KF - 1:
                            ins.then_inc(y_in_psum, 1)

            def turn_h(n, slot):
                pe.wait_ge(hh_ready, n + 1)
                turn(5, hh[:, slot, :], KF // 2).then_inc(h_turned, 1)

            turn_x(0, 0, 1, first=True)
            gate_up(0, 0, 1)
            turn_x(1, 1, 1)
            turn_h(0, 0)
            gate_up(1, 1, 1)
            turn_x(2, 0, 2)
            down(0, 0, 1, first=True)
            turn_h(1, 1)
            with pe.Fori(1, NEXP // 2 - 1) as i:
                for slot in range(2):
                    n = i * 2 + slot
                    gate_up(n, slot, i + 1)
                    turn_x(n + 1, 1 - slot, i + 1 + slot)
                    down(n + (-1), 1 - slot, i + slot)
                    turn_h(n, slot)
            n, half = NEXP - 2, NEXP // 2
            gate_up(n, 0, half)
            turn_x(n + 1, 1, half)
            down(n - 1, 1, half - 1)
            turn_h(n, 0)
            gate_up(n + 1, 1, half)
            down(n, 0, half)
            turn_h(n + 1, 1)
            down(n + 1, 1, half)

        @block.vector
        def _(dve):
            def link(ins, count):
                ins.then_inc(steps, 1)
                dve.wait_ge(steps, count)

            def take_x(n, slot):
                dve.wait_ge(x_turned, n + 1)
                nc.vector.tensor_copy(xT[:, slot, :, :].rearrange("p k s -> p (k s)"), ps[:, 4, 0:KD * CAP]).then_inc(xT_ready, 1)

            def act_fn(n, slot):
                g, u = ps[0:2 * CAP, slot, 0:FH], ps[0:2 * CAP, 2 + slot, 0:FH]
                dve.wait_ge(gate_done, n * 2 + 2)
                nc.vector.tensor_scalar(gc[:, slot, :], g, -80.0, None, ALU.max).then_inc(gc_ready, 1)
                dve.wait_ge(ge_ready, n + 1)
                link(nc.vector.tensor_scalar(gc[:, slot, :], gc[:, slot, :], 1.0, None, ALU.add), n * 3 + 1)
                link(nc.vector.reciprocal(gc[:, slot, :], gc[:, slot, :]), n * 3 + 2)
                link(nc.vector.tensor_tensor(gc[:, slot, :], gc[:, slot, :], g, ALU.mult), n * 3 + 3)
                dve.wait_ge(up_done, n * 2 + 2)
                nc.vector.tensor_tensor(hh[:, slot, :], gc[:, slot, :], u, ALU.mult).then_inc(hh_ready, 1)

            def take_h(n):
                dve.wait_ge(h_turned, n + 1)
                nc.vector.tensor_copy(hT[:, :, :].rearrange("p k s -> p (k s)"), ps[:, 5, 0:KF * CAP]).then_inc(hT_ready, 1)

            take_x(0, 0)
            take_x(1, 1)
            act_fn(0, 0)
            take_h(0)
            take_x(2, 0)
            act_fn(1, 1)
            take_h(1)
            take_x(3, 1)
            act_fn(2, 0)
            take_h(2)
            with dve.Fori(1, NEXP // 2 - 1) as i:
                for s in range(2):
                    n = i * 2 + (1 + s)
                    slot = (1 + s) % 2
                    take_x(n + 1, 1 - slot)
                    act_fn(n, slot)
                    take_h(n)
            n = NEXP - 1
            act_fn(n, 1)
            take_h(n)

        @block.scalar
        def _(act):
            def exp(n, slot):
                act.wait_ge(gc_ready, n + 1)
                nc.scalar.activation(gc[:, slot, :], gc[:, slot, :], ACT.Exp, scale=-1.0).then_inc(ge_ready, 1)

            def take_y(n, slot, uses):
                act.wait_ge(y_in_psum, n * 2 + 2)
                if uses is not None:
                    act.wait_ge(y_out[slot], uses * 32)
                nc.scalar.copy(yb[:, slot, :], ps[0:2 * CAP, 6 + slot, :]).then_inc(y_copied, 1)
                act.wait_ge(y_copied, n + 1)
                for h in range(2):
                    act.dma_start(ys[bass.ds(n, 1), :, 512 * h:512 * h + 512].rearrange("o s d -> (o s) d"), yb[h * CAP:h * CAP + CAP, slot, :]).then_inc(y_out[slot], 16)

            exp(0, 0)
            exp(1, 1)
            take_y(0, 0, None)
            exp(2, 0)
            take_y(1, 1, None)
            with act.Fori(1, NEXP // 2 - 1) as i:
                for s in range(2):
                    n = i * 2 + (1 + s)
                    slot = (1 + s) % 2
                    exp(n, slot)
                    take_y(n + (-1), 1 - slot, i)
            n = NEXP - 1
            exp(n, 1)
            take_y(n - 1, 0, NEXP // 2 - 1)
            take_y(n, 1, NEXP // 2 - 1)
            for slot in range(2):
                act.wait_ge(y_out[slot], 32 * (NEXP // 2))

        self.close(st)

    def overflow(self):
        nc, I = self.nc, self.ins
        st = ExitStack()
        S = lambda n: self.sem(n, st)
        ps = self.ps
        wg = self.sb("wgo", [P, KD, FF], stack=st)
        wu = self.sb("wuo", [P, KD, FF], stack=st)
        wd = self.sb("wdo", [P, KF, D], stack=st)
        xg = self.sb("xgo", [CAP, D], stack=st)
        xT = self.sb("xTo", [P, KD, CAP], stack=st)
        gc = self.sb("gco", [CAP, FF], stack=st)
        hh = self.sb("hho", [CAP, FF], stack=st)
        hT = self.sb("hTo", [P, KF, CAP], stack=st)
        yb = self.sb("ybo", [CAP, D], stack=st)
        (tile_free, w_in, xg_in, x_turned, xT_ready, gate_up, gc_ready, ge_ready, a1, a2, a3, hh_ready, h_turned, hT_ready,
         y_in_psum, y_ready, y_out) = (S(n) for n in (
             "tile_free", "o_w_in", "o_xg_in", "o_x_turned", "o_xT", "o_gate_up", "o_gc", "o_ge", "o_a1", "o_a2", "o_a3",
             "o_hh", "o_h_turned", "o_hT", "o_y_psum", "o_y_ready", "o_y_out"))
        vg = I["w_gate"].rearrange("(e p k) f -> e p k f", p=P, k=KD)
        vu = I["w_up"].rearrange("(e p k) f -> e p k f", p=P, k=KD)
        vd = I["w_down"].rearrange("(e p k) f -> e p k f", p=P, k=KF)
        ys = self.ys_dram.rearrange("(n s) d -> n s d", s=CAP)
        at = lambda v, n: v[bass.ds(n, 1), :, :, :].rearrange("e p k f -> (e p) k f")

        def needed(eng):
            return eng.If(eng.value_load(self.n_over[0:1, 0:1], min_val=0, max_val=NOVER) > 0)

        block = st.enter_context(nc.Block("overflow"))

        @block.sync
        def _(sp):
            with needed(sp):
                with sp.Fori(0, NOVER) as j:
                    sp.wait_ge(tile_free, j + 1)
                    e = sp.value_load(self.over_e[0:1, bass.ds(j, 1)], min_val=0, max_val=NEXP - 1)
                    sp.dma_start(wg[:, :, :], at(vg, e)).then_inc(w_in, 16)
                    sp.dma_start(wu[:, :, :], at(vu, e)).then_inc(w_in, 16)
                    sp.dma_start(wd[:, :, :], at(vd, e)).then_inc(w_in, 16)

        @block.gpsimd
        def _(pool):
            with needed(pool):
                pool.sem_inc(tile_free, 1)
                for j in range(NOVER):
                    pool.indirect_dma_start(out=xg[:, :], out_offset=None, in_=self.hn_dram,
                                            in_offset=bass.IndirectOffsetOnAxis(ap=self.table[:, NEXP + j:NEXP + j + 1].bitcast(U32), axis=0)).then_inc(xg_in, 16)
                    pool.wait_ge(y_out, 16 * (j + 1))
                    pool.sem_inc(tile_free, 1)

        @block.tensor
        def _(pe):
            ident = self.consts[0:CAP, C_ID:C_ID + CAP]

            def turn(out, rows, chunks):
                w = rows.shape[-1]
                for k in range(chunks):
                    dst, src = ps[:, out, CAP * k:CAP * k + CAP], rows[:, k:w:chunks]
                    if k == 0:
                        ins = nc.tensor.matmul(dst, src, ident, start=True, stop=True)
                    else:
                        ins = nc.tensor.transpose(dst, src, ident)
                return ins

            with needed(pe):
                with pe.Fori(0, NOVER) as j:
                    pe.wait_ge(xg_in, j * 16 + 16)
                    turn(4, xg[:, :], KD).then_inc(x_turned, 1)
                    pe.wait_ge(xT_ready, j + 1)
                    pe.wait_ge(w_in, j * 48 + 48)
                    for a, w in enumerate((wg, wu)):
                        for k in range(KD):
                            ins = nc.tensor.matmul(ps[0:CAP, a, :], xT[:, k, :], w[:, k, :], start=(k == 0), stop=(k == KD - 1))
                    ins.then_inc(gate_up, 1)
                    pe.wait_ge(hh_ready, j + 1)
                    turn(5, hh[:, :], KF).then_inc(h_turned, 1)
                    pe.wait_ge(hT_ready, j + 1)
                    for a in range(2):
                        for k in range(KF):
                            ins = nc.tensor.matmul(ps[0:CAP, 6 + a, :], hT[:, k, :], wd[:, k, 512 * a:512 * a + 512], start=(k == 0), stop=(k == KF - 1))
                    ins.then_inc(y_in_psum, 1)

        @block.vector
        def _(dve):
            with needed(dve):
                with dve.Fori(0, NOVER) as j:
                    dve.wait_ge(x_turned, j + 1)
                    nc.vector.tensor_copy(xT[:, :, :].rearrange("p k s -> p (k s)"), ps[:, 4, 0:KD * CAP]).then_inc(xT_ready, 1)
                    dve.wait_ge(gate_up, j + 1)
                    nc.vector.tensor_scalar(gc[:, :], ps[0:CAP, 0, :], -80.0, None, ALU.max).then_inc(gc_ready, 1)
                    dve.wait_ge(ge_ready, j + 1)
                    nc.vector.tensor_scalar(gc[:, :], gc[:, :], 1.0, None, ALU.add).then_inc(a1, 1)
                    dve.wait_ge(a1, j + 1)
                    nc.vector.reciprocal(gc[:, :], gc[:, :]).then_inc(a2, 1)
                    dve.wait_ge(a2, j + 1)
                    nc.vector.tensor_tensor(gc[:, :], gc[:, :], ps[0:CAP, 0, :], ALU.mult).then_inc(a3, 1)
                    dve.wait_ge(a3, j + 1)
                    nc.vector.tensor_tensor(hh[:, :], gc[:, :], ps[0:CAP, 1, :], ALU.mult).then_inc(hh_ready, 1)
                    dve.wait_ge(h_turned, j + 1)
                    nc.vector.tensor_copy(hT[:, :, :].rearrange("p k s -> p (k s)"), ps[:, 5, 0:KF * CAP]).then_inc(hT_ready, 1)
                    dve.wait_ge(y_in_psum, j + 1)
                    nc.vector.tensor_copy(yb[:, :].rearrange("p (a n) -> p a n", a=2), ps[0:CAP, 6:8, :]).then_inc(y_ready, 1)

        @block.scalar
        def _(act):
            with needed(act):
                with act.Fori(0, NOVER) as j:
                    act.wait_ge(gc_ready, j + 1)
                    nc.scalar.activation(gc[:, :], gc[:, :], ACT.Exp, scale=-1.0).then_inc(ge_ready, 1)
                    act.wait_ge(y_ready, j + 1)
                    act.dma_start(ys[bass.ds(j + NEXP, 1), :, :].rearrange("o s d -> (o s) d"), yb[:, :]).then_inc(y_out, 16)

        self.close(st)

    def combine(self):
        nc, O = self.nc, self.outs
        st = ExitStack()
        S = lambda n: self.sem(n, st)
        NT = TILES + 1
        rows = self.sb("rows", [P, NT, 2, D], stack=st)
        h = self.sb("h7", [P, NT, D], stack=st)
        rows_in = [S(f"rows_in{t}") for t in range(NT)]
        h_in = S("h_in")
        steps, y_ready, stored = S("combine_dve"), S("y_ready"), S("y_stored")
        block = st.enter_context(nc.Block("combine"))

        @block.gpsimd
        def _(pool):
            for t in range(NT):
                for k in range(2):
                    pool.indirect_dma_start(out=rows[0:ROWS[t], t, k, :], out_offset=None, in_=self.ys_dram,
                                            in_offset=bass.IndirectOffsetOnAxis(ap=self.pair_row[0:ROWS[t], 2 * t + k:2 * t + k + 1].bitcast(U32), axis=0)).then_inc(rows_in[t], 16)
            pool.wait_ge(self.moved, 32)
            pool.wait_ge(self.blanked, 16)

        @block.vector
        def _(dve):
            ch = Chain(dve, steps)
            dve.wait_ge(h_in, 16 * NT)
            for t in range(NT):
                r = ROWS[t]
                dve.wait_ge(rows_in[t], 32)
                ch.then(nc.vector.scalar_tensor_tensor(h[0:r, t, :], rows[0:r, t, 0, :], self.pair_w[0:r, t, 0:1], h[0:r, t, :], ALU.mult, ALU.add))
                nc.vector.scalar_tensor_tensor(h[0:r, t, :], rows[0:r, t, 1, :], self.pair_w[0:r, t, 1:2], h[0:r, t, :], ALU.mult, ALU.add).then_inc(y_ready, 1)

        @block.sync
        def _(sp):
            for t in range(NT):
                sp.dma_start(h[0:ROWS[t], t, :], self.h_dram[t * P:t * P + ROWS[t], :]).then_inc(h_in, 16)
            for t in range(NT):
                sp.wait_ge(y_ready, t + 1)
                sp.dma_start(O["y"][t * P:t * P + ROWS[t], :], h[0:ROWS[t], t, :]).then_inc(stored, 16)
            sp.wait_ge(stored, 16 * NT)

        self.close(st)

    def run(self):
        nc = self.nc
        sb = self.sb
        with self.stack:
            self.moved = self.sem("moved", self.stack)
            self.blanked = self.sem("blanked", self.stack)
            self.ps = self.stack.enter_context(nc.psum_tensor("ps", [P, 8, 512], F32))
            self.pz = self.ps[:, 0:4, :]
            self.pt = self.ps[:, 4:6, :].rearrange("p a (k t) -> p (a k) t", t=P)
            self.gate_dram = nc.dram_tensor("gate_dram", [NB, 24], F32).ap()
            self.h_dram = nc.dram_tensor("h_dram", [NTOK, D], F32).ap()
            self.hn_dram = nc.dram_tensor("hn_dram", [NTOK, D], F32).ap()
            self.table_dram = nc.dram_tensor("table_dram", [CAP * NTILE, 1], I32).ap()
            self.ys_dram = nc.dram_tensor("ys_dram", [CAP * NTILE, D], F32).ap()
            self.consts = sb("consts", [P, CW])
            self.table = sb("table", [CAP, NTILE], I32)
            self.pair_w = sb("pair_w", [P, TILES + 1, 2])
            self.pair_row = sb("pair_row", [P, 2 * (TILES + 1)], I32)
            self.over_e = sb("over_e", [1, NOVER], I32)
            self.n_over = sb("n_over", [1, 1], I32)
            with ExitStack() as front:
                self.z = sb("z", [P, TILES + 1, ZW], stack=front)
                self.o_s = sb("o_s", [NB, 768], stack=front)
                with ExitStack() as blocks:
                    self.kcT = sb("kcT", [P, NSEQ, 64], stack=blocks)
                    self.vc = sb("vc", [64, NSEQ, 128], stack=blocks)
                    self.project()
                    self.stream()
                    self.o = sb("o", [P, TILES, 768], stack=blocks)
                    self.attend()
                    self.mix()
            self.experts()
            self.overflow()
            self.combine()


def kernel(**inputs):
    import numpy as np
    import concourse.bacc as bacc
    from concourse.bass_utils import run_bass_kernel_spmd

    f = {k: np.asarray(v) for k, v in inputs.items()}
    heads = [g * R + r for r in range(R) for g in range(G)]
    col = lambda base, unit, order: [base + o * unit + j for o in order for j in range(unit)]
    kv = 768
    order = (list(range(256)) + col(256, HD, heads)
             + [kv + ((br * 2 + 0) * G + g) * HD + j for br in range(3) for g in range(G) for j in range(HD)]
             + list(range(1560, 1816))
             + [kv + ((br * 2 + 1) * G + g) * HD + j for br in range(3) for g in range(G) for j in range(HD)]
             + [1536 + h * 3 + br for br in range(3) for h in heads])
    mixed = list(range(256)) + col(256, HD, heads) + list(range(768, 1024))
    arrays = {
        "consts": constants()[0], "bands": constants()[1],
        "x": np.concatenate([f["x_prompt"][0], f["x_sample"][:, 0]], 0),
        "mem": f["mem_prompt"][0],
        "w_in": f["w_in"][0][:, order],
        "w_mem": f["w_mem_kv"][0],
        "g_rows": np.concatenate([f["g_attn"], f["g_mem"]], 0),
        "g_head": np.concatenate([np.tile(f["g_q"][0], H), np.repeat(f["g_k"][0][:, None], G, 1).reshape(-1),
                                  np.tile(f["g_mq"][0], MH), np.tile(f["g_mk"][0], MH)]),
        "cache_kv": f["cache_kv"][0].reshape(-1, 512),
        "cache_win": f["cache_win"][0].reshape(-1, 256),
        "cache_mem": f["cache_mem_kv"][0].reshape(-1, 512),
        "state_pool": f["state_pool"][0].reshape(-1, 256),
        "page_table": f["page_table"].reshape(1, -1).astype(np.int32),
        "pe": np.ascontiguousarray(f["pe_cmp"][0].reshape(2, 16, 128).transpose(2, 0, 1)),
        "w_cmp1": f["w_cmp1"][0], "w_cmp2": f["w_cmp2"][0],
        "w_pool": f["w_pool"][0].reshape(-1, 64),
        "w_out": f["w_out"][0][mixed],
        "mix_rows": np.concatenate([f["g_mix"][0][mixed], f["g_ffn"][0], f["s_pool"][0], f["b_router1"][0], f["b_router2"][0].reshape(-1)]),
        "w_router": np.concatenate([f["w_router1"][0], f["w_router2"][0].reshape(D, -1)], 1),
        "w_gate": f["w_gate"][0].reshape(-1, FF), "w_up": f["w_up"][0].reshape(-1, FF),
        "w_down": f["w_down"][0].reshape(-1, D),
    }
    shapes = {
        "y": (NTOK, D), "kv_p": (T, 512), "kv_s": (NB, 512), "win_p": (T, 256), "win_s": (NB * T, 256),
        "pool_p": (STATE, 256), "pool_s": (NB * STATE, 256), "mem_p": (MEM, 512),
    }
    nc = bacc.Bacc("TRN2", target_bir_lowering=False, num_devices=1)
    arrays = {k: np.ascontiguousarray(v) for k, v in arrays.items()}
    ins = {k: nc.dram_tensor(f"in_{k}", v.shape, mybir.dt.from_np(v.dtype), kind="ExternalInput").ap() for k, v in arrays.items()}
    outs = {k: nc.dram_tensor(f"out_{k}", s, F32, kind="ExternalOutput").ap() for k, s in shapes.items()}
    Kernel(nc, ins, outs).run()
    r = run_bass_kernel_spmd(nc, [{f"in_{k}": v for k, v in arrays.items()}], core_ids=[0]).results[0]
    o = {k: r[f"out_{k}"] for k in shapes}
    return (o["y"][:T].reshape(1, T, D), o["y"][T:].reshape(NB, 1, D),
            o["kv_p"].reshape(1, 1, T, 4, 2, 64), o["kv_s"].reshape(1, NB, 1, 4, 2, 64),
            o["win_p"].reshape(1, 1, T, 2, 2, 64), o["win_s"].reshape(1, NB, T, 2, 2, 64),
            o["pool_p"].reshape(1, 1, STATE, 256), o["pool_s"].reshape(1, NB, STATE, 256),
            o["mem_p"].reshape(1, 1, MEM, 2, 4, 64))
```

```python
from contextlib import ExitStack

import concourse.bass as bass
from concourse import mybir

F32 = mybir.dt.float32
BF16 = mybir.dt.bfloat16
I32 = mybir.dt.int32
U32 = mybir.dt.uint32
ALU = mybir.AluOpType
ACT = mybir.ActivationFunctionType
AX = mybir.AxisListType

P = 128
D = 1024
KD = D // P
T = 512
NB = 8
PAST = 1024
PAGE = 128
HD = 64
R, G = 4, 2
H = R * G
MEM = 256
MH = 4
EPS = 1e-6
SCALE = HD ** -0.5
NEG = -1e30
WINDOWS = (2, 4, 8, 16)
STATE = 15
TILES = T // P
ROWS = [P] * TILES + [NB]
NC_P = T // 16 - 1
NC_S = PAST // 16 - 1
NSEQ = NB + 1

U0, Q0, K0, M0, V0, G0 = 0, 256, 768, 1152, 1408, 1792
ZW = 1816
ZC = ZW // 4
NG = (V0 - Q0) // HD

NEXP = 32
FF = 512
KF = FF // P
CAP = 64
NTOK = T + NB
NOVER = (2 * NTOK) // (CAP + 1)
NTILE = NEXP + NOVER
QMAX = (NTOK - 1) // CAP

C_ID = 0
C_CAUS = C_ID + P
C_CADD = C_CAUS + P
C_CMUL = C_CADD + TILES * 32
C_COS = C_CMUL + TILES * 32
C_SIN = C_COS + 5 * 8
C_UP = C_SIN + 5 * 8
C_ONE = C_UP + P
C_RG = C_ONE + P
C_S8 = C_RG + 64
C_BLK = C_S8 + NB
C_G4 = C_BLK + 14
C_E8 = C_G4 + 4
C_EI = C_E8 + 8
C_MAIN = C_EI + 32
C_TOK = C_MAIN + NOVER
C_SEL = C_TOK + TILES + 1
CW = C_SEL + 16 * NB

C_BAND = 0
C_PST = C_BAND + 12 * P
C_PDG = C_PST + 4 * NB
BW = C_PDG + 4 * NB

def constants():
    import numpy as np
    c = np.zeros((P, CW), np.float32)
    i = np.arange(P)
    c[:, C_ID:C_ID + P] = np.eye(P)
    c[:, C_CAUS:C_CAUS + P] = np.where(i[None, :] <= i[:, None], 0.0, NEG)
    for t in range(TILES):
        ok = (np.arange(32)[None, :] * 16 + 31 <= (t * P + i)[:, None]) & (np.arange(32) < NC_P)[None, :]
        c[:, C_CADD + 32 * t:C_CADD + 32 * t + 32] = np.where(ok, 0.0, NEG)
        c[:, C_CMUL + 32 * t:C_CMUL + 32 * t + 32] = ok
    inv = np.power(np.float32(500000.0), -np.arange(8, dtype=np.float32) * np.float32(2.0) / np.float32(16))
    for t in range(5):
        pos = (t * P + i if t < TILES else np.full(P, PAST)).astype(np.float32)
        ang = pos[:, None] * inv[None, :]
        c[:, C_COS + 8 * t:C_COS + 8 * t + 8] = np.cos(ang)
        c[:, C_SIN + 8 * t:C_SIN + 8 * t + 8] = np.sin(ang)
    bands = np.zeros((P, BW), np.float32)
    for w, win in enumerate(WINDOWS):
        tin, tout = i[:, None], i[None, :]
        eye = (tin == tout).astype(np.float32)
        own = ((tin <= tout) & (tout - tin < win)) / np.float32(win) - eye
        before = ((tout + P - tin < win) & (tout + P - tin > 0)) / np.float32(win)
        first = ((tin <= tout) & (tout - tin < win)) / np.minimum(tout + 1, win).astype(np.float32) - eye
        for j, m in enumerate((own, before, first)):
            o = C_BAND + (3 * w + j) * P
            bands[:, o:o + P] = m
        for b in range(NB):
            for s in range(STATE):
                if s >= STATE - (win - 1):
                    bands[b * STATE + s, C_PST + w * NB + b] = 1.0 / win
            bands[b, C_PDG + w * NB + b] = 1.0 / win - 1.0
    c[:, C_UP:C_UP + P] = i[:, None] < i[None, :]
    c[:, C_ONE:C_ONE + P] = 1.0
    j = np.arange(64)
    c[:64, C_RG:C_RG + 64] = (j[:, None] // 8 == j[None, :] // 8) & (j[:, None] % 2 == j[None, :] % 2)
    c[:64, C_S8:C_S8 + NB] = j[:, None] // 8 == np.arange(NB)[None, :]
    c[:, C_BLK:C_BLK + 14] = np.arange(1, 15)
    c[:, C_G4:C_G4 + 4] = [4, 3, 2, 1]
    c[:, C_E8:C_E8 + 8] = np.arange(8, 0, -1)
    c[:, C_EI:C_EI + 32] = np.arange(32)
    c[:, C_MAIN:C_MAIN + NOVER] = np.arange(NOVER)
    c[:, C_TOK:C_TOK + 5] = i[:, None] + P * np.arange(5)[None, :]
    for u in range(2):
        for h in range(8):
            for b in range(4):
                c[32 * b + h, C_SEL + NB * (8 * u + h) + 4 * u + b] = 1.0
    return c, bands


class Chain:

    def __init__(self, eng, sem):
        self.eng, self.sem, self.n = eng, sem, 0

    def then(self, ins):
        self.n += 1
        ins.then_inc(self.sem, 1)
        self.eng.wait_ge(self.sem, self.n)


class Kernel:
    def __init__(self, nc, ins, outs):
        self.nc, self.ins, self.outs = nc, ins, outs
        self.stack = ExitStack()
        self.n_sems, self.stage_sems = 0, []

    def sb(self, name, shape, dt=F32, stack=None):
        return (stack or self.stack).enter_context(self.nc.sbuf_tensor(name, shape, dt))

    def sem(self, name, stack):
        self.n_sems += 1
        s = self.nc.alloc_semaphore(f"{name}_{self.n_sems}")
        if stack is not self.stack:
            self.stage_sems.append(s)
        return s

    def close(self, stage):
        stage.close()
        self.nc.clear_and_free_semaphores(self.stage_sems)
        self.nc.all_engine_barrier()
        self.stage_sems = []

    def c(self, at, n, rows=P):
        return self.consts[0:rows, at:at + n]

    def load_pages(self, eng, b, slot):
        src = self.ins["cache_kv"].rearrange("(g p t) c -> g p (t c)", p=64, t=2)
        for pg in range(PAST // PAGE):
            at = eng.value_load(self.pages[0:1, bass.ds(b * NB + pg, 1)], min_val=0, max_val=src.shape[0] - 1)
            half = slice(64 * (pg % 2), 64 * (pg % 2) + 64)
            eng.dma_start(self.raw[half, slot, pg // 2, :, :].rearrange("p t c -> p (t c)"),
                          src[bass.ds(at, 1), :, :].rearrange("g p c -> (g p) c")).then_inc(self.kv_in[slot], 16)

    def project(self):
        nc, I, O = self.nc, self.ins, self.outs
        st = ExitStack()
        n_items = 7
        rows = ROWS + [P, P]
        w_in = self.sb("w_in", [P, KD, ZW], stack=st)
        w_mem = self.raw[:, 1, :, :, :].rearrange("p a b c -> p (a b) c")
        g_rows = self.sb("g_rows", [P, 2, D], stack=st)
        g_head = self.sb("g_head", [P, V0 - Q0 + HD * MH], stack=st)
        xin = self.sb("xin", [P, 3, D], stack=st)
        xn = self.sb("xn", [P, 2, D], stack=st)
        xT = self.sb("xT", [P, 2, KD, P], stack=st)
        junk = self.sb("junk", [P, 2, V0 - Q0], stack=st)
        stat = self.sb("stat", [P, n_items, 4], stack=st)
        gstat = self.sb("gstat", [P, n_items, NG], stack=st)
        blank = self.w1[0:CAP, :, :, :].rearrange("p a b c -> p (a b c)")[:, 0:D]
        blank_ready = self.sem("blank_ready", st)
        S = lambda n: self.sem(n, st)
        consts_in, gains_in, win_in, wmem_in = S("consts_in"), S("gains_in"), S("win_in"), S("wmem_in")
        x_in = [S(f"x_in{j}") for j in range(3)]
        dve_step, act_step = S("dve_step"), S("act_step")
        xn_ready, xT_in_psum, xT_ready, z_in_psum, z_ready = (S(n) for n in (
            "xn_ready", "xT_in_psum", "xT_ready", "z_in_psum", "z_ready"))
        ms_ready, rms_ready, sq_ready, gms_ready, grms_ready, z_done, stored = (S(n) for n in (
            "ms_ready", "rms_ready", "sq_ready", "gms_ready", "grms_ready", "z_done", "stored"))
        pz, pt = self.pz, self.pt
        z = self.z
        memz = w_in[:, 0, 0:1024].rearrange("p (j n) -> p j n", j=2)
        xs = [I["x"][t * P:t * P + rows[t], :] for t in range(5)] + [I["mem"][j * P:(j + 1) * P, :] for j in range(2)]

        def zt(t):
            return z[:, t, :] if t < 5 else memz[:, t - 5, :]

        def groups(t):
            return (Q0, NG) if t < 5 else (0, MH)

        chunks = [4] * 5 + [1, 1]
        done = lambda t: sum(chunks[:t])

        def in_psum(t, a):
            if t < TILES:
                return pz[:, a, 0:ZC]
            return pz[32 * a:32 * a + NB, a, 0:ZC] if t == TILES else pz[:, t - 5, :]

        block = st.enter_context(nc.Block("project"))

        @block.sync
        def _(sp):
            sp.dma_start(xin[0:rows[0], 0, :], xs[0]).then_inc(x_in[0], 16)
            sp.dma_start(self.consts[:, :], I["consts"]).then_inc(consts_in, 16)
            sp.dma_start(g_rows[:, :, :], I["g_rows"].partition_broadcast(P)).then_inc(gains_in, 16)
            for j in range(4):
                sp.dma_start(w_in[:, 2 * j:2 * j + 2, :], I["w_in"].rearrange("(p k) n -> p k n", k=KD)[:, 2 * j:2 * j + 2, :]).then_inc(win_in, 16)
                if j == 0:
                    sp.dma_start(xin[0:rows[1], 1, :], xs[1]).then_inc(x_in[1], 16)
            for t in range(1, n_items):
                if t >= 3:
                    sp.wait_ge(xn_ready, t - 2)
                if t >= 2:
                    sp.dma_start(xin[0:rows[t], t % 3, :], xs[t]).then_inc(x_in[t % 3], 16)
                if t == 1:
                    sp.dma_start(g_head[:, :], I["g_head"].partition_broadcast(P)).then_inc(gains_in, 16)
                    sp.dma_start(w_mem[:, :, :], I["w_mem"].rearrange("(p k) n -> p k n", k=KD)).then_inc(wmem_in, 16)
            sp.dma_start(self.pages[:, :], I["page_table"]).then_inc(self.pages_in, 16)
            sp.wait_ge(self.pages_in, 16)
            self.load_pages(sp, 0, 0)
            sp.wait_ge(self.blanked, 16)
            sp.dma_start(self.w1[:, :, :, :], I["w_cmp1"].rearrange("q (l p) n -> p q l n", p=P)).then_inc(self.w1_in, 16)
            k3 = lambda t, r: z[0:r, t, K0:K0 + 384].rearrange("p (b c) -> p b c", b=3)
            v3 = lambda t, r: z[0:r, t, V0:V0 + 384].rearrange("p (b c) -> p b c", b=3)
            for t in range(5):
                r = rows[t]
                sp.wait_ge(z_done, t + 1)
                if t < TILES:
                    kv, win, at = O["kv_p"], O["win_p"], t * P
                else:
                    kv, win, at = O["kv_s"], None, 0
                dst = kv[at:at + r, :].rearrange("p (b s c) -> p b s c", b=2, s=2)
                sp.dma_start(dst[:, :, 0, :], k3(t, r)[:, 0:2, :]).then_inc(stored, 16)
                sp.dma_start(dst[:, :, 1, :], v3(t, r)[:, 0:2, :]).then_inc(stored, 16)
                if t < TILES:
                    sp.dma_start(win[at:at + r, 0:128], k3(t, r)[:, 2, :]).then_inc(stored, 16)
                    sp.dma_start(win[at:at + r, 128:256], v3(t, r)[:, 2, :]).then_inc(stored, 16)
                else:
                    dst = O["win_s"].rearrange("(b n) c -> b n c", b=NB)[:, T - 1, :]
                    sp.dma_start(dst[:, 0:128], k3(t, r)[:, 2, :]).then_inc(stored, 16)
                    sp.dma_start(dst[:, 128:256], v3(t, r)[:, 2, :]).then_inc(stored, 16)
                    sp.dma_start(O["pool_s"].rearrange("(b n) c -> b n c", b=NB)[:, STATE - 1, :],
                                 z[0:NB, t, U0:U0 + 256]).then_inc(stored, 16)
            sp.dma_start(O["pool_p"], z[P - STATE:P, TILES - 1, U0:U0 + 256]).then_inc(stored, 16)
            for j in range(2):
                sp.wait_ge(z_done, 6 + j)
                sp.dma_start(O["mem_p"][j * P:(j + 1) * P, :], memz[:, j, :]).then_inc(stored, 16)
            sp.wait_ge(stored, 16 * (4 * TILES + 5 + 1 + 2))

        @block.gpsimd
        def _(pool):
            nc.gpsimd.memset(blank[:, :], 0.0).then_inc(blank_ready, 1)
            pool.wait_ge(blank_ready, 1)
            pool.wait_ge(win_in, 64)
            pool.dma_start(self.ys_dram[NEXP * CAP:, :].rearrange("(a p) d -> p a d", p=CAP), blank[:, :].unsqueeze(1).broadcast_to([CAP, NOVER, D])).then_inc(self.blanked, 16)
            src = I["cache_win"].rearrange("(b n) c -> b (n c)", b=NB)
            dst = O["win_s"].rearrange("(b n) c -> b (n c)", b=NB)
            w = (T - 1) * 256
            pool.dma_start(dst[:, 0:w].rearrange("b (a n) -> b a n", a=7), src[:, 256:256 + w].rearrange("b (a n) -> b a n", a=7)).then_inc(self.moved, 16)
            src = I["state_pool"].rearrange("(b n) c -> b (n c)", b=NB)
            dst = O["pool_s"].rearrange("(b n) c -> b (n c)", b=NB)
            pool.dma_start(dst[:, 0:(STATE - 1) * 256], src[:, 256:STATE * 256]).then_inc(self.moved, 16)
            pool.wait_ge(self.blanked, 16)

        @block.vector
        def _(dve):
            ch = Chain(dve, dve_step)

            def norm(t):
                r = rows[t]
                dve.wait_ge(x_in[t % 3], 16 * (t // 3 + 1))
                if t >= 2:
                    dve.wait_ge(xT_in_psum, t - 1)
                ch.then(nc.vector.tensor_tensor_reduce(xn[0:r, t % 2, :], xin[0:r, t % 3, :], xin[0:r, t % 3, :], 1.0, 0.0,
                                                       ALU.mult, ALU.add, stat[0:r, t, 0:1]))
                nc.vector.tensor_scalar(stat[0:r, t, 1:2], stat[0:r, t, 0:1], 1.0 / D, EPS, ALU.mult, ALU.add).then_inc(ms_ready, 1)
                dve.wait_ge(rms_ready, t + 1)
                ch.then(nc.vector.reciprocal(stat[0:r, t, 3:4], stat[0:r, t, 2:3]))
                if t == 0:
                    dve.wait_ge(gains_in, 32)
                nc.vector.scalar_tensor_tensor(xn[0:r, t % 2, :], xin[0:r, t % 3, :], stat[0:r, t, 3:4],
                                               g_rows[0:r, 0 if t < 5 else 1, :], ALU.mult, ALU.mult).then_inc(xn_ready, 1)

            def heads(t):
                r = rows[t]
                at, n = groups(t)
                w = n * HD
                buf = zt(t)[0:r, at:at + w]
                b3 = buf.rearrange("p (n d) -> p n d", d=HD)
                dve.wait_ge(sq_ready, t + 1)
                ch.then(nc.vector.tensor_reduce(gstat[0:r, t, 0:n], junk[0:r, t % 2, 0:w].rearrange("p (n d) -> p n d", d=HD), AX.X, ALU.add))
                nc.vector.tensor_scalar(gstat[0:r, t, 0:n], gstat[0:r, t, 0:n], 1.0 / HD, EPS, ALU.mult, ALU.add).then_inc(gms_ready, 1)
                dve.wait_ge(grms_ready, t + 1)
                ch.then(nc.vector.reciprocal(gstat[0:r, t, 0:n], gstat[0:r, t, 0:n]))
                ch.then(nc.vector.tensor_tensor(b3, b3, gstat[0:r, t, 0:n].unsqueeze(2).broadcast_to([r, n, HD]), ALU.mult))
                last = nc.vector.tensor_tensor(buf, buf, g_head[0:r, 0:w] if t < 5 else g_head[0:r, V0 - Q0:V0 - Q0 + w], ALU.mult)
                if t >= 5:
                    last.then_inc(z_done, 1)
                    return
                ch.then(last)
                h3 = zt(t)[0:r, Q0:M0].rearrange("p (n d) -> p n d", d=HD)
                x1, x2 = h3[:, :, 0:8], h3[:, :, 8:16]
                cos = self.c(C_COS + 8 * t, 8, r).unsqueeze(1).broadcast_to([r, 14, 8])
                sin = self.c(C_SIN + 8 * t, 8, r).unsqueeze(1).broadcast_to([r, 14, 8])
                if t == 0:
                    dve.wait_ge(consts_in, 16)
                rot = junk[0:r, t % 2, 0:448].rearrange("p (j n d) -> p j n d", j=4, d=8)
                for j, (a, b) in enumerate(((x1, cos), (x2, sin), (x2, cos), (x1, sin))):
                    last = nc.vector.tensor_tensor(rot[:, j, :, :], a, b, ALU.mult)
                ch.then(last)
                nc.vector.tensor_tensor(x1, rot[:, 0, :, :], rot[:, 1, :, :], ALU.subtract)
                nc.vector.tensor_tensor(x2, rot[:, 2, :, :], rot[:, 3, :, :], ALU.add).then_inc(z_done, 1)

            norm(0)
            norm(1)
            for t in range(n_items):
                if t + 2 < n_items:
                    norm(t + 2)
                heads(t)

        @block.scalar
        def _(act):
            def root(t):
                act.wait_ge(ms_ready, t + 1)
                nc.scalar.activation(stat[0:rows[t], t, 2:3], stat[0:rows[t], t, 1:2], ACT.Sqrt).then_inc(rms_ready, 1)

            def roots(t):
                n = groups(t)[1]
                act.wait_ge(gms_ready, t + 1)
                nc.scalar.activation(gstat[0:rows[t], t, 0:n], gstat[0:rows[t], t, 0:n], ACT.Sqrt).then_inc(grms_ready, 1)

            def take_x(t):
                act.wait_ge(xT_in_psum, t + 1)
                if t >= 2:
                    act.wait_ge(z_in_psum, done(t - 1))
                nc.scalar.copy(xT[:, t % 2, :, 0:rows[t]], pt[:, :, 0:rows[t]]).then_inc(xT_ready, 1)

            root(0)
            root(1)
            take_x(0)
            for t in range(n_items):
                r = rows[t]
                if t + 1 < n_items:
                    take_x(t + 1)
                if t + 2 < n_items:
                    root(t + 2)
                for a in range(chunks[t]):
                    act.wait_ge(z_in_psum, done(t) + a + 1)
                    dst = z[0:r, t, a * ZC:(a + 1) * ZC] if t < 5 else memz[:, t - 5, :]
                    nc.scalar.copy(dst, in_psum(t, a)).then_inc(z_ready, 1)
                act.wait_ge(z_ready, done(t + 1))
                at, n = groups(t)
                if t >= 2:
                    act.wait_ge(z_done, t - 1)
                nc.scalar.activation(junk[0:r, t % 2, 0:n * HD], zt(t)[0:r, at:at + n * HD], ACT.Square).then_inc(sq_ready, 1)
                roots(t)

        @block.tensor
        def _(pe):
            def turn(t):
                r = rows[t]
                pe.wait_ge(xn_ready, t + 1)
                if t >= 1:
                    pe.wait_ge(xT_ready, t)
                for k in range(KD):
                    ins = nc.tensor.transpose(pt[:, k, 0:r], xn[0:r, t % 2, k:D:KD], self.c(C_ID, r, r))
                ins.then_inc(xT_in_psum, 1)

            def bank_free(t, a):
                if t < 5:
                    before = done(t - 1) + a + 1 if t >= 1 else 0
                else:
                    before = done(5)
                if before:
                    pe.wait_ge(z_ready, before)

            def product(t, a, k):
                r = rows[t]
                rhs = w_in[:, k, a * ZC:(a + 1) * ZC] if t < 5 else w_mem[:, k, :]
                ins = nc.tensor.matmul(in_psum(t, a), xT[:, t % 2, k, 0:r], rhs, start=(k == 0), stop=(k == KD - 1))
                if k == KD - 1:
                    ins.then_inc(z_in_psum, 1)

            pe.wait_ge(consts_in, 16)
            turn(0)
            for t in range(n_items):
                if t + 1 < n_items:
                    turn(t + 1)
                pe.wait_ge(xT_ready, t + 1)
                if t == 5:
                    pe.wait_ge(wmem_in, 16)
                if t == 0 or t == TILES:
                    for a in range(4):
                        bank_free(t, a)
                    for k in range(KD):
                        if t == 0 and k % 2 == 0:
                            pe.wait_ge(win_in, 16 * (k // 2 + 1))
                        for a in range(4):
                            product(t, a, k)
                else:
                    for a in range(chunks[t]):
                        bank_free(t, a)
                        for k in range(KD):
                            product(t, a, k)

        self.close(st)

    def stream(self):
        nc, I, O = self.nc, self.ins, self.outs
        st = ExitStack()
        S = lambda n: self.sem(n, st)
        raw, w1 = self.raw, self.w1
        kvc = self.sb("kvc", [P, 4, 4, 2, 64], stack=st)
        winK = self.sb("winK", [P, 2, 4, 128], stack=st)
        memK = self.sb("memK", [P, 2, 2, 256], stack=st)
        XT = self.sb("XT", [P, 2, G, 512], stack=st)
        KsT = self.sb("KsT", [P, 1024], stack=st)
        KwT = self.sb("KwT", [P, 512], stack=st)
        KmT = self.sb("KmT", [P, 2, 256], stack=st)
        w2 = self.sb("w2", [P, 2, 64], stack=st)
        w2pad = self.sb("w2pad", [P, G, 128], stack=st)
        pe_pos = self.sb("pe_pos", [P, 2, 16], stack=st)
        hbias = self.sb("hbias", [P, 2], stack=st)
        hx = self.sb("hx", [P, 2, 256], stack=st)
        ht = self.sb("ht", [P, 256], stack=st)
        gel = self.sb("gel", [P, 2, 256], stack=st)
        Vs = self.sb("Vs", [P, NB, 4, 2, 128], stack=st)
        Vw = self.sb("Vw", [P, NB, 4, 128], stack=st)
        Vm = self.sb("Vm", [P, NB, 2, 256], stack=st)
        Q = self.sb("Q", [P, NB * 72], stack=st)
        Qm = self.sb("Qm", [P, 2, NB * 36], stack=st)
        kTn = self.sb("kTn", [P, 2, NB], stack=st)
        zb = self.sb("zb", [1, 512], BF16, stack=st)
        pages, kv_in = self.pages, self.kv_in
        gat = self.sb("gat", [NB, 24], stack=st)
        g64 = self.sb("g64", [64, 3], stack=st)
        wk_in, mk_in = ([S(f"{n}_in{j}") for j in range(2)] for n in ("wk", "mk"))
        v_in, w_in_, zeroed, steps_d, vs_ready = (S(n) for n in ("v_in", "cmp_w_in", "zeroed", "stream_dve", "vs_ready"))
        small_in_psum, q_ready, turned, out_a, out_d, kvc_ready = (S(n) for n in (
            "small_in_psum", "q_ready", "turned", "out_a", "out_d", "kvc_ready"))
        hid_in_psum, hx_ready, he_ready, gel_ready, cmp_in_psum, cmp_ready = (S(n) for n in (
            "hid_in_psum", "hx_ready", "he_ready", "gel_ready", "cmp_in_psum", "cmp_ready"))
        gate_out, gate_in, gclamp, gexp, gsig = (S(n) for n in ("gate_out", "gate_in", "gclamp", "gexp", "gsig"))
        cs_in_psum, ec, pc, imp_in_psum, es, ps_ready, pT_in_psum, pT_ready, o_in_psum, oT_ready, os_in_psum = (S(n) for n in (
            "cs_in_psum", "ec", "pc", "imp_in_psum", "es", "ps_ready", "pT_in_psum", "pT_ready", "o_in_psum", "oT_ready", "os_in_psum"))
        ps, z = self.ps, self.z
        sel0, win0, misc, hid, cmp_ = ps[:, 0:2, :], ps[:, 2, :], ps[:, 3, :], ps[:, 6, :], ps[:, 7, :]
        kcT, vc = self.kcT, self.vc
        smp = TILES
        blocks = [NC_S] * NB + [NC_P]
        ntile = [4] * NB + [2]
        units = [8] * NB + [4]
        first = [8 * s for s in range(NSEQ)]
        kind = lambda s, u: u if s < NB else u + 4
        hidv = hid.rearrange("p (q n) -> p q n", q=4)

        late = raw[:, 1, :, :, :].rearrange("p a b c -> p (a b c)")
        ssb, swb, smb = late[0:64, 0:1040], late[0:64, 1040:1568], late[0:32, 2400:2656]
        pTw = late[:, 1568:1824].rearrange("p (a b) -> p a b", a=4)
        pTm = late[:, 1824:1888].rearrange("p (a b) -> p a b", a=2)
        pTs = late[:, 1888:2400].rearrange("p (a b) -> p a b", a=8)
        dgn = late[0:64, 2656:2784].rearrange("p (a b) -> p a b", a=2)
        nw = late[0:NB, 2784:2912].rearrange("p (a b) -> p a b", a=2)
        oa, om = late[:, 2912:3168], late[:, 3168:3680]
        scb = self.sb("scb", [64, 64], stack=st)
        sst = self.sb("sst", [64, 4, 4], stack=st)
        imp = self.sb("imp", [64, 6, 16], stack=st)
        pTc = self.sb("pTc", [64, 64], stack=st)

        block = st.enter_context(nc.Block("stream"))

        marks = {}

        @block.vector
        def _(dve):
            ch = Chain(dve, steps_d)
            dve.wait_ge(zeroed, 6)
            def out(s):
                for u in range(1, units[s], 2):
                    dve.wait_ge(turned, first[s] + u + 1)
                    k = kind(s, u)
                    dst = (XT[:, (k - 4) // 2, 1, :] if k >= 4 else KsT[:, 512:1024] if k == 1
                           else KmT[:, :, :].rearrange("p a n -> p (a n)"))
                    w = 128 * ntile[s]
                    nc.vector.tensor_copy(dst[:, 0:w], ps[:, 5, 0:w]).then_inc(out_d, 1)

            def gelu(s):
                n = blocks[s]
                dve.wait_ge(hid_in_psum, s + 1)
                x = hx[:, s % 2, :].rearrange("p (q n) -> p q n", q=4)[:, :, 0:n]
                t = ht[:, :].rearrange("p (q n) -> p q n", q=4)[:, :, 0:n]
                for q in range(2):
                    ins = nc.vector.tensor_scalar(x[:, 2 * q:2 * q + 2, :], hidv[:, 2 * q:2 * q + 2, 0:n], hbias[:, q:q + 1], None, ALU.add)
                ch.then(ins)
                ch.then(nc.vector.tensor_tensor(t, x, x, ALU.mult))
                ch.then(nc.vector.tensor_scalar(t, t, 0.044715, 1.0, ALU.mult, ALU.add))
                ch.then(nc.vector.tensor_tensor(t, t, x, ALU.mult))
                nc.vector.tensor_scalar(t, t, -50.0, None, ALU.max).then_inc(hx_ready, 1)
                dve.wait_ge(he_ready, s + 1)
                ch.then(nc.vector.tensor_scalar(t, t, 1.0, None, ALU.add))
                ch.then(nc.vector.reciprocal(t, t))
                if s >= 2:
                    dve.wait_ge(cmp_in_psum, s - 1)
                nc.vector.tensor_tensor(gel[:, s % 2, :].rearrange("p (q n) -> p q n", q=4)[:, :, 0:n], t, x, ALU.mult).then_inc(gel_ready, 1)

            def keep(s):
                n = blocks[s]
                dve.wait_ge(cmp_in_psum, s + 1)
                nc.vector.tensor_copy(kcT[:, s, 0:n], cmp_[:, 0:n])
                nc.vector.tensor_copy(vc[0:n, s, :], cmp_[0:n, 128:256]).then_inc(cmp_ready, 1)

            nc.vector.tensor_scalar(gat[:, :], z[0:NB, smp, G0:G0 + 24], -80.0, None, ALU.max).then_inc(gclamp, 1)
            out(0)
            dve.wait_ge(small_in_psum, 1)
            nc.vector.tensor_copy(hbias[:, :], hid[:, 0:2])
            nc.vector.tensor_copy(w2pad[:, 0, 0:64], w2[:, 0, :])
            nc.vector.tensor_copy(w2pad[:, 1, 64:128], w2[:, 0, :])
            nc.vector.tensor_copy(kTn[:, :, :], cmp_[:, 48:64].rearrange("p (a b) -> p a b", a=2))
            for g in range(G):
                half = slice(64 * g, 64 * g + 64)
                nc.vector.tensor_copy(Q[half, :].rearrange("p (b x) -> p b x", x=72)[:, :, g:g + 2 * R:2],
                                      cmp_[half, 0:32].rearrange("p (r b) -> p b r", r=R))
                for hp in range(2):
                    h = 2 * hp + g
                    ins = nc.vector.tensor_copy(Qm[half, hp, :].rearrange("p (b x) -> p b x", x=36)[:, :, h:h + 1],
                                                cmp_[half, 32 + 8 * hp:40 + 8 * hp].unsqueeze(2))
            ins.then_inc(q_ready, 1)
            dve.wait_ge(gexp, 1)
            ch.then(nc.vector.tensor_scalar(gat[:, :], gat[:, :], 1.0, None, ALU.add))
            nc.vector.reciprocal(gat[:, :], gat[:, :]).then_inc(gsig, 1)
            for s in range(NSEQ):
                if s + 1 < NSEQ:
                    out(s + 1)
                gelu(s)
                if s >= 1:
                    keep(s - 1)
            keep(NSEQ - 1)

            def peak(j, rows, src, mark):
                ch.then(nc.vector.tensor_reduce(sst[0:rows, j, 0:1], src, AX.X, ALU.max))
                ch.then(nc.vector.tensor_scalar(sst[0:rows, j, 1:2], sst[0:rows, j, 0:1], -SCALE, None, ALU.mult))
                marks[mark] = ch.n

            def weights(j, rows, probs, gate, mark):
                ch.then(nc.vector.reciprocal(sst[0:rows, j, 3:4], sst[0:rows, j, 2:3]))
                if gate is None:
                    ch.then(nc.vector.tensor_scalar(probs, probs, sst[0:rows, j, 3:4], None, ALU.mult))
                else:
                    ch.then(nc.vector.tensor_scalar(probs, probs, sst[0:rows, j, 3:4], gate, ALU.mult, ALU.mult))
                if mark:
                    marks[mark] = ch.n

            dve.wait_ge(cs_in_psum, 1)
            dve.wait_ge(vs_ready, NB)
            ch.then(nc.vector.tensor_copy(scb[:, 0:NC_S], misc[0:64, 0:NC_S]))
            peak(0, 64, scb[:, 0:NC_S], "cmax")
            ch.then(nc.vector.tensor_copy(smb[:, :], misc[0:32, 128:384]))
            peak(1, 32, smb[:, :], "mmax")
            nc.vector.memset(swb[:, 0:1], 0.0)
            nc.vector.tensor_copy(swb[:, 1:512], win0[0:64, 1:512])
            ch.then(nc.vector.tensor_copy(swb[:, 512:513], misc[0:64, 65:66]))
            peak(2, 64, swb[:, 1:513], "wmax")
            dve.wait_ge(es, 1)
            weights(0, 64, scb[:, 0:NC_S], None, "pc")
            dve.wait_ge(es, 2)
            weights(1, 32, smb[:, :], None, "mp")
            dve.wait_ge(imp_in_psum, 1)
            ch.then(nc.vector.tensor_reduce(imp[:, 0, :], hid[0:64, 0:64].rearrange("p (n k) -> p n k", k=4), AX.X, ALU.add))
            ch.then(nc.vector.tensor_reduce(sst[:, 0, 0:1], imp[:, 0, 1:15], AX.X, ALU.min))
            ch.then(nc.vector.scalar_tensor_tensor(imp[:, 1, 1:15], imp[:, 0, 1:15], sst[:, 0, 0:1], self.c(C_BLK, 14, 64), ALU.is_equal, ALU.mult))
            ch.then(nc.vector.tensor_reduce(sst[:, 0, 1:2], imp[:, 1, 1:15], AX.X, ALU.max))
            ch.then(nc.vector.tensor_scalar(imp[:, 2, 1:15], self.c(C_BLK, 14, 64), sst[:, 0, 1:2], NEG, ALU.is_equal, ALU.mult))
            for par in range(2):
                v = lambda a: a.rearrange("p (c t k j) -> p c t k j", c=4, t=2, k=4)[:, :, par, :, :]
                out4 = ssb[:, 0:1024].rearrange("p (c t k j) -> p c t k j", c=4, t=2, k=4)
                in4 = sel0[0:64, :, :].rearrange("p a (c t k j) -> p (a c) t k j", c=2, t=2, k=4)
                mask = imp[:, 2, :].rearrange("p (c k) -> p c k", c=4).unsqueeze(3).broadcast_to([64, 4, 4, 32])
                nc.vector.tensor_tensor(out4[:, :, par, :, :], in4[:, :, par, :, :], mask, ALU.add)
            ch.then(nc.vector.tensor_copy(ssb[:, 1024:1025], misc[0:64, 64:65]))
            peak(3, 64, ssb[:, 0:1025], "smax")
            dve.wait_ge(gate_in, 16 * NB)
            ch.then(nc.vector.tensor_scalar(scb[:, 0:NC_S], scb[:, 0:NC_S], g64[:, 0:1], None, ALU.mult))
            dve.wait_ge(es, 3)
            weights(2, 64, swb[:, 1:513], g64[:, 2:3], None)
            ch.then(nc.vector.tensor_scalar(dgn[:, 1, :], self.c(C_ID, 64, 64), swb[:, 512:513], None, ALU.mult))
            marks["wp"] = ch.n
            dve.wait_ge(es, 4)
            weights(3, 64, ssb[:, 0:1025], g64[:, 1:2], None)
            ch.then(nc.vector.tensor_scalar(dgn[:, 0, :], self.c(C_ID, 64, 64), ssb[:, 1024:1025], None, ALU.mult))
            marks["sp"] = ch.n
            dve.wait_ge(pT_in_psum, 1)
            nc.vector.tensor_copy(late[:, 1568:1824], ps[:, 5, 0:256])
            nc.vector.tensor_copy(pTc[0:NC_S, :], ps[0:NC_S, 5, 256:320])
            nc.vector.tensor_copy(late[:, 1824:1888], ps[:, 5, 448:512])
            nc.vector.tensor_copy(nw[:, 1, :], ps[0:NB, 5, 384:448]).then_inc(pT_ready, 1)
            dve.wait_ge(pT_in_psum, 2)
            nc.vector.tensor_copy(late[:, 1888:2400], ps[:, 4, :])
            nc.vector.tensor_copy(nw[:, 0, :], hid[0:NB, 256:320]).then_inc(pT_ready, 1)
            dve.wait_ge(o_in_psum, 4)
            nc.vector.tensor_copy(oa, cmp_[:, 0:256])
            nc.vector.tensor_copy(om, ps[:, 0, :]).then_inc(oT_ready, 1)
            dve.wait_ge(os_in_psum, 1)
            nc.vector.tensor_copy(self.o_s[:, 0:512], ps[0:NB, 4, :])
            nc.vector.tensor_copy(self.o_s[:, 512:768], ps[0:NB, 5, 0:256])

        @block.sync
        def _(sp):
            sp.dma_start(w2[:, :, :], I["w_cmp2"].rearrange("q p n -> p q n")).then_inc(w_in_, 16)
            sp.dma_start(pe_pos[:, :, :], I["pe"]).then_inc(w_in_, 16)
            self.load_pages(sp, 1, 1)
            with sp.Fori(1, NB // 2) as i:
                for slot in range(2):
                    sp.wait_ge(turned, i * 16 + (slot * 8 - 8))
                    sp.wait_ge(vs_ready, i * 2 + (slot - 1))
                    self.load_pages(sp, i * 2 + slot, slot)
            sp.wait_ge(turned, 8 * (NB - 1))
            sp.wait_ge(vs_ready, NB - 1)
            for c in range(2):
                sp.dma_start(raw[:, 0, c, :, 0:256], O["kv_p"][256 * c:256 * c + 256, 0:256].rearrange("(p t) c -> p t c", t=2)).then_inc(kv_in[0], 16)

        @block.gpsimd
        def _(pool):
            nc.gpsimd.memset(Q[:, :], 0.0).then_inc(zeroed, 1)
            nc.gpsimd.memset(Qm[:, :, :], 0.0).then_inc(zeroed, 1)
            nc.gpsimd.memset(w2pad[:, :, :], 0.0).then_inc(zeroed, 1)
            nc.gpsimd.memset(zb[:, :], 0.0).then_inc(zeroed, 1)
            nc.gpsimd.memset(scb[:, :], 0.0).then_inc(zeroed, 1)
            nc.gpsimd.memset(imp[:, :, :], 0.0).then_inc(zeroed, 1)

            def sort(s):
                pool.wait_ge(kv_in[s % 2], 128 * (s // 2 + 1) if s < NB else 128 * (NB // 2) + 32)
                if s >= 1:
                    pool.wait_ge(turned, first[s - 1] + 8)
                for c in range(ntile[s]):
                    ins = nc.gpsimd.tensor_copy(kvc[:, c, :, :, :], raw[:, s % 2, c, :, 0:256].rearrange("p t (a d) -> p a t d", a=4))
                ins.then_inc(kvc_ready, 1)

            sort(0)
            pool.wait_ge(gsig, 1)
            pool.dma_start(self.gate_dram, gat[:, :]).then_inc(gate_out, 16)
            pool.wait_ge(gate_out, 16)
            with nc.allow_non_contiguous_dma("192 gates"):
                for b in range(NB):
                    pool.dma_start(g64[H * b:H * b + H, :], self.gate_dram[b].rearrange("(q c) -> c q", q=3)).then_inc(gate_in, 16)
            for s in range(1, NSEQ):
                sort(s)

        @block.scalar
        def _(act):
            srcw = I["cache_win"].rearrange("(b p j) c -> b p j c", b=NB, j=4)
            srcm = I["cache_mem"].rearrange("(b p j) c -> b p j c", b=NB, j=2)

            def load(b):
                act.dma_start(winK[:, b % 2, :, :], srcw[b, :, :, 0:128]).then_inc(wk_in[b % 2], 16)
                act.dma_start(memK[:, b % 2, :, :], srcm[b, :, :, 0:256]).then_inc(mk_in[b % 2], 16)
                act.dma_start(Vw[:, b, :, :], srcw[b, :, :, 128:256]).then_inc(v_in, 16)
                act.dma_start(Vm[:, b, :, :], srcm[b, :, :, 256:512]).then_inc(v_in, 16)

            load(0)
            load(1)
            act.wait_ge(gclamp, 1)
            nc.scalar.activation(gat[:, :], gat[:, :], ACT.Exp, scale=-1.0).then_inc(gexp, 1)

            def out(s):
                for u in range(0, units[s], 2):
                    act.wait_ge(turned, first[s] + u + 1)
                    src, k = ps[:, 4, :], kind(s, u)
                    dst = XT[:, (k - 4) // 2, 0, :] if k >= 4 else KsT[:, 0:512] if k == 0 else KwT[:, :]
                    w = 128 * ntile[s]
                    nc.scalar.copy(dst[:, 0:w], src[:, 0:w]).then_inc(out_a, 1)
                if s < NB:
                    act.wait_ge(kv_in[s % 2], 128 * (s // 2 + 1))
                    nc.scalar.copy(Vs[:, s, :, :, :].rearrange("p c t d -> p (c t) d"),
                                   raw[:, s % 2, :, :, 384:512].rearrange("p c t d -> p (c t) d")).then_inc(vs_ready, 1)
                if s + 2 < NB:
                    act.wait_ge(turned, first[s] + 4)
                    load(s + 2)

            out(0)
            for s in range(NSEQ):
                if s + 1 < NSEQ:
                    out(s + 1)
                n = blocks[s]
                act.wait_ge(hx_ready, s + 1)
                v = ht[:, :].rearrange("p (q n) -> p q n", q=4)[:, :, 0:n]
                nc.scalar.activation(v, v, ACT.Exp, scale=-2.0 * 0.7978845608028654).then_inc(he_ready, 1)
            act.wait_ge(steps_d, marks["cmax"])
            nc.scalar.activation(scb[:, 0:NC_S], scb[:, 0:NC_S], ACT.Exp, bias=sst[:, 0, 1:2], scale=SCALE,
                                 accum_out=sst[:, 0, 2:3]).then_inc(es, 1)
            act.wait_ge(steps_d, marks["mmax"])
            nc.scalar.activation(smb[:, :], smb[:, :], ACT.Exp, bias=sst[0:32, 1, 1:2], scale=SCALE,
                                 accum_out=sst[0:32, 1, 2:3]).then_inc(es, 1)
            act.wait_ge(steps_d, marks["wmax"])
            nc.scalar.activation(swb[:, 1:513], swb[:, 1:513], ACT.Exp, bias=sst[:, 2, 1:2], scale=SCALE,
                                 accum_out=sst[:, 2, 2:3]).then_inc(es, 1)
            act.wait_ge(steps_d, marks["smax"])
            nc.scalar.activation(ssb[:, 0:1025], ssb[:, 0:1025], ACT.Exp, bias=sst[:, 3, 1:2], scale=SCALE,
                                 accum_out=sst[:, 3, 2:3]).then_inc(es, 1)

        @block.tensor
        def _(pe):
            ident = lambda n, at=0: self.consts[at:at + n, C_ID + at:C_ID + at + n]
            pe.wait_ge(zeroed, 6)
            for a in range(4):
                nc.tensor.matmul(ps[0:64, a, :], zb[0:1, 0:64], zb[0:1, :], start=True, stop=False, skip_group_check=True)
            def turn(s):
                k, w, m = kvc[:, :, :, :, :], winK[:, s % 2, :, :], memK[:, s % 2, :, :]
                for u in range(units[s]):
                    n, a = first[s] + u, kind(s, u)
                    if a == 0:
                        pe.wait_ge(kv_in[s % 2], 128 * (s // 2 + 1))
                    if a == 2:
                        pe.wait_ge(wk_in[s % 2], 16 * (s // 2 + 1))
                    if a == 3:
                        pe.wait_ge(mk_in[s % 2], 16 * (s // 2 + 1))
                    if a == 4:
                        pe.wait_ge(kvc_ready, s + 1)
                    if n >= 2:
                        pe.wait_ge(out_d if n % 2 else out_a, n // 2)
                    dst = ps[:, 4 + n % 2, :]
                    for c in range(ntile[s]):
                        if a < 2:
                            src = raw[:, s % 2, 2 * a + c // 2, c % 2, 256:384]
                        elif a == 2:
                            src = w[:, c, :]
                        elif a == 3:
                            src = m[:, c % 2, 128 * (c // 2):128 * (c // 2) + 128]
                        else:
                            src = k[:, c, a - 4, :, :].rearrange("p t d -> p (t d)")
                        ins = nc.tensor.transpose(dst[:, 128 * c:128 * c + 128], src, ident(P))
                    ins.then_inc(turned, 1)

            def small():
                for r in range(R):
                    nc.tensor.transpose(cmp_[:, 8 * r:8 * r + 8], z[0:NB, smp, Q0 + 128 * r:Q0 + 128 * r + 128], ident(NB))
                for j in range(2):
                    nc.tensor.transpose(cmp_[:, 32 + 8 * j:40 + 8 * j], z[0:NB, smp, M0 + 128 * j:M0 + 128 * j + 128], ident(NB))
                for j in range(2):
                    ins = nc.tensor.transpose(cmp_[:, 48 + 8 * j:56 + 8 * j], z[0:NB, smp, K0 + 128 * (j + 1):K0 + 128 * (j + 2)], ident(NB))
                pe.wait_ge(self.w1_in, 16)
                pe.wait_ge(w_in_, 32)
                for q in range(2):
                    for l in range(16):
                        ins = nc.tensor.matmul(hid[:, q:q + 1], w1[:, q, l, :], pe_pos[:, q, l:l + 1], start=(l == 0), stop=(l == 15))
                ins.then_inc(small_in_psum, 1)

            def compress(s):
                n = blocks[s]
                pe.wait_ge(out_a, (first[s] + units[s]) // 2)
                pe.wait_ge(out_d, (first[s] + units[s]) // 2)
                if s == 0:
                    pe.wait_ge(q_ready, 1)
                else:
                    pe.wait_ge(hx_ready, s)
                for q in range(2):
                    for l in range(16):
                        ins = nc.tensor.matmul(hidv[:, 2 * q:2 * q + 2, 0:n], w1[:, q, l, :],
                                               XT[:, q, :, l:l + 8 * (n - 1) + 1:8], start=(l == 0), stop=(l == 15))
                ins.then_inc(hid_in_psum, 1)

            def score(s):
                if s == NB:
                    return
                if s == 0:
                    pe.wait_ge(q_ready, 1)
                pe.wait_ge(out_a, first[s] // 2 + 2)
                pe.wait_ge(out_d, first[s] // 2 + 2)
                add = dict(start=False, stop=False, skip_group_check=True)
                q = Q[:, 64 * s:64 * s + 64]
                for a in range(2):
                    nc.tensor.matmul(sel0[0:64, a, :], q, KsT[:, 512 * a:512 * a + 512], **add)
                nc.tensor.matmul(win0[0:64, :], q, KwT[:, :], **add)
                for a in range(2):
                    nc.tensor.matmul(misc[0:64, 64 + a:65 + a], q, kTn[:, a, s:s + 1], **add)
                for a in range(2):
                    nc.tensor.matmul(misc[0:32, 128:384], Qm[:, a, 32 * s:32 * s + 32], KmT[:, a, :], **add)

            def project_blocks(s):
                n = blocks[s]
                pe.wait_ge(gel_ready, s + 1)
                if s >= 1:
                    pe.wait_ge(cmp_ready, s)
                gk = gel[:, s % 2, :].rearrange("p (q n) -> p q n", q=4)
                for g in range(G):
                    nc.tensor.matmul(cmp_[:, 0:n], w2pad[:, g, :], gk[:, g, 0:n], start=(g == 0), stop=(g == 1))
                for g in range(G):
                    ins = nc.tensor.matmul(cmp_[0:n, 128 + 64 * g:192 + 64 * g], gk[:, 2 + g, 0:n], w2[:, 1, :], start=True, stop=True)
                ins.then_inc(cmp_in_psum, 1)

            for s in range(NSEQ):
                turn(s)
                if s == 0:
                    small()
                score(s)
                compress(s)
                if s >= 1:
                    project_blocks(s - 1)
            project_blocks(NSEQ - 1)
            pe.wait_ge(cmp_ready, NSEQ)
            for b in range(NB):
                ins = nc.tensor.matmul(misc[0:64, 0:NC_S], Q[:, 64 * b:64 * b + 64], kcT[:, b, 0:NC_S], start=False, stop=False, skip_group_check=True)
            ins.then_inc(cs_in_psum, 1)
            pe.wait_ge(steps_d, marks["pc"])
            nc.tensor.matmul(hid[0:64, 0:64], self.c(C_RG, 64, 64), scb[:, :], start=True, stop=True).then_inc(imp_in_psum, 1)
            pe.wait_ge(steps_d, marks["wp"])
            for j in range(2):
                nc.tensor.transpose(ps[:, 5, 448 + 32 * j:480 + 32 * j], smb[:, 128 * j:128 * j + 128], ident(32))
            for j in range(4):
                nc.tensor.transpose(ps[:, 5, 64 * j:64 * j + 64], swb[:, 128 * j:128 * j + 128], ident(64))
            nc.tensor.transpose(ps[0:NC_S, 5, 256:320], scb[:, 0:NC_S], ident(64))
            nc.tensor.matmul(ps[0:NB, 5, 384:448], self.c(C_S8, NB, 64), dgn[:, 1, :], start=True, stop=True).then_inc(pT_in_psum, 1)
            pe.wait_ge(steps_d, marks["sp"])
            for j in range(8):
                nc.tensor.transpose(ps[:, 4, 64 * j:64 * j + 64], ssb[:, 128 * j:128 * j + 128], ident(64))
            nc.tensor.matmul(hid[0:NB, 256:320], self.c(C_S8, NB, 64), dgn[:, 0, :], start=True, stop=True).then_inc(pT_in_psum, 1)
            nc.tensor.matmul(cmp_, zb[0:1, 0:128], zb[0:1, :], start=True, stop=False, skip_group_check=True)
            nc.tensor.matmul(ps[:, 0, :], zb[0:1, 0:128], zb[0:1, :], start=True, stop=False, skip_group_check=True)
            add = dict(start=False, stop=False, skip_group_check=True)
            at = lambda b, n: slice(32 * (b % 4), 32 * (b % 4) + n)
            heads = lambda b: slice(8 * b, 8 * b + 8)
            o = lambda b: cmp_[at(b, 8), 128 * (b // 4):128 * (b // 4) + 128]
            pe.wait_ge(v_in, 16 * 2 * NB)
            pe.wait_ge(vs_ready, NB)
            pe.wait_ge(pT_ready, 1)
            for b in range(NB):
                nc.tensor.matmul(o(b), nw[:, 1, heads(b)], z[0:NB, smp, V0 + 256:V0 + 384], **add)
            for j in range(4):
                for b in range(NB):
                    nc.tensor.matmul(o(b), pTw[:, j, heads(b)], Vw[:, b, j, :], **add)
            for b in range(NB):
                nc.tensor.matmul(o(b), pTc[0:NC_S, heads(b)], vc[0:NC_S, b, :], **add)
            for j in range(2):
                for b in range(NB):
                    nc.tensor.matmul(ps[at(b, 4), 0, 256 * (b // 4):256 * (b // 4) + 256], pTm[:, j, 4 * b:4 * b + 4], Vm[:, b, j, :], **add)
            pe.wait_ge(pT_ready, 2)
            for b in range(NB):
                nc.tensor.matmul(o(b), nw[:, 0, heads(b)], z[0:NB, smp, V0 + 128:V0 + 256], **add)
            for j in range(8):
                for b in range(NB):
                    ins = nc.tensor.matmul(o(b), pTs[:, j, heads(b)], Vs[:, b, j // 2, j % 2, :], **add)
                    if j == 7 and b >= NB - 4:
                        ins.then_inc(o_in_psum, 1)
            pe.wait_ge(oT_ready, 1)
            for n, (src, bank, wide) in enumerate(((oa, 4, 128), (om, 5, 256))):
                for c in range(H if n == 0 else MH):
                    for u in range(2):
                        v = src[:, wide * u + (64 * (c % 2) if n == 0 else 64 * c):][:, 0:64]
                        ins = nc.tensor.matmul(ps[0:NB, bank, 64 * c:64 * c + 64], self.c(C_SEL + NB * (8 * u + c), NB), v, start=(u == 0), stop=(u == 1))
            ins.then_inc(os_in_psum, 1)

        self.close(st)

    def attend(self):
        nc, I, O = self.nc, self.ins, self.outs
        st = ExitStack()
        S = lambda n: self.sem(n, st)
        ps, z, o = self.ps, self.z, self.o
        qT = self.sb("qT", [P, R, T], stack=st)
        kT = self.sb("kT", [P, 2, T], stack=st)
        qmT = self.sb("qmT", [P, 2, T], stack=st)
        mz = self.sb("mz", [P, 2, 512], stack=st)
        mkT = self.sb("mkT", [P, 2, MEM], stack=st)
        gate = self.sb("gate", [P, TILES, 24], stack=st)
        prob = self.sb("prob", [P, 2, 2, 512], stack=st)
        pT = self.sb("pT", [P, 2, 512], stack=st)
        stt = self.sb("stt", [P, 2, 4, 8], stack=st)
        zb = self.sb("zb2", [1, 512], BF16, stack=st)
        mz_in, gclamp, gexp, steps, zeroed, turned, out_a, out_d = (S(n) for n in (
            "mz_in", "gate_clamped", "gate_exp", "attend_dve", "zb_zeroed", "qk_turned", "qk_out_a", "qk_out_d"))
        scores, peaks, exps, probs, p_turned, pT_a, pT_d, pv, o_in_psum, o_out = (S(n) for n in (
            "scores", "peaks", "exps", "probs", "p_turned", "pT_a", "pT_d", "pv", "o_in_psum", "o_out"))

        pre = []
        for r in range(R):
            pre.append(([z[:, t, Q0 + 128 * r:Q0 + 128 * r + 128] for t in range(TILES)], qT[:, r, :]))
        for a in range(2):
            pre.append(([z[:, t, K0 + 128 * (a + 1):K0 + 128 * (a + 2)] for t in range(TILES)], kT[:, a, :]))
        for a in range(2):
            pre.append(([z[:, t, M0 + 128 * a:M0 + 128 * a + 128] for t in range(TILES)], qmT[:, a, :]))
        pre.append(([mz[:, j, 128 * a:128 * a + 128] for a in range(2) for j in range(2)], mkT[:, :, :].rearrange("p a n -> p (a n)")))
        units = [(t, kind, r) for t in range(TILES)
                 for kind, r in [("cmp", 0), ("mem", 0)] + [(br, r) for br in ("sel", "win") for r in range(R)]]
        NU = len(units)
        per = NU // TILES

        block = st.enter_context(nc.Block("attend"))

        @block.sync
        def _(sp):
            for j in range(2):
                sp.dma_start(mz[:, j, :], O["mem_p"][j * P:(j + 1) * P, :]).then_inc(mz_in, 16)

        @block.gpsimd
        def _(pool):
            nc.gpsimd.memset(zb[:, :], 0.0).then_inc(zeroed, 1)

        @block.tensor
        def _(pe):
            ident = self.consts[:, C_ID:C_ID + P]
            pe.wait_ge(zeroed, 1)
            for n, (srcs, _) in enumerate(pre):
                if n == len(pre) - 1:
                    pe.wait_ge(mz_in, 32)
                if n >= 2:
                    pe.wait_ge(out_d if n % 2 else out_a, n // 2)
                for c, src in enumerate(srcs):
                    ins = nc.tensor.transpose(ps[:, 4 + n % 2, 128 * c:128 * c + 128], src, ident)
                ins.then_inc(turned, 1)

            def score(u):
                t, kind, r = units[u]
                q = slice(t * P, (t + 1) * P)
                if u >= 2:
                    pe.wait_ge(exps, u - 1)
                b = 2 * (u % 2)
                last = {}
                if kind == "cmp":
                    for r in range(R):
                        for g in range(G):
                            hs = slice(64 * g, 64 * g + 64)
                            ins = nc.tensor.matmul(ps[:, b + g, 32 * r:32 * r + NC_P], qT[hs, r, q], self.kcT[hs, NB, 0:NC_P], start=True, stop=True)
                            last[g] = ins
                elif kind == "mem":
                    for h in range(MH):
                        hs = slice(64 * (h % 2), 64 * (h % 2) + 64)
                        hp = h // 2
                        ins = nc.tensor.matmul(ps[:, b + h % 2, MEM * hp:MEM * hp + MEM], qmT[hs, hp, q], mkT[hs, hp, :], start=True, stop=True)
                        last[h % 2] = ins
                else:
                    for g in range(G):
                        hs = slice(64 * g, 64 * g + 64)
                        ins = nc.tensor.matmul(ps[:, b + g, 0:(t + 1) * P], qT[hs, r, q], kT[hs, int(kind == "win"), 0:(t + 1) * P], start=True, stop=True)
                        if g == 0:
                            ins.then_inc(scores, 1)
                if kind in ("cmp", "mem"):
                    last[0].then_inc(scores, 1)
                ins.then_inc(scores, 1)

            def turn(u):
                t, kind, r = units[u]
                pe.wait_ge(probs, u + 1)
                if u >= 1:
                    pe.wait_ge(pT_a, u)
                    pe.wait_ge(pT_d, u)
                p = prob[:, u % 2, :, :]
                for j in range(2):
                    for c in range(t + 1 if kind in ("sel", "win") else 4):
                        if kind == "cmp":
                            ins = nc.tensor.transpose(ps[0:NC_P, 4 + j, 128 * c:128 * c + 128], p[:, j, 32 * c:32 * c + NC_P], ident)
                        else:
                            ins = nc.tensor.transpose(ps[:, 4 + j, 128 * c:128 * c + 128], p[:, j, 128 * c:128 * c + 128], ident)
                ins.then_inc(p_turned, 1)

            def value(u):
                t, kind, r = units[u]
                add = dict(start=False, stop=False, skip_group_check=True)
                if u % per == 0:
                    if t >= 1:
                        pe.wait_ge(o_out, t)
                    for a in range(2):
                        nc.tensor.matmul(ps[:, 6 + a, :], zb[0:1, 0:P], zb[0:1, :], start=True, stop=False, skip_group_check=True)
                pe.wait_ge(pT_a, u + 1)
                pe.wait_ge(pT_d, u + 1)
                for j in range(2):
                    if kind == "cmp":
                        for r in range(R):
                            c = 2 * r + j
                            ins = nc.tensor.matmul(ps[:, 6, 64 * c:64 * c + 64], pT[0:NC_P, j, 128 * r:128 * r + 128], self.vc[0:NC_P, NB, 64 * j:64 * j + 64], **add)
                    elif kind == "mem":
                        for hp in range(2):
                            h = 2 * hp + j
                            for k in range(2):
                                ins = nc.tensor.matmul(ps[:, 7, 64 * h:64 * h + 64], pT[:, j, 128 * (2 * hp + k):128 * (2 * hp + k) + 128],
                                                       mz[:, k, 256 + 64 * h:320 + 64 * h], **add)
                    else:
                        c = 2 * r + j
                        v = V0 + 128 * (1 if kind == "sel" else 2) + 64 * j
                        for k in range(t + 1):
                            ins = nc.tensor.matmul(ps[:, 6, 64 * c:64 * c + 64], pT[:, j, 128 * k:128 * k + 128], z[:, k, v:v + 64], **add)
                if u % per == per - 1:
                    ins.then_inc(o_in_psum, 1)

            pe.wait_ge(out_a, (len(pre) + 1) // 2)
            pe.wait_ge(out_d, len(pre) // 2)
            score(0)
            score(1)
            for u in range(NU):
                if u + 2 < NU:
                    score(u + 2)
                if u >= 1:
                    value(u - 1)
                turn(u)
            value(NU - 1)

        def shape(u):
            t, kind = units[u][0:2]
            return {"cmp": (4, NC_P, 32), "mem": (2, MEM, MEM)}.get(kind, (1, (t + 1) * P, 512))

        def view(a, u):
            n, w, s = shape(u)
            return a[:, :, 0:n * s].rearrange("p j (n s) -> p j n s", n=n)[:, :, :, 0:w]

        @block.vector
        def _(dve):
            ch = Chain(dve, steps)
            nc.vector.tensor_scalar(gate[:, :, :], z[:, 0:TILES, G0:G0 + 24], -80.0, None, ALU.max).then_inc(gclamp, 1)
            dve.wait_ge(gexp, 1)
            ch.then(nc.vector.tensor_scalar(gate[:, :, :], gate[:, :, :], 1.0, None, ALU.add))
            ch.then(nc.vector.reciprocal(gate[:, :, :], gate[:, :, :]))
            for n in range(1, len(pre), 2):
                dve.wait_ge(turned, n + 1)
                nc.vector.tensor_copy(pre[n][1], ps[:, 5, :]).then_inc(out_d, 1)

            def peak(u):
                t, kind = units[u][0:2]
                n, w, s = shape(u)
                b = 2 * (u % 2)
                dve.wait_ge(scores, 2 * u + 2)
                sc = view(ps[:, b:b + 2, :], u)
                st_ = stt[:, u % 2, 0:2, :]
                if kind == "cmp":
                    mask = self.c(C_CADD + 32 * t, NC_P).unsqueeze(1).broadcast_to([P, R, NC_P])
                    for j in range(2):
                        ins = nc.vector.tensor_tensor(sc[:, j, :, :], sc[:, j, :, :], mask, ALU.add)
                    ch.then(ins)
                elif kind != "mem":
                    d = sc[:, :, 0, t * P:(t + 1) * P]
                    ch.then(nc.vector.tensor_tensor(d, d, self.c(C_CAUS, P).unsqueeze(1).broadcast_to([P, 2, P]), ALU.add))
                top = stt[:, u % 2, 0, 0:2 * n]
                ch.then(nc.vector.tensor_reduce(top.rearrange("p (j n) -> p j n", j=2), sc, AX.X, ALU.max))
                if kind == "cmp":
                    pr = view(prob[:, u % 2, :, :], u)
                    if u >= 2:
                        dve.wait_ge(p_turned, u - 1)
                    for j in range(2):
                        ins = nc.vector.tensor_tensor(pr[:, j, :, :], sc[:, j, :, :], top[:, 4 * j:4 * j + 4].unsqueeze(2).broadcast_to([P, 4, NC_P]), ALU.subtract)
                    ins.then_inc(peaks, 1)
                else:
                    nc.vector.tensor_scalar(stt[:, u % 2, 1, 0:2 * n], top, -SCALE, None, ALU.mult).then_inc(peaks, 1)

            def weigh(u):
                t, kind, r = units[u]
                n, w, s = shape(u)
                dve.wait_ge(exps, u + 1)
                pr = view(prob[:, u % 2, :, :], u)
                total, f = stt[:, u % 2, 2, 0:2 * n], stt[:, u % 2, 3, 0:2 * n]
                if kind == "cmp":
                    mask = self.c(C_CMUL + 32 * t, NC_P).unsqueeze(1).broadcast_to([P, R, NC_P])
                    for j in range(2):
                        ins = nc.vector.tensor_tensor(pr[:, j, :, :], pr[:, j, :, :], mask, ALU.mult)
                    ch.then(ins)
                    ch.then(nc.vector.tensor_reduce(total.rearrange("p (j n) -> p j n", j=2), pr, AX.X, ALU.add))
                    ch.then(nc.vector.tensor_scalar(total, total, 1e-30, None, ALU.max))
                ch.then(nc.vector.reciprocal(f, total))
                if kind == "cmp":
                    ch.then(nc.vector.tensor_tensor(f.rearrange("p (j r) -> p j r", j=2), f.rearrange("p (j r) -> p j r", j=2),
                                                    gate[:, t, 0:8].rearrange("p (r j) -> p j r", j=2), ALU.mult))
                    for j in range(2):
                        ins = nc.vector.tensor_tensor(pr[:, j, :, :], pr[:, j, :, :], f[:, 4 * j:4 * j + 4].unsqueeze(2).broadcast_to([P, 4, NC_P]), ALU.mult)
                elif kind == "mem":
                    for i in range(4):
                        ins = nc.vector.tensor_scalar(pr[:, i // 2, i % 2, :], pr[:, i // 2, i % 2, :], f[:, i:i + 1], None, ALU.mult)
                else:
                    for j in range(2):
                        c = 8 * (1 if kind == "sel" else 2) + 2 * r + j
                        ins = nc.vector.tensor_scalar(pr[:, j, 0, :], pr[:, j, 0, :], f[:, j:j + 1], gate[:, t, c:c + 1], ALU.mult, ALU.mult)
                ins.then_inc(probs, 1)

            peak(0)
            peak(1)
            for u in range(NU):
                t, kind = units[u][0:2]
                weigh(u)
                if u + 2 < NU:
                    peak(u + 2)
                dve.wait_ge(p_turned, u + 1)
                rows = NC_P if kind == "cmp" else P
                w = 512 if kind in ("cmp", "mem") else (t + 1) * P
                nc.vector.tensor_copy(pT[0:rows, 1, 0:w], ps[0:rows, 5, 0:w]).then_inc(pT_d, 1)

        @block.scalar
        def _(act):
            act.wait_ge(gclamp, 1)
            nc.scalar.activation(gate[:, :, :], gate[:, :, :], ACT.Exp, scale=-1.0).then_inc(gexp, 1)
            for n in range(0, len(pre), 2):
                act.wait_ge(turned, n + 1)
                nc.scalar.copy(pre[n][1], ps[:, 4, :]).then_inc(out_a, 1)

            def exp(u):
                t, kind = units[u][0:2]
                b = 2 * (u % 2)
                act.wait_ge(peaks, u + 1)
                if u >= 2:
                    act.wait_ge(p_turned, u - 1)
                pr, sc = view(prob[:, u % 2, :, :], u), view(ps[:, b:b + 2, :], u)
                if kind == "cmp":
                    for j in range(2):
                        ins = nc.scalar.activation(pr[:, j, :, :], pr[:, j, :, :], ACT.Exp, scale=SCALE)
                else:
                    n = shape(u)[0]
                    for i in range(2 * n):
                        ins = nc.scalar.activation(pr[:, i // n, i % n, :], sc[:, i // n, i % n, :], ACT.Exp, bias=stt[:, u % 2, 1, i:i + 1],
                                                   scale=SCALE, accum_out=stt[:, u % 2, 2, i:i + 1])
                ins.then_inc(exps, 1)

            exp(0)
            exp(1)
            for u in range(NU):
                t, kind = units[u][0:2]
                act.wait_ge(p_turned, u + 1)
                rows = NC_P if kind == "cmp" else P
                w = 512 if kind in ("cmp", "mem") else (t + 1) * P
                nc.scalar.copy(pT[0:rows, 0, 0:w], ps[0:rows, 4, 0:w]).then_inc(pT_a, 1)
                if u + 2 < NU:
                    exp(u + 2)
                if u >= 1 and u % per == 0:
                    act.wait_ge(o_in_psum, t)
                    nc.scalar.copy(o[:, t - 1, 0:512], ps[:, 6, :])
                    nc.scalar.copy(o[:, t - 1, 512:768], ps[:, 7, 0:256]).then_inc(o_out, 1)
            act.wait_ge(o_in_psum, TILES)
            nc.scalar.copy(o[:, TILES - 1, 0:512], ps[:, 6, :])
            nc.scalar.copy(o[:, TILES - 1, 512:768], ps[:, 7, 0:256]).then_inc(o_out, 1)

        self.close(st)

    def mix(self):
        nc, I, O = self.nc, self.ins, self.outs
        st = ExitStack()
        S = lambda n: self.sem(n, st)
        ps, z, o = self.ps, self.z, self.o
        NT = TILES + 1
        bands = self.sb("bands", [P, BW], stack=st)
        state = self.sb("state", [P, 256], stack=st)
        w_pool = self.sb("w_pool", [64, 4, 64], stack=st)
        w_out = self.sb("w_out", [P, KD, D], stack=st)
        rows_g = self.sb("rows_g", [P, 2 * D + 256 + 36], stack=st)
        w_router = self.sb("w_router", [P, KD, 36], stack=st)
        xin = self.sb("xin4", [P, 2, D], stack=st)
        rT = self.sb("rT", [64, 4, P], stack=st)
        mixed = self.sb("mixed", [P, D], stack=st)
        mT = self.sb("mT", [P, KD, P], stack=st)
        h = self.sb("h", [P, 2, D], stack=st)
        hn = self.sb("hn", [P, 2, D], stack=st)
        hT = self.sb("hT", [P, KD, P], stack=st)
        junk = self.sb("junk4", [P, 512], stack=st)
        sq = self.sb("sq", [P, 2, 8], stack=st)
        lg = self.sb("lg", [P, 36], stack=st)
        ro = self.sb("ro", [P, 160], stack=st)
        one = self.sb("one", [P, NT, 2, NEXP], stack=st)
        both = self.sb("both", [P, NT, NEXP], stack=st)
        cnt = self.sb("cnt", [P, NT + 1, NEXP], stack=st)
        scan = self.sb("scan", [P, 3, NEXP], stack=st)
        prod = self.sb("prod", [P, NT, 2, NEXP], stack=st)
        place = self.sb("place", [P, 8, NT * 2], stack=st)
        dest = self.sb("dest", [P, NT * 2], I32, stack=st)
        tok = self.sb("tok", [P, NT], I32, stack=st)
        zero_i = self.sb("zero_i", [CAP, NTILE], I32, stack=st)
        last = self.sb("last", [1, NOVER, NEXP], stack=st)
        consts_in, wout_in = S("mix_consts_in"), S("wout_in")
        stored = [S(f"h_stored{j}") for j in range(2)]
        x_in = [S(f"x4_in{j}") for j in range(2)]
        names = ("mix_dve", "cleared", "r_in_psum", "r_ready", "y_in_psum", "ss_ready", "ms_ready4", "root_ready", "mixed_ready",
                 "mT_in_psum", "mT_ready", "h_in_psum", "hms", "hroot", "hn_ready", "hT_in_psum", "hT_ready", "l_in_psum",
                 "lclear", "lexp", "pair_ready", "cnt_in_psum", "table_zero", "dest_ready", "scattered", "table_in")
        (steps, cleared, r_in_psum, r_ready, y_in_psum, ss_ready, ms_ready, root_ready, mixed_ready,
         mT_in_psum, mT_ready, h_in_psum, hms, hroot, hn_ready, hT_in_psum, hT_ready, l_in_psum,
         lclear, lexp, pair_ready, cnt_in_psum, table_zero, dest_ready, scattered, table_in) = (S(n) for n in names)
        gm, gf, sp_, br = rows_g[:, 0:D], rows_g[:, D:2 * D], rows_g[:, 2 * D:2 * D + 256], rows_g[:, 2 * D + 256:]

        block = st.enter_context(nc.Block("mix"))

        @block.sync
        def _(sp):
            sp.dma_start(bands[:, :], I["bands"]).then_inc(consts_in, 16)
            sp.dma_start(state[0:NB * STATE, :], I["state_pool"]).then_inc(consts_in, 16)
            sp.dma_start(w_pool[:, :, :], I["w_pool"].rearrange("(w c) d -> c w d", w=4)).then_inc(consts_in, 16)
            sp.dma_start(rows_g[:, :], I["mix_rows"].partition_broadcast(P)).then_inc(consts_in, 16)
            for t in range(2):
                sp.dma_start(xin[0:ROWS[t], t, :], I["x"][t * P:t * P + ROWS[t], :]).then_inc(x_in[t], 16)
            for j in range(2):
                sp.dma_start(w_out[:, 4 * j:4 * j + 4, :], I["w_out"].rearrange("(p k) n -> p k n", k=KD)[:, 4 * j:4 * j + 4, :]).then_inc(wout_in, 16)
            sp.dma_start(w_router[:, :, :], I["w_router"].rearrange("(p k) n -> p k n", k=KD)).then_inc(wout_in, 16)
            for t in range(NT):
                r = ROWS[t]
                sp.wait_ge(hn_ready, t + 1)
                sp.dma_start(self.hn_dram[t * P:t * P + r, :], hn[0:r, t % 2, :]).then_inc(stored[t % 2], 16)
                sp.dma_start(self.h_dram[t * P:t * P + r, :], h[0:r, t % 2, :]).then_inc(stored[t % 2], 16)
                if t + 2 < NT:
                    sp.dma_start(xin[0:ROWS[t + 2], t % 2, :], I["x"][(t + 2) * P:(t + 2) * P + ROWS[t + 2], :]).then_inc(x_in[t % 2], 16)
            sp.wait_ge(stored[0], 32 * ((NT + 1) // 2))
            sp.wait_ge(stored[1], 32 * (NT // 2))

        @block.gpsimd
        def _(pool):
            nc.gpsimd.memset(one[:, :, :, :], 0.0).then_inc(cleared, 1)
            nc.gpsimd.memset(cnt[:, :, :], 0.0).then_inc(cleared, 1)
            nc.gpsimd.memset(self.pair_w[:, :, :], 0.0).then_inc(cleared, 1)
            nc.gpsimd.memset(zero_i[:, :], 0).then_inc(cleared, 1)
            pool.wait_ge(cleared, 4)
            pool.dma_start(self.table_dram.rearrange("(s t) o -> s (t o)", t=NTILE), zero_i[:, :]).then_inc(table_zero, 16)
            pool.wait_ge(table_zero, 16)
            pool.wait_ge(dest_ready, 1)
            for t in range(NT):
                for k in range(2):
                    pool.indirect_dma_start(out=self.table_dram, out_offset=bass.IndirectOffsetOnAxis(ap=dest[0:ROWS[t], 2 * t + k:2 * t + k + 1].bitcast(U32), axis=0),
                                            in_=tok[0:ROWS[t], t:t + 1], in_offset=None).then_inc(scattered, 16)
            pool.wait_ge(scattered, 16 * 2 * NT)
            pool.dma_start(self.table[:, :], self.table_dram.rearrange("(s t) o -> s (t o)", t=NTILE)).then_inc(table_in, 16)
            pool.wait_ge(table_in, 16)

        @block.tensor
        def _(pe):
            ident = lambda n: self.consts[0:n, C_ID:C_ID + n]
            pe.wait_ge(consts_in, 64)

            def pool_mix(t):
                r = ROWS[t]
                if t >= 1:
                    pe.wait_ge(r_ready, t)
                band = lambda w, j: bands[:, C_BAND + (3 * w + j) * P:C_BAND + (3 * w + j + 1) * P]
                for w in range(4):
                    u = z[0:r, t, U0 + 64 * w:U0 + 64 * w + 64]
                    out = ps[0:64, 0, 128 * w:128 * w + r]
                    if t == 0:
                        ins = nc.tensor.matmul(out, u, band(w, 2), start=True, stop=True)
                    elif t < TILES:
                        nc.tensor.matmul(out, u, band(w, 0), start=True, stop=False)
                        ins = nc.tensor.matmul(out, z[:, t - 1, U0 + 64 * w:U0 + 64 * w + 64], band(w, 1), start=False, stop=True)
                    else:
                        n = NB * STATE
                        nc.tensor.matmul(out, state[0:n, 64 * w:64 * w + 64], bands[0:n, C_PST + NB * w:C_PST + NB * w + NB], start=True, stop=False)
                        ins = nc.tensor.matmul(out, z[0:NB, t, U0 + 64 * w:U0 + 64 * w + 64], bands[0:NB, C_PDG + NB * w:C_PDG + NB * w + NB], start=False, stop=True)
                ins.then_inc(r_in_psum, 1)
                pe.wait_ge(r_ready, t + 1)
                if t >= 1:
                    pe.wait_ge(ss_ready, t)
                for w in range(4):
                    ins = nc.tensor.matmul(ps[0:r, 1, 64 * w:64 * w + 64], rT[:, w, 0:r], w_pool[:, w, :], start=True, stop=True)
                ins.then_inc(y_in_psum, 1)

            def out_proj(t):
                r = ROWS[t]
                pe.wait_ge(mixed_ready, t + 1)
                if t >= 1:
                    pe.wait_ge(hT_ready, t)
                for k in range(KD):
                    ins = nc.tensor.transpose(ps[:, 2 + k // 4, 128 * (k % 4):128 * (k % 4) + r], mixed[0:r, k:D:KD], ident(r))
                ins.then_inc(mT_in_psum, 1)
                pe.wait_ge(mT_ready, t + 1)
                if t == 0:
                    pe.wait_ge(wout_in, 48)
                for a in range(2):
                    for k in range(KD):
                        ins = nc.tensor.matmul(ps[0:r, 4 + a, :], mT[:, k, 0:r], w_out[:, k, 512 * a:512 * a + 512], start=(k == 0), stop=(k == KD - 1))
                ins.then_inc(h_in_psum, 1)

            def route(t):
                r = ROWS[t]
                pe.wait_ge(hn_ready, t + 1)
                for k in range(KD):
                    ins = nc.tensor.transpose(ps[:, 2 + k // 4, 128 * (k % 4):128 * (k % 4) + r], hn[0:r, t % 2, k:D:KD], ident(r))
                ins.then_inc(hT_in_psum, 1)
                pe.wait_ge(hT_ready, t + 1)
                if t >= 1:
                    pe.wait_ge(lclear, t)
                for k in range(KD):
                    ins = nc.tensor.matmul(ps[0:r, 6, 0:36], hT[:, k, 0:r], w_router[:, k, :], start=(k == 0), stop=(k == KD - 1))
                ins.then_inc(l_in_psum, 1)

            pool_mix(0)
            for t in range(NT):
                if t + 1 < NT:
                    pool_mix(t + 1)
                out_proj(t)
                route(t)
            pe.wait_ge(pair_ready, NT)
            for t in range(NT + 1):
                r = ROWS[t] if t < NT else P
                out = ps[0:r, 7, NEXP * t:NEXP * t + NEXP]
                for s in range(min(t, NT)):
                    ins = nc.tensor.matmul(out, self.c(C_ONE, r, ROWS[s]), both[0:ROWS[s], s, :], start=(s == 0), stop=(t == NT and s == NT - 1))
                if t < NT:
                    ins = nc.tensor.matmul(out, self.c(C_UP, r, r), both[0:r, t, :], start=(t == 0), stop=True)
            ins.then_inc(cnt_in_psum, 1)

        @block.scalar
        def _(act):
            def mixed_T(t):
                r = ROWS[t]
                act.wait_ge(mT_in_psum, t + 1)
                nc.scalar.copy(mT[:, :, 0:r], ps[:, 2:4, :].rearrange("p a (k t) -> p (a k) t", t=P)[:, :, 0:r]).then_inc(mT_ready, 1)

            def root(t):
                act.wait_ge(ms_ready, t + 1)
                nc.scalar.activation(sq[0:ROWS[t], 0, 3:6], sq[0:ROWS[t], 0, 0:3], ACT.Sqrt).then_inc(root_ready, 1)

            root(0)
            for t in range(NT):
                r = ROWS[t]
                mixed_T(t)
                act.wait_ge(hms, t + 1)
                nc.scalar.activation(sq[0:r, 1, 1:2], sq[0:r, 1, 0:1], ACT.Sqrt).then_inc(hroot, 1)
                act.wait_ge(hT_in_psum, t + 1)
                nc.scalar.copy(hT[:, :, 0:r], ps[:, 2:4, :].rearrange("p a (k t) -> p (a k) t", t=P)[:, :, 0:r]).then_inc(hT_ready, 1)
                if t + 1 < NT:
                    root(t + 1)
                act.wait_ge(lclear, t + 1)
                nc.scalar.activation(ro[0:r, 0:5], ro[0:r, 0:5], ACT.Exp).then_inc(lexp, 1)

        @block.vector
        def _(dve):
            ch = Chain(dve, steps)
            dve.wait_ge(consts_in, 64)
            dve.wait_ge(cleared, 4)

            def first_top(dst, src, order, r, n, tmp):
                ch.then(nc.vector.tensor_reduce(tmp[:, 0:1], src, AX.X, ALU.max))
                ch.then(nc.vector.scalar_tensor_tensor(dst, src, tmp[:, 0:1], self.c(order, n, r), ALU.is_equal, ALU.mult))
                ch.then(nc.vector.tensor_reduce(tmp[:, 1:2], dst, AX.X, ALU.max))
                ch.then(nc.vector.tensor_scalar(dst, self.c(order, n, r), tmp[:, 1:2], None, ALU.is_equal))

            def pooled(t):
                r = ROWS[t]
                dve.wait_ge(r_in_psum, t + 1)
                nc.vector.tensor_copy(rT[:, :, 0:r], ps[0:64, 0, :].rearrange("p (w t) -> p w t", w=4)[:, :, 0:r]).then_inc(r_ready, 1)

            def norm_mix(t):
                r = ROWS[t]
                ot = o[:, t, :] if t < TILES else self.o_s[:, :]
                if t >= 1:
                    dve.wait_ge(mT_in_psum, t)
                dve.wait_ge(y_in_psum, t + 1)
                ins = nc.vector.tensor_tensor(mixed[0:r, 0:256], ps[0:r, 1, 0:256], sp_[0:r, :], ALU.mult)
                ins.then_inc(ss_ready, 1)
                dve.wait_ge(ss_ready, t + 1)
                s = sq[0:r, 0, :]
                parts = ((mixed[0:r, 0:256], 0, 256), (ot[0:r, 0:512], 256, 512), (ot[0:r, 512:768], 768, 256))
                for j, (a, at, n) in enumerate(parts):
                    ch.then(nc.vector.tensor_tensor_reduce(junk[0:r, 0:n], a, a, 1.0, 0.0, ALU.mult, ALU.add, s[:, j:j + 1]))
                for j, (a, at, n) in enumerate(parts):
                    ins = nc.vector.tensor_scalar(s[:, j:j + 1], s[:, j:j + 1], 1.0 / n, EPS, ALU.mult, ALU.add)
                ins.then_inc(ms_ready, 1)
                dve.wait_ge(root_ready, t + 1)
                ch.then(nc.vector.reciprocal(s[:, 3:6], s[:, 3:6]))
                for j, (a, at, n) in enumerate(parts):
                    ins = nc.vector.scalar_tensor_tensor(mixed[0:r, at:at + n], a, s[:, 3 + j:4 + j], gm[0:r, at:at + n], ALU.mult, ALU.mult)
                ins.then_inc(mixed_ready, 1)

            def norm_h(t):
                r = ROWS[t]
                dve.wait_ge(h_in_psum, t + 1)
                dve.wait_ge(x_in[t % 2], 16 * (t // 2 + 1))
                if t >= 2:
                    dve.wait_ge(stored[t % 2], 32 * (t // 2))
                ch.then(nc.vector.tensor_tensor(h[0:r, t % 2, :].rearrange("p (a n) -> p a n", a=2), ps[0:r, 4:6, :],
                                                xin[0:r, t % 2, :].rearrange("p (a n) -> p a n", a=2), ALU.add))
                ch.then(nc.vector.tensor_tensor_reduce(hn[0:r, t % 2, :], h[0:r, t % 2, :], h[0:r, t % 2, :], 1.0, 0.0, ALU.mult, ALU.add, sq[0:r, 1, 2:3]))
                nc.vector.tensor_scalar(sq[0:r, 1, 0:1], sq[0:r, 1, 2:3], 1.0 / D, EPS, ALU.mult, ALU.add).then_inc(hms, 1)
                dve.wait_ge(hroot, t + 1)
                ch.then(nc.vector.reciprocal(sq[0:r, 1, 3:4], sq[0:r, 1, 1:2]))
                nc.vector.scalar_tensor_tensor(hn[0:r, t % 2, :], h[0:r, t % 2, :], sq[0:r, 1, 3:4], gf[0:r, :], ALU.mult, ALU.mult).then_inc(hn_ready, 1)

            def choose(t):
                r = ROWS[t]
                dve.wait_ge(l_in_psum, t + 1)
                L = lg[0:r, :]
                ch.then(nc.vector.tensor_tensor(L, ps[0:r, 6, 0:36], br[0:r, :], ALU.add))
                f = lambda a, n: ro[0:r, a:a + n]
                first_top(f(8, 4), L[:, 0:4], C_G4, r, 4, f(72, 2))
                ch.then(nc.vector.tensor_scalar(f(0, 4), L[:, 0:4], f(72, 1), None, ALU.subtract))
                ch.then(nc.vector.tensor_tensor(f(16, 32).rearrange("p (g e) -> p g e", g=4), L[:, 4:36].rearrange("p (g e) -> p g e", g=4),
                                                f(8, 4).unsqueeze(2).broadcast_to([r, 4, 8]), ALU.mult))
                ch.then(nc.vector.tensor_reduce(f(48, 8), f(16, 32).rearrange("p (g e) -> p e g", g=4), AX.X, ALU.add))
                first_top(f(56, 8), f(48, 8), C_E8, r, 8, f(74, 2))
                ch.then(nc.vector.scalar_tensor_tensor(f(80, 8), f(56, 8), NEG, f(48, 8), ALU.mult, ALU.add))
                first_top(f(64, 8), f(80, 8), C_E8, r, 8, f(76, 2))
                nc.vector.tensor_tensor(f(4, 1), f(76, 1), f(74, 1), ALU.subtract).then_inc(lclear, 1)
                dve.wait_ge(lexp, t + 1)
                ch.then(nc.vector.tensor_reduce(f(90, 1), f(0, 4), AX.X, ALU.add))
                ch.then(nc.vector.tensor_scalar(f(91, 1), f(4, 1), 1.0, None, ALU.add))
                ch.then(nc.vector.tensor_tensor(f(92, 1), f(90, 1), f(91, 1), ALU.mult))
                ch.then(nc.vector.reciprocal(self.pair_w[0:r, t, 0:1], f(92, 1)))
                ch.then(nc.vector.tensor_tensor(self.pair_w[0:r, t, 1:2], self.pair_w[0:r, t, 0:1], f(4, 1), ALU.mult))
                for k in range(2):
                    ch.then(nc.vector.tensor_tensor(one[0:r, t, k, :].rearrange("p (g e) -> p g e", g=4), f(8, 4).unsqueeze(2).broadcast_to([r, 4, 8]),
                                                    f(56 + 8 * k, 8).unsqueeze(1).broadcast_to([r, 4, 8]), ALU.mult))
                nc.vector.tensor_tensor(both[0:r, t, :], one[0:r, t, 0, :], one[0:r, t, 1, :], ALU.add).then_inc(pair_ready, 1)

            pooled(0)
            norm_mix(0)
            for t in range(NT):
                if t + 1 < NT:
                    pooled(t + 1)
                norm_h(t)
                if t + 1 < NT:
                    norm_mix(t + 1)
                choose(t)

            dve.wait_ge(cnt_in_psum, 1)
            nc.vector.tensor_copy(cnt[:, 0:TILES, :], ps[:, 7, 0:TILES * NEXP].rearrange("p (t e) -> p t e", t=TILES))
            nc.vector.tensor_copy(cnt[0:NB, TILES, :], ps[0:NB, 7, TILES * NEXP:NT * NEXP])
            ch.then(nc.vector.tensor_copy(cnt[:, NT, :], ps[:, 7, NT * NEXP:(NT + 1) * NEXP]))
            over, a, b = scan[:, 0, :], scan[:, 1, :], scan[:, 2, :]
            ch.then(nc.vector.tensor_scalar(over, cnt[:, NT, :], float(CAP), None, ALU.is_gt))
            for i in range(2, QMAX + 1):
                ch.then(nc.vector.scalar_tensor_tensor(over, cnt[:, NT, :], float(CAP * i), over, ALU.is_gt, ALU.add))
            ch.then(nc.vector.tensor_copy(a, over))
            d = 1
            while d < NEXP:
                nc.vector.tensor_copy(b[:, 0:d], a[:, 0:d])
                ch.then(nc.vector.tensor_tensor(b[:, d:NEXP], a[:, d:NEXP], a[:, 0:NEXP - d], ALU.add))
                a, b = b, a
                d *= 2
            ch.then(nc.vector.tensor_copy(self.n_over[:, :], a[0:1, NEXP - 1:NEXP]))
            ch.then(nc.vector.tensor_tensor(last[:, :, :], a[0:1, :].unsqueeze(1).broadcast_to([1, NOVER, NEXP]),
                                            self.c(C_MAIN, NOVER, 1).unsqueeze(2).broadcast_to([1, NOVER, NEXP]), ALU.is_le))
            ch.then(nc.vector.tensor_reduce(prod[0:1, 0, 0, 0:NOVER], last[:, :, :], AX.X, ALU.add))
            ch.then(nc.vector.tensor_scalar(self.over_e[:, :], prod[0:1, 0, 0, 0:NOVER], float(NEXP - 1), None, ALU.min))
            ch.then(nc.vector.tensor_tensor(b, a, over, ALU.subtract))
            v = lambda j: place[:, j, :]
            one3 = one[:, :, :, :].rearrange("p t k e -> p (t k) e")
            prod3 = prod[:, :, :, :].rearrange("p t k e -> p (t k) e")
            RANK, EXP, BASE, QQ, SLOT, TILE, OV = range(7)
            for k in range(2):
                ins = nc.vector.tensor_tensor(prod[:, :, k, :], one[:, :, k, :], cnt[:, 0:NT, :], ALU.mult)
            ch.then(ins)
            ch.then(nc.vector.tensor_reduce(v(RANK), prod3, AX.X, ALU.add))
            ch.then(nc.vector.tensor_tensor(prod3, one3, self.c(C_EI, NEXP).unsqueeze(1).broadcast_to([P, 2 * NT, NEXP]), ALU.mult))
            ch.then(nc.vector.tensor_reduce(v(EXP), prod3, AX.X, ALU.add))
            ch.then(nc.vector.tensor_tensor(prod3, one3, b.unsqueeze(1).broadcast_to([P, 2 * NT, NEXP]), ALU.mult))
            ch.then(nc.vector.tensor_reduce(v(BASE), prod3, AX.X, ALU.add))
            ch.then(nc.vector.tensor_scalar(v(QQ), v(RANK), float(CAP), None, ALU.is_ge))
            for i in range(2, QMAX + 1):
                ch.then(nc.vector.scalar_tensor_tensor(v(QQ), v(RANK), float(CAP * i), v(QQ), ALU.is_ge, ALU.add))
            ch.then(nc.vector.scalar_tensor_tensor(v(SLOT), v(QQ), -float(CAP), v(RANK), ALU.mult, ALU.add))
            ch.then(nc.vector.tensor_scalar(v(OV), v(QQ), 0.0, None, ALU.is_gt))
            ch.then(nc.vector.scalar_tensor_tensor(v(TILE), v(QQ), float(NEXP - 1), v(BASE), ALU.add, ALU.add))
            ch.then(nc.vector.tensor_tensor(v(TILE), v(TILE), v(EXP), ALU.subtract))
            ch.then(nc.vector.tensor_tensor(v(TILE), v(TILE), v(OV), ALU.mult))
            ch.then(nc.vector.tensor_tensor(v(TILE), v(TILE), v(EXP), ALU.add))
            ch.then(nc.vector.scalar_tensor_tensor(v(RANK), v(SLOT), float(NTILE), v(TILE), ALU.mult, ALU.add))
            nc.vector.tensor_copy(dest[:, :], v(RANK))
            ch.then(nc.vector.tensor_copy(tok[:, :], self.c(C_TOK, NT)))
            ch.then(nc.vector.scalar_tensor_tensor(v(BASE), v(TILE), float(CAP), v(SLOT), ALU.mult, ALU.add))
            nc.vector.tensor_copy(self.pair_row[:, :], v(BASE)).then_inc(dest_ready, 1)

        self.close(st)

    def experts(self):
        nc, I = self.nc, self.ins
        st = ExitStack()
        S = lambda n: self.sem(n, st)
        ps = self.ps
        FH = FF // 2
        wg = self.sb("wg", [P, 2, KD, FF], stack=st)
        wu = self.sb("wu", [P, 2, KD, FF], stack=st)
        wd = self.sb("wd", [P, 2, 2, KF // 2, D], stack=st)
        xg = self.sb("xg", [CAP, 2, D], stack=st)
        xT = self.sb("xTe", [P, 2, KD, CAP], stack=st)
        gc = self.sb("gc", [2 * CAP, 2, FF // 2], stack=st)
        hh = self.sb("hh", [2 * CAP, 2, FF // 2], stack=st)
        hT = self.sb("hTe", [P, KF // 2, 2 * CAP], stack=st)
        yb = self.sb("yb", [2 * CAP, 2, D // 2], stack=st)
        g_in, u_in, d_in = ([S(f"{n}_in{j}") for j in range(2)] for n in ("wg", "wu", "wd"))
        xg_in, y_out = ([S(f"{n}{j}") for j in range(2)] for n in ("xg_in", "y_out"))
        (x_turned, xT_ready, gate_done, up_done, gc_ready, ge_ready, hh_ready, h_turned, hT_ready, y_in_psum, y_copied, steps) = (
            S(n) for n in ("x_turned", "xTe_ready", "gate_done", "up_done", "gc_ready", "ge_ready", "hh_ready",
                           "h_turned", "hTe_ready", "ye_in_psum", "y_copied", "experts_dve"))
        vg = I["w_gate"].rearrange("(e p k) f -> e p k f", p=P, k=KD)
        vu = I["w_up"].rearrange("(e p k) f -> e p k f", p=P, k=KD)
        vd = I["w_down"].rearrange("(e h p j) f -> e p h j f", h=2, p=P, j=KF // 2)
        ys = self.ys_dram.rearrange("(n s) d -> n s d", s=CAP)
        at = lambda v, n: v[bass.ds(n, 1), :, :, :].rearrange("e p k f -> (e p) k f")
        block = st.enter_context(nc.Block("experts"))

        @block.sync
        def _(sp):
            def load(n, slot):
                sp.dma_start(wg[:, slot, :, :], at(vg, n)).then_inc(g_in[slot], 16)
                sp.dma_start(wu[:, slot, :, :], at(vu, n)).then_inc(u_in[slot], 16)

            def load_down(n, slot):
                sp.dma_start(wd[:, slot, :, :, :], vd[bass.ds(n, 1), :, :, :, :].rearrange("e p h j f -> (e p) h j f")).then_inc(d_in[slot], 16)

            for n in range(2):
                load(n, n)
                load_down(n, n)
            with sp.Fori(1, NEXP // 2) as i:
                for slot in range(2):
                    sp.wait_ge(up_done, i * 4 + 2 * (slot - 1))
                    load(i * 2 + slot, slot)
                    sp.wait_ge(y_in_psum, i * 4 + 2 * (slot - 1))
                    load_down(i * 2 + slot, slot)

        @block.gpsimd
        def _(pool):

            for n in range(NEXP):
                if n >= 2:
                    pool.wait_ge(x_turned, n - 1)
                pool.indirect_dma_start(out=xg[:, n % 2, :], out_offset=None, in_=self.hn_dram,
                                        in_offset=bass.IndirectOffsetOnAxis(ap=self.table[:, n:n + 1].bitcast(U32), axis=0)).then_inc(xg_in[n % 2], 16)

        @block.tensor
        def _(pe):
            def turn(out, rows, chunks):
                m, w = rows.shape
                ident = self.consts[0:m, C_ID:C_ID + m]
                for k in range(chunks):
                    dst, src = ps[:, out, m * k:m * k + m], rows[:, k:w:chunks]
                    if k == 0:
                        ins = nc.tensor.matmul(dst, src, ident, start=True, stop=True)
                    else:
                        ins = nc.tensor.transpose(dst, src, ident)
                return ins

            def gate_up(n, slot, half):
                pe.wait_ge(xT_ready, n + 1)
                for w, sem, bank, done in ((wg, g_in, slot, gate_done), (wu, u_in, 2 + slot, up_done)):
                    pe.wait_ge(sem[slot], half * 16)
                    for k in range(KD):
                        for h in range(2):
                            ins = nc.tensor.matmul(ps[h * CAP:h * CAP + CAP, bank, 0:FH], xT[:, slot, k, :], w[:, slot, k, h * FH:h * FH + FH],
                                                   start=(k == 0), stop=(k == KD - 1))
                            if k == KD - 1:
                                ins.then_inc(done, 1)

            def turn_x(n, slot, half, first=False):
                pe.wait_ge(xg_in[slot], half * 16)
                if not first:
                    pe.wait_ge(xT_ready, n)
                turn(4, xg[:, slot, :], KD).then_inc(x_turned, 1)

            def down(n, slot, half, first=False):
                pe.wait_ge(hT_ready, n + 1)
                pe.wait_ge(d_in[slot], half * 16)
                if not first:
                    pe.wait_ge(y_copied, n)
                for k in range(KF):
                    h, j = k // (KF // 2), k % (KF // 2)
                    for a in range(2):
                        ins = nc.tensor.matmul(ps[a * CAP:a * CAP + CAP, 6 + slot, :], hT[:, j, h * CAP:h * CAP + CAP], wd[:, slot, h, j, 512 * a:512 * a + 512],
                                               start=(k == 0), stop=(k == KF - 1))
                        if k == KF - 1:
                            ins.then_inc(y_in_psum, 1)

            def turn_h(n, slot):
                pe.wait_ge(hh_ready, n + 1)
                turn(5, hh[:, slot, :], KF // 2).then_inc(h_turned, 1)

            turn_x(0, 0, 1, first=True)
            gate_up(0, 0, 1)
            turn_x(1, 1, 1)
            turn_h(0, 0)
            gate_up(1, 1, 1)
            turn_x(2, 0, 2)
            down(0, 0, 1, first=True)
            turn_h(1, 1)
            with pe.Fori(1, NEXP // 2 - 1) as i:
                for slot in range(2):
                    n = i * 2 + slot
                    gate_up(n, slot, i + 1)
                    turn_x(n + 1, 1 - slot, i + 1 + slot)
                    down(n + (-1), 1 - slot, i + slot)
                    turn_h(n, slot)
            n, half = NEXP - 2, NEXP // 2
            gate_up(n, 0, half)
            turn_x(n + 1, 1, half)
            down(n - 1, 1, half - 1)
            turn_h(n, 0)
            gate_up(n + 1, 1, half)
            down(n, 0, half)
            turn_h(n + 1, 1)
            down(n + 1, 1, half)

        @block.vector
        def _(dve):
            def link(ins, count):
                ins.then_inc(steps, 1)
                dve.wait_ge(steps, count)

            def take_x(n, slot):
                dve.wait_ge(x_turned, n + 1)
                nc.vector.tensor_copy(xT[:, slot, :, :].rearrange("p k s -> p (k s)"), ps[:, 4, 0:KD * CAP]).then_inc(xT_ready, 1)

            def act_fn(n, slot):
                g, u = ps[0:2 * CAP, slot, 0:FH], ps[0:2 * CAP, 2 + slot, 0:FH]
                dve.wait_ge(gate_done, n * 2 + 2)
                nc.vector.tensor_scalar(gc[:, slot, :], g, -80.0, None, ALU.max).then_inc(gc_ready, 1)
                dve.wait_ge(ge_ready, n + 1)
                link(nc.vector.tensor_scalar(gc[:, slot, :], gc[:, slot, :], 1.0, None, ALU.add), n * 3 + 1)
                link(nc.vector.reciprocal(gc[:, slot, :], gc[:, slot, :]), n * 3 + 2)
                link(nc.vector.tensor_tensor(gc[:, slot, :], gc[:, slot, :], g, ALU.mult), n * 3 + 3)
                dve.wait_ge(up_done, n * 2 + 2)
                nc.vector.tensor_tensor(hh[:, slot, :], gc[:, slot, :], u, ALU.mult).then_inc(hh_ready, 1)

            def take_h(n):
                dve.wait_ge(h_turned, n + 1)
                nc.vector.tensor_copy(hT[:, :, :].rearrange("p k s -> p (k s)"), ps[:, 5, 0:KF * CAP]).then_inc(hT_ready, 1)

            take_x(0, 0)
            take_x(1, 1)
            act_fn(0, 0)
            take_h(0)
            take_x(2, 0)
            act_fn(1, 1)
            take_h(1)
            take_x(3, 1)
            act_fn(2, 0)
            take_h(2)
            with dve.Fori(1, NEXP // 2 - 1) as i:
                for s in range(2):
                    n = i * 2 + (1 + s)
                    slot = (1 + s) % 2
                    take_x(n + 1, 1 - slot)
                    act_fn(n, slot)
                    take_h(n)
            n = NEXP - 1
            act_fn(n, 1)
            take_h(n)

        @block.scalar
        def _(act):
            def exp(n, slot):
                act.wait_ge(gc_ready, n + 1)
                nc.scalar.activation(gc[:, slot, :], gc[:, slot, :], ACT.Exp, scale=-1.0).then_inc(ge_ready, 1)

            def take_y(n, slot, uses):
                act.wait_ge(y_in_psum, n * 2 + 2)
                if uses is not None:
                    act.wait_ge(y_out[slot], uses * 32)
                nc.scalar.copy(yb[:, slot, :], ps[0:2 * CAP, 6 + slot, :]).then_inc(y_copied, 1)
                act.wait_ge(y_copied, n + 1)
                for h in range(2):
                    act.dma_start(ys[bass.ds(n, 1), :, 512 * h:512 * h + 512].rearrange("o s d -> (o s) d"), yb[h * CAP:h * CAP + CAP, slot, :]).then_inc(y_out[slot], 16)

            exp(0, 0)
            exp(1, 1)
            take_y(0, 0, None)
            exp(2, 0)
            take_y(1, 1, None)
            with act.Fori(1, NEXP // 2 - 1) as i:
                for s in range(2):
                    n = i * 2 + (1 + s)
                    slot = (1 + s) % 2
                    exp(n, slot)
                    take_y(n + (-1), 1 - slot, i)
            n = NEXP - 1
            exp(n, 1)
            take_y(n - 1, 0, NEXP // 2 - 1)
            take_y(n, 1, NEXP // 2 - 1)
            for slot in range(2):
                act.wait_ge(y_out[slot], 32 * (NEXP // 2))

        self.close(st)

    def overflow(self):
        nc, I = self.nc, self.ins
        st = ExitStack()
        S = lambda n: self.sem(n, st)
        ps = self.ps
        wg = self.sb("wgo", [P, KD, FF], stack=st)
        wu = self.sb("wuo", [P, KD, FF], stack=st)
        wd = self.sb("wdo", [P, KF, D], stack=st)
        xg = self.sb("xgo", [CAP, D], stack=st)
        xT = self.sb("xTo", [P, KD, CAP], stack=st)
        gc = self.sb("gco", [CAP, FF], stack=st)
        hh = self.sb("hho", [CAP, FF], stack=st)
        hT = self.sb("hTo", [P, KF, CAP], stack=st)
        yb = self.sb("ybo", [CAP, D], stack=st)
        (tile_free, w_in, xg_in, x_turned, xT_ready, gate_up, gc_ready, ge_ready, a1, a2, a3, hh_ready, h_turned, hT_ready,
         y_in_psum, y_ready, y_out) = (S(n) for n in (
             "tile_free", "o_w_in", "o_xg_in", "o_x_turned", "o_xT", "o_gate_up", "o_gc", "o_ge", "o_a1", "o_a2", "o_a3",
             "o_hh", "o_h_turned", "o_hT", "o_y_psum", "o_y_ready", "o_y_out"))
        vg = I["w_gate"].rearrange("(e p k) f -> e p k f", p=P, k=KD)
        vu = I["w_up"].rearrange("(e p k) f -> e p k f", p=P, k=KD)
        vd = I["w_down"].rearrange("(e p k) f -> e p k f", p=P, k=KF)
        ys = self.ys_dram.rearrange("(n s) d -> n s d", s=CAP)
        at = lambda v, n: v[bass.ds(n, 1), :, :, :].rearrange("e p k f -> (e p) k f")

        def needed(eng):
            return eng.If(eng.value_load(self.n_over[0:1, 0:1], min_val=0, max_val=NOVER) > 0)

        block = st.enter_context(nc.Block("overflow"))

        @block.sync
        def _(sp):
            with needed(sp):
                with sp.Fori(0, NOVER) as j:
                    sp.wait_ge(tile_free, j + 1)
                    e = sp.value_load(self.over_e[0:1, bass.ds(j, 1)], min_val=0, max_val=NEXP - 1)
                    sp.dma_start(wg[:, :, :], at(vg, e)).then_inc(w_in, 16)
                    sp.dma_start(wu[:, :, :], at(vu, e)).then_inc(w_in, 16)
                    sp.dma_start(wd[:, :, :], at(vd, e)).then_inc(w_in, 16)

        @block.gpsimd
        def _(pool):
            with needed(pool):
                pool.sem_inc(tile_free, 1)
                for j in range(NOVER):
                    pool.indirect_dma_start(out=xg[:, :], out_offset=None, in_=self.hn_dram,
                                            in_offset=bass.IndirectOffsetOnAxis(ap=self.table[:, NEXP + j:NEXP + j + 1].bitcast(U32), axis=0)).then_inc(xg_in, 16)
                    pool.wait_ge(y_out, 16 * (j + 1))
                    pool.sem_inc(tile_free, 1)

        @block.tensor
        def _(pe):
            ident = self.consts[0:CAP, C_ID:C_ID + CAP]

            def turn(out, rows, chunks):
                w = rows.shape[-1]
                for k in range(chunks):
                    dst, src = ps[:, out, CAP * k:CAP * k + CAP], rows[:, k:w:chunks]
                    if k == 0:
                        ins = nc.tensor.matmul(dst, src, ident, start=True, stop=True)
                    else:
                        ins = nc.tensor.transpose(dst, src, ident)
                return ins

            with needed(pe):
                with pe.Fori(0, NOVER) as j:
                    pe.wait_ge(xg_in, j * 16 + 16)
                    turn(4, xg[:, :], KD).then_inc(x_turned, 1)
                    pe.wait_ge(xT_ready, j + 1)
                    pe.wait_ge(w_in, j * 48 + 48)
                    for a, w in enumerate((wg, wu)):
                        for k in range(KD):
                            ins = nc.tensor.matmul(ps[0:CAP, a, :], xT[:, k, :], w[:, k, :], start=(k == 0), stop=(k == KD - 1))
                    ins.then_inc(gate_up, 1)
                    pe.wait_ge(hh_ready, j + 1)
                    turn(5, hh[:, :], KF).then_inc(h_turned, 1)
                    pe.wait_ge(hT_ready, j + 1)
                    for a in range(2):
                        for k in range(KF):
                            ins = nc.tensor.matmul(ps[0:CAP, 6 + a, :], hT[:, k, :], wd[:, k, 512 * a:512 * a + 512], start=(k == 0), stop=(k == KF - 1))
                    ins.then_inc(y_in_psum, 1)

        @block.vector
        def _(dve):
            with needed(dve):
                with dve.Fori(0, NOVER) as j:
                    dve.wait_ge(x_turned, j + 1)
                    nc.vector.tensor_copy(xT[:, :, :].rearrange("p k s -> p (k s)"), ps[:, 4, 0:KD * CAP]).then_inc(xT_ready, 1)
                    dve.wait_ge(gate_up, j + 1)
                    nc.vector.tensor_scalar(gc[:, :], ps[0:CAP, 0, :], -80.0, None, ALU.max).then_inc(gc_ready, 1)
                    dve.wait_ge(ge_ready, j + 1)
                    nc.vector.tensor_scalar(gc[:, :], gc[:, :], 1.0, None, ALU.add).then_inc(a1, 1)
                    dve.wait_ge(a1, j + 1)
                    nc.vector.reciprocal(gc[:, :], gc[:, :]).then_inc(a2, 1)
                    dve.wait_ge(a2, j + 1)
                    nc.vector.tensor_tensor(gc[:, :], gc[:, :], ps[0:CAP, 0, :], ALU.mult).then_inc(a3, 1)
                    dve.wait_ge(a3, j + 1)
                    nc.vector.tensor_tensor(hh[:, :], gc[:, :], ps[0:CAP, 1, :], ALU.mult).then_inc(hh_ready, 1)
                    dve.wait_ge(h_turned, j + 1)
                    nc.vector.tensor_copy(hT[:, :, :].rearrange("p k s -> p (k s)"), ps[:, 5, 0:KF * CAP]).then_inc(hT_ready, 1)
                    dve.wait_ge(y_in_psum, j + 1)
                    nc.vector.tensor_copy(yb[:, :].rearrange("p (a n) -> p a n", a=2), ps[0:CAP, 6:8, :]).then_inc(y_ready, 1)

        @block.scalar
        def _(act):
            with needed(act):
                with act.Fori(0, NOVER) as j:
                    act.wait_ge(gc_ready, j + 1)
                    nc.scalar.activation(gc[:, :], gc[:, :], ACT.Exp, scale=-1.0).then_inc(ge_ready, 1)
                    act.wait_ge(y_ready, j + 1)
                    act.dma_start(ys[bass.ds(j + NEXP, 1), :, :].rearrange("o s d -> (o s) d"), yb[:, :]).then_inc(y_out, 16)

        self.close(st)

    def combine(self):
        nc, O = self.nc, self.outs
        st = ExitStack()
        S = lambda n: self.sem(n, st)
        NT = TILES + 1
        rows = self.sb("rows", [P, NT, 2, D], stack=st)
        h = self.sb("h7", [P, NT, D], stack=st)
        rows_in = [S(f"rows_in{t}") for t in range(NT)]
        h_in = S("h_in")
        steps, y_ready, stored = S("combine_dve"), S("y_ready"), S("y_stored")
        block = st.enter_context(nc.Block("combine"))

        @block.gpsimd
        def _(pool):
            for t in range(NT):
                for k in range(2):
                    pool.indirect_dma_start(out=rows[0:ROWS[t], t, k, :], out_offset=None, in_=self.ys_dram,
                                            in_offset=bass.IndirectOffsetOnAxis(ap=self.pair_row[0:ROWS[t], 2 * t + k:2 * t + k + 1].bitcast(U32), axis=0)).then_inc(rows_in[t], 16)
            pool.wait_ge(self.moved, 32)
            pool.wait_ge(self.blanked, 16)

        @block.vector
        def _(dve):
            ch = Chain(dve, steps)
            dve.wait_ge(h_in, 16 * NT)
            for t in range(NT):
                r = ROWS[t]
                dve.wait_ge(rows_in[t], 32)
                ch.then(nc.vector.scalar_tensor_tensor(h[0:r, t, :], rows[0:r, t, 0, :], self.pair_w[0:r, t, 0:1], h[0:r, t, :], ALU.mult, ALU.add))
                nc.vector.scalar_tensor_tensor(h[0:r, t, :], rows[0:r, t, 1, :], self.pair_w[0:r, t, 1:2], h[0:r, t, :], ALU.mult, ALU.add).then_inc(y_ready, 1)

        @block.sync
        def _(sp):
            for t in range(NT):
                sp.dma_start(h[0:ROWS[t], t, :], self.h_dram[t * P:t * P + ROWS[t], :]).then_inc(h_in, 16)
            for t in range(NT):
                sp.wait_ge(y_ready, t + 1)
                sp.dma_start(O["y"][t * P:t * P + ROWS[t], :], h[0:ROWS[t], t, :]).then_inc(stored, 16)
            sp.wait_ge(stored, 16 * NT)

        self.close(st)

    def run(self):
        nc = self.nc
        sb = self.sb
        with self.stack:
            self.moved = self.sem("moved", self.stack)
            self.blanked = self.sem("blanked", self.stack)
            self.kv_in = [self.sem(f"kv_in{j}", self.stack) for j in range(2)]
            self.pages_in, self.w1_in = self.sem("pages_in", self.stack), self.sem("w1_in", self.stack)
            self.ps = self.stack.enter_context(nc.psum_tensor("ps", [P, 8, 512], F32))
            self.pz = self.ps[:, 0:4, :]
            self.pt = self.ps[:, 4:6, :].rearrange("p a (k t) -> p (a k) t", t=P)
            self.gate_dram = nc.dram_tensor("gate_dram", [NB, 24], F32).ap()
            self.h_dram = nc.dram_tensor("h_dram", [NTOK, D], F32).ap()
            self.hn_dram = nc.dram_tensor("hn_dram", [NTOK, D], F32).ap()
            self.table_dram = nc.dram_tensor("table_dram", [CAP * NTILE, 1], I32).ap()
            self.ys_dram = nc.dram_tensor("ys_dram", [CAP * NTILE, D], F32).ap()
            self.consts = sb("consts", [P, CW])
            self.table = sb("table", [CAP, NTILE], I32)
            self.pair_w = sb("pair_w", [P, TILES + 1, 2])
            self.pair_row = sb("pair_row", [P, 2 * (TILES + 1)], I32)
            self.over_e = sb("over_e", [1, NOVER], I32)
            self.n_over = sb("n_over", [1, 1], I32)
            with ExitStack() as front:
                self.z = sb("z", [P, TILES + 1, ZW], stack=front)
                self.o_s = sb("o_s", [NB, 768], stack=front)
                with ExitStack() as blocks:
                    self.kcT = sb("kcT", [P, NSEQ, 64], stack=blocks)
                    self.vc = sb("vc", [64, NSEQ, 128], stack=blocks)
                    with ExitStack() as pages:
                        self.raw = self.sb("raw", [P, 2, 4, 2, 512], stack=pages)
                        self.w1 = self.sb("w1", [P, 2, 16, 128], stack=pages)
                        self.pages = self.sb("pages", [1, NB * NB], I32, stack=pages)
                        self.project()
                        self.stream()
                    self.o = sb("o", [P, TILES, 768], stack=blocks)
                    self.attend()
                    self.mix()
            self.experts()
            self.overflow()
            self.combine()


def kernel(**inputs):
    import numpy as np
    import concourse.bacc as bacc
    from concourse.bass_utils import run_bass_kernel_spmd

    f = {k: np.asarray(v) for k, v in inputs.items()}
    heads = [g * R + r for r in range(R) for g in range(G)]
    col = lambda base, unit, order: [base + o * unit + j for o in order for j in range(unit)]
    kv = 768
    order = (list(range(256)) + col(256, HD, heads)
             + [kv + ((br * 2 + 0) * G + g) * HD + j for br in range(3) for g in range(G) for j in range(HD)]
             + list(range(1560, 1816))
             + [kv + ((br * 2 + 1) * G + g) * HD + j for br in range(3) for g in range(G) for j in range(HD)]
             + [1536 + h * 3 + br for br in range(3) for h in heads])
    mixed = list(range(256)) + col(256, HD, heads) + list(range(768, 1024))
    arrays = {
        "consts": constants()[0], "bands": constants()[1],
        "x": np.concatenate([f["x_prompt"][0], f["x_sample"][:, 0]], 0),
        "mem": f["mem_prompt"][0],
        "w_in": f["w_in"][0][:, order],
        "w_mem": f["w_mem_kv"][0],
        "g_rows": np.concatenate([f["g_attn"], f["g_mem"]], 0),
        "g_head": np.concatenate([np.tile(f["g_q"][0], H), np.repeat(f["g_k"][0][:, None], G, 1).reshape(-1),
                                  np.tile(f["g_mq"][0], MH), np.tile(f["g_mk"][0], MH)]),
        "cache_kv": f["cache_kv"][0].reshape(-1, 512),
        "cache_win": f["cache_win"][0].reshape(-1, 256),
        "cache_mem": f["cache_mem_kv"][0].reshape(-1, 512),
        "state_pool": f["state_pool"][0].reshape(-1, 256),
        "page_table": f["page_table"].reshape(1, -1).astype(np.int32),
        "pe": np.ascontiguousarray(f["pe_cmp"][0].reshape(2, 16, 128).transpose(2, 0, 1)),
        "w_cmp1": f["w_cmp1"][0], "w_cmp2": f["w_cmp2"][0],
        "w_pool": f["w_pool"][0].reshape(-1, 64),
        "w_out": f["w_out"][0][mixed],
        "mix_rows": np.concatenate([f["g_mix"][0][mixed], f["g_ffn"][0], f["s_pool"][0], f["b_router1"][0], f["b_router2"][0].reshape(-1)]),
        "w_router": np.concatenate([f["w_router1"][0], f["w_router2"][0].reshape(D, -1)], 1),
        "w_gate": f["w_gate"][0].reshape(-1, FF), "w_up": f["w_up"][0].reshape(-1, FF),
        "w_down": f["w_down"][0].reshape(-1, D),
    }
    shapes = {
        "y": (NTOK, D), "kv_p": (T, 512), "kv_s": (NB, 512), "win_p": (T, 256), "win_s": (NB * T, 256),
        "pool_p": (STATE, 256), "pool_s": (NB * STATE, 256), "mem_p": (MEM, 512),
    }
    nc = bacc.Bacc("TRN2", target_bir_lowering=False, num_devices=1)
    arrays = {k: np.ascontiguousarray(v) for k, v in arrays.items()}
    ins = {k: nc.dram_tensor(f"in_{k}", v.shape, mybir.dt.from_np(v.dtype), kind="ExternalInput").ap() for k, v in arrays.items()}
    outs = {k: nc.dram_tensor(f"out_{k}", s, F32, kind="ExternalOutput").ap() for k, s in shapes.items()}
    Kernel(nc, ins, outs).run()
    r = run_bass_kernel_spmd(nc, [{f"in_{k}": v for k, v in arrays.items()}], core_ids=[0]).results[0]
    o = {k: r[f"out_{k}"] for k in shapes}
    return (o["y"][:T].reshape(1, T, D), o["y"][T:].reshape(NB, 1, D),
            o["kv_p"].reshape(1, 1, T, 4, 2, 64), o["kv_s"].reshape(1, NB, 1, 4, 2, 64),
            o["win_p"].reshape(1, 1, T, 2, 2, 64), o["win_s"].reshape(1, NB, T, 2, 2, 64),
            o["pool_p"].reshape(1, 1, STATE, 256), o["pool_s"].reshape(1, NB, STATE, 256),
            o["mem_p"].reshape(1, 1, MEM, 2, 4, 64))
```

```python
from contextlib import ExitStack

import concourse.bass as bass
from concourse import mybir

F32 = mybir.dt.float32
BF16 = mybir.dt.bfloat16
I32 = mybir.dt.int32
U32 = mybir.dt.uint32
ALU = mybir.AluOpType
ACT = mybir.ActivationFunctionType
AX = mybir.AxisListType

P = 128
D = 1024
KD = D // P
T = 512
NB = 8
PAST = 1024
PAGE = 128
HD = 64
R, G = 4, 2
H = R * G
MEM = 256
MH = 4
EPS = 1e-6
SCALE = HD ** -0.5
NEG = -1e30
WINDOWS = (2, 4, 8, 16)
STATE = 15
TILES = T // P
ROWS = [P] * TILES + [NB]
NC_P = T // 16 - 1
NC_S = PAST // 16 - 1
NSEQ = NB + 1

U0, Q0, K0, M0, V0, G0 = 0, 256, 768, 1152, 1408, 1792
ZW = 1816
ZC = ZW // 4
NG = (V0 - Q0) // HD

NEXP = 32
FF = 512
KF = FF // P
CAP = 64
NTOK = T + NB
NOVER = (2 * NTOK) // (CAP + 1)
NTILE = NEXP + NOVER
QMAX = (NTOK - 1) // CAP

C_ID = 0
C_CAUS = C_ID + P
C_CADD = C_CAUS + P
C_CMUL = C_CADD + TILES * 32
C_COS = C_CMUL + TILES * 32
C_SIN = C_COS + 5 * 8
C_UP = C_SIN + 5 * 8
C_ONE = C_UP + P
C_RG = C_ONE + P
C_S8 = C_RG + 64
C_BLK = C_S8 + NB
C_G4 = C_BLK + 14
C_E8 = C_G4 + 4
C_EI = C_E8 + 8
C_TOK = C_EI + 64
C_CAP = C_TOK + TILES + 1
C_SEL = C_CAP + QMAX
CW = C_SEL + 16 * NB

C_BAND = 0
C_PST = C_BAND + 12 * P
C_PDG = C_PST + 4 * NB
BW = C_PDG + 4 * NB

def constants():
    import numpy as np
    c = np.zeros((P, CW), np.float32)
    i = np.arange(P)
    c[:, C_ID:C_ID + P] = np.eye(P)
    c[:, C_CAUS:C_CAUS + P] = np.where(i[None, :] <= i[:, None], 0.0, NEG)
    for t in range(TILES):
        ok = (np.arange(32)[None, :] * 16 + 31 <= (t * P + i)[:, None]) & (np.arange(32) < NC_P)[None, :]
        c[:, C_CADD + 32 * t:C_CADD + 32 * t + 32] = np.where(ok, 0.0, NEG)
        c[:, C_CMUL + 32 * t:C_CMUL + 32 * t + 32] = ok
    inv = np.power(np.float32(500000.0), -np.arange(8, dtype=np.float32) * np.float32(2.0) / np.float32(16))
    for t in range(5):
        pos = (t * P + i if t < TILES else np.full(P, PAST)).astype(np.float32)
        ang = pos[:, None] * inv[None, :]
        c[:, C_COS + 8 * t:C_COS + 8 * t + 8] = np.cos(ang)
        c[:, C_SIN + 8 * t:C_SIN + 8 * t + 8] = np.sin(ang)
    bands = np.zeros((P, BW), np.float32)
    for w, win in enumerate(WINDOWS):
        tin, tout = i[:, None], i[None, :]
        eye = (tin == tout).astype(np.float32)
        own = ((tin <= tout) & (tout - tin < win)) / np.float32(win) - eye
        before = ((tout + P - tin < win) & (tout + P - tin > 0)) / np.float32(win)
        first = ((tin <= tout) & (tout - tin < win)) / np.minimum(tout + 1, win).astype(np.float32) - eye
        for j, m in enumerate((own, before, first)):
            o = C_BAND + (3 * w + j) * P
            bands[:, o:o + P] = m
        for b in range(NB):
            for s in range(STATE):
                if s >= STATE - (win - 1):
                    bands[b * STATE + s, C_PST + w * NB + b] = 1.0 / win
            bands[b, C_PDG + w * NB + b] = 1.0 / win - 1.0
    c[:, C_UP:C_UP + P] = i[:, None] < i[None, :]
    c[:, C_ONE:C_ONE + P] = 1.0
    j = np.arange(64)
    c[:64, C_RG:C_RG + 64] = (j[:, None] // 8 == j[None, :] // 8) & (j[:, None] % 2 == j[None, :] % 2)
    c[:64, C_S8:C_S8 + NB] = j[:, None] // 8 == np.arange(NB)[None, :]
    c[:, C_BLK:C_BLK + 14] = np.arange(1, 15)
    c[:, C_G4:C_G4 + 4] = [4, 3, 2, 1]
    c[:, C_E8:C_E8 + 8] = np.arange(8, 0, -1)
    c[:, C_EI:C_EI + 64] = np.arange(64)
    c[:, C_CAP:C_CAP + QMAX] = CAP * np.arange(1, QMAX + 1)
    c[:, C_TOK:C_TOK + 5] = i[:, None] + P * np.arange(5)[None, :]
    for u in range(2):
        for h in range(8):
            for b in range(4):
                c[32 * b + h, C_SEL + NB * (8 * u + h) + 4 * u + b] = 1.0
    return c, bands


class Chain:

    def __init__(self, eng, sem):
        self.eng, self.sem, self.n = eng, sem, 0

    def then(self, ins):
        self.n += 1
        ins.then_inc(self.sem, 1)
        self.eng.wait_ge(self.sem, self.n)


class Kernel:
    def __init__(self, nc, ins, outs):
        self.nc, self.ins, self.outs = nc, ins, outs
        self.stack = ExitStack()
        self.n_sems, self.stage_sems = 0, []

    def sb(self, name, shape, dt=F32, stack=None):
        return (stack or self.stack).enter_context(self.nc.sbuf_tensor(name, shape, dt))

    def sem(self, name, stack):
        self.n_sems += 1
        s = self.nc.alloc_semaphore(f"{name}_{self.n_sems}")
        if stack is not self.stack:
            self.stage_sems.append(s)
        return s

    def close(self, stage):
        stage.close()
        self.nc.clear_and_free_semaphores(self.stage_sems)
        self.nc.all_engine_barrier()
        self.stage_sems = []

    def c(self, at, n, rows=P):
        return self.consts[0:rows, at:at + n]

    def load_pages(self, eng, b, slot):
        src = self.ins["cache_kv"].rearrange("(g p t) c -> g p (t c)", p=64, t=2)
        for pg in range(PAST // PAGE):
            at = eng.value_load(self.pages[0:1, bass.ds(b * NB + pg, 1)], min_val=0, max_val=src.shape[0] - 1)
            half = slice(64 * (pg % 2), 64 * (pg % 2) + 64)
            eng.dma_start(self.raw[half, slot, pg // 2, :, :].rearrange("p t c -> p (t c)"),
                          src[bass.ds(at, 1), :, :].rearrange("g p c -> (g p) c")).then_inc(self.kv_in[slot], 16)

    def project(self):
        nc, I, O = self.nc, self.ins, self.outs
        st = ExitStack()
        n_items = 7
        rows = ROWS + [P, P]
        w_in = self.sb("w_in", [P, KD, ZW], stack=st)
        w_mem = self.raw[:, 1, :, :, :].rearrange("p a b c -> p (a b) c")
        g_rows = self.sb("g_rows", [P, 2, D], stack=st)
        g_head = self.sb("g_head", [P, V0 - Q0 + HD * MH], stack=st)
        xin = self.sb("xin", [P, 3, D], stack=st)
        xn = self.sb("xn", [P, 2, D], stack=st)
        xT = self.sb("xT", [P, 2, KD, P], stack=st)
        junk = self.sb("junk", [P, 2, V0 - Q0], stack=st)
        stat = self.sb("stat", [P, n_items, 4], stack=st)
        gstat = self.sb("gstat", [P, n_items, NG], stack=st)
        blank = self.w1[0:CAP, :, :, :].rearrange("p a b c -> p (a b c)")[:, 0:D]
        blank_ready = self.sem("blank_ready", st)
        S = lambda n: self.sem(n, st)
        consts_in, gains_in, win_in, wmem_in = S("consts_in"), S("gains_in"), S("win_in"), S("wmem_in")
        x_in = [S(f"x_in{j}") for j in range(3)]
        dve_step, act_step = S("dve_step"), S("act_step")
        xn_ready, xT_in_psum, xT_ready, z_in_psum, z_ready = (S(n) for n in (
            "xn_ready", "xT_in_psum", "xT_ready", "z_in_psum", "z_ready"))
        ms_ready, rms_ready, sq_ready, gms_ready, grms_ready, z_done, stored = (S(n) for n in (
            "ms_ready", "rms_ready", "sq_ready", "gms_ready", "grms_ready", "z_done", "stored"))
        pz, pt = self.pz, self.pt
        z = self.z
        memz = w_in[:, 0, 0:1024].rearrange("p (j n) -> p j n", j=2)
        xs = [I["x"][t * P:t * P + rows[t], :] for t in range(5)] + [I["mem"][j * P:(j + 1) * P, :] for j in range(2)]

        def zt(t):
            return z[:, t, :] if t < 5 else memz[:, t - 5, :]

        def groups(t):
            return (Q0, NG) if t < 5 else (0, MH)

        chunks = [4] * 5 + [1, 1]
        done = lambda t: sum(chunks[:t])

        def in_psum(t, a):
            if t < TILES:
                return pz[:, a, 0:ZC]
            return pz[32 * a:32 * a + NB, a, 0:ZC] if t == TILES else pz[:, t - 5, :]

        block = st.enter_context(nc.Block("project"))

        @block.sync
        def _(sp):
            sp.dma_start(xin[0:rows[0], 0, :], xs[0]).then_inc(x_in[0], 16)
            sp.dma_start(self.consts[:, :], I["consts"]).then_inc(consts_in, 16)
            sp.dma_start(g_rows[:, :, :], I["g_rows"].partition_broadcast(P)).then_inc(gains_in, 16)
            for j in range(4):
                sp.dma_start(w_in[:, 2 * j:2 * j + 2, :], I["w_in"].rearrange("(p k) n -> p k n", k=KD)[:, 2 * j:2 * j + 2, :]).then_inc(win_in, 16)
                if j == 0:
                    sp.dma_start(xin[0:rows[1], 1, :], xs[1]).then_inc(x_in[1], 16)
            for t in range(1, n_items):
                if t >= 3:
                    sp.wait_ge(xn_ready, t - 2)
                if t >= 2:
                    sp.dma_start(xin[0:rows[t], t % 3, :], xs[t]).then_inc(x_in[t % 3], 16)
                if t == 1:
                    sp.dma_start(g_head[:, :], I["g_head"].partition_broadcast(P)).then_inc(gains_in, 16)
                    sp.dma_start(w_mem[:, :, :], I["w_mem"].rearrange("(p k) n -> p k n", k=KD)).then_inc(wmem_in, 16)
            sp.dma_start(self.pages[:, :], I["page_table"]).then_inc(self.pages_in, 16)
            sp.wait_ge(self.pages_in, 16)
            self.load_pages(sp, 0, 0)
            sp.wait_ge(self.blanked, 16)
            sp.dma_start(self.w1[:, :, :, :], I["w_cmp1"].rearrange("q (l p) n -> p q l n", p=P)).then_inc(self.w1_in, 16)
            k3 = lambda t, r: z[0:r, t, K0:K0 + 384].rearrange("p (b c) -> p b c", b=3)
            v3 = lambda t, r: z[0:r, t, V0:V0 + 384].rearrange("p (b c) -> p b c", b=3)
            for t in range(5):
                r = rows[t]
                sp.wait_ge(z_done, t + 1)
                if t < TILES:
                    kv, win, at = O["kv_p"], O["win_p"], t * P
                else:
                    kv, win, at = O["kv_s"], None, 0
                dst = kv[at:at + r, :].rearrange("p (b s c) -> p b s c", b=2, s=2)
                sp.dma_start(dst[:, :, 0, :], k3(t, r)[:, 0:2, :]).then_inc(stored, 16)
                sp.dma_start(dst[:, :, 1, :], v3(t, r)[:, 0:2, :]).then_inc(stored, 16)
                if t < TILES:
                    sp.dma_start(win[at:at + r, 0:128], k3(t, r)[:, 2, :]).then_inc(stored, 16)
                    sp.dma_start(win[at:at + r, 128:256], v3(t, r)[:, 2, :]).then_inc(stored, 16)
                else:
                    dst = O["win_s"].rearrange("(b n) c -> b n c", b=NB)[:, T - 1, :]
                    sp.dma_start(dst[:, 0:128], k3(t, r)[:, 2, :]).then_inc(stored, 16)
                    sp.dma_start(dst[:, 128:256], v3(t, r)[:, 2, :]).then_inc(stored, 16)
                    sp.dma_start(O["pool_s"].rearrange("(b n) c -> b n c", b=NB)[:, STATE - 1, :],
                                 z[0:NB, t, U0:U0 + 256]).then_inc(stored, 16)
            sp.dma_start(O["pool_p"], z[P - STATE:P, TILES - 1, U0:U0 + 256]).then_inc(stored, 16)
            for j in range(2):
                sp.wait_ge(z_done, 6 + j)
                sp.dma_start(O["mem_p"][j * P:(j + 1) * P, :], memz[:, j, :]).then_inc(stored, 16)
            sp.wait_ge(stored, 16 * (4 * TILES + 5 + 1 + 2))

        @block.gpsimd
        def _(pool):
            nc.gpsimd.memset(blank[:, :], 0.0).then_inc(blank_ready, 1)
            pool.wait_ge(blank_ready, 1)
            pool.wait_ge(win_in, 64)
            pool.dma_start(self.ys_dram[NEXP * CAP:, :].rearrange("(a p) d -> p a d", p=CAP), blank[:, :].unsqueeze(1).broadcast_to([CAP, NOVER, D])).then_inc(self.blanked, 16)
            src = I["cache_win"].rearrange("(b n) c -> b (n c)", b=NB)
            dst = O["win_s"].rearrange("(b n) c -> b (n c)", b=NB)
            w = (T - 1) * 256
            pool.dma_start(dst[:, 0:w].rearrange("b (a n) -> b a n", a=7), src[:, 256:256 + w].rearrange("b (a n) -> b a n", a=7)).then_inc(self.moved, 16)
            src = I["state_pool"].rearrange("(b n) c -> b (n c)", b=NB)
            dst = O["pool_s"].rearrange("(b n) c -> b (n c)", b=NB)
            pool.dma_start(dst[:, 0:(STATE - 1) * 256], src[:, 256:STATE * 256]).then_inc(self.moved, 16)
            pool.wait_ge(self.blanked, 16)

        @block.vector
        def _(dve):
            ch = Chain(dve, dve_step)

            def norm(t):
                r = rows[t]
                dve.wait_ge(x_in[t % 3], 16 * (t // 3 + 1))
                if t >= 2:
                    dve.wait_ge(xT_in_psum, t - 1)
                ch.then(nc.vector.tensor_tensor_reduce(xn[0:r, t % 2, :], xin[0:r, t % 3, :], xin[0:r, t % 3, :], 1.0, 0.0,
                                                       ALU.mult, ALU.add, stat[0:r, t, 0:1]))
                nc.vector.tensor_scalar(stat[0:r, t, 1:2], stat[0:r, t, 0:1], 1.0 / D, EPS, ALU.mult, ALU.add).then_inc(ms_ready, 1)
                dve.wait_ge(rms_ready, t + 1)
                ch.then(nc.vector.reciprocal(stat[0:r, t, 3:4], stat[0:r, t, 2:3]))
                if t == 0:
                    dve.wait_ge(gains_in, 32)
                nc.vector.scalar_tensor_tensor(xn[0:r, t % 2, :], xin[0:r, t % 3, :], stat[0:r, t, 3:4],
                                               g_rows[0:r, 0 if t < 5 else 1, :], ALU.mult, ALU.mult).then_inc(xn_ready, 1)

            def heads(t):
                r = rows[t]
                at, n = groups(t)
                w = n * HD
                buf = zt(t)[0:r, at:at + w]
                b3 = buf.rearrange("p (n d) -> p n d", d=HD)
                dve.wait_ge(sq_ready, t + 1)
                ch.then(nc.vector.tensor_reduce(gstat[0:r, t, 0:n], junk[0:r, t % 2, 0:w].rearrange("p (n d) -> p n d", d=HD), AX.X, ALU.add))
                nc.vector.tensor_scalar(gstat[0:r, t, 0:n], gstat[0:r, t, 0:n], 1.0 / HD, EPS, ALU.mult, ALU.add).then_inc(gms_ready, 1)
                dve.wait_ge(grms_ready, t + 1)
                ch.then(nc.vector.reciprocal(gstat[0:r, t, 0:n], gstat[0:r, t, 0:n]))
                ch.then(nc.vector.tensor_tensor(b3, b3, gstat[0:r, t, 0:n].unsqueeze(2).broadcast_to([r, n, HD]), ALU.mult))
                last = nc.vector.tensor_tensor(buf, buf, g_head[0:r, 0:w] if t < 5 else g_head[0:r, V0 - Q0:V0 - Q0 + w], ALU.mult)
                if t >= 5:
                    last.then_inc(z_done, 1)
                    return
                ch.then(last)
                h3 = zt(t)[0:r, Q0:M0].rearrange("p (n d) -> p n d", d=HD)
                x1, x2 = h3[:, :, 0:8], h3[:, :, 8:16]
                cos = self.c(C_COS + 8 * t, 8, r).unsqueeze(1).broadcast_to([r, 14, 8])
                sin = self.c(C_SIN + 8 * t, 8, r).unsqueeze(1).broadcast_to([r, 14, 8])
                if t == 0:
                    dve.wait_ge(consts_in, 16)
                rot = junk[0:r, t % 2, 0:448].rearrange("p (j n d) -> p j n d", j=4, d=8)
                for j, (a, b) in enumerate(((x1, cos), (x2, sin), (x2, cos), (x1, sin))):
                    last = nc.vector.tensor_tensor(rot[:, j, :, :], a, b, ALU.mult)
                ch.then(last)
                nc.vector.tensor_tensor(x1, rot[:, 0, :, :], rot[:, 1, :, :], ALU.subtract)
                nc.vector.tensor_tensor(x2, rot[:, 2, :, :], rot[:, 3, :, :], ALU.add).then_inc(z_done, 1)

            norm(0)
            norm(1)
            for t in range(n_items):
                if t + 2 < n_items:
                    norm(t + 2)
                heads(t)

        @block.scalar
        def _(act):
            def root(t):
                act.wait_ge(ms_ready, t + 1)
                nc.scalar.activation(stat[0:rows[t], t, 2:3], stat[0:rows[t], t, 1:2], ACT.Sqrt).then_inc(rms_ready, 1)

            def roots(t):
                n = groups(t)[1]
                act.wait_ge(gms_ready, t + 1)
                nc.scalar.activation(gstat[0:rows[t], t, 0:n], gstat[0:rows[t], t, 0:n], ACT.Sqrt).then_inc(grms_ready, 1)

            def take_x(t):
                act.wait_ge(xT_in_psum, t + 1)
                if t >= 2:
                    act.wait_ge(z_in_psum, done(t - 1))
                nc.scalar.copy(xT[:, t % 2, :, 0:rows[t]], pt[:, :, 0:rows[t]]).then_inc(xT_ready, 1)

            root(0)
            root(1)
            take_x(0)
            for t in range(n_items):
                r = rows[t]
                if t + 1 < n_items:
                    take_x(t + 1)
                if t + 2 < n_items:
                    root(t + 2)
                for a in range(chunks[t]):
                    act.wait_ge(z_in_psum, done(t) + a + 1)
                    dst = z[0:r, t, a * ZC:(a + 1) * ZC] if t < 5 else memz[:, t - 5, :]
                    nc.scalar.copy(dst, in_psum(t, a)).then_inc(z_ready, 1)
                act.wait_ge(z_ready, done(t + 1))
                at, n = groups(t)
                if t >= 2:
                    act.wait_ge(z_done, t - 1)
                nc.scalar.activation(junk[0:r, t % 2, 0:n * HD], zt(t)[0:r, at:at + n * HD], ACT.Square).then_inc(sq_ready, 1)
                roots(t)

        @block.tensor
        def _(pe):
            def turn(t):
                r = rows[t]
                pe.wait_ge(xn_ready, t + 1)
                if t >= 1:
                    pe.wait_ge(xT_ready, t)
                for k in range(KD):
                    ins = nc.tensor.transpose(pt[:, k, 0:r], xn[0:r, t % 2, k:D:KD], self.c(C_ID, r, r))
                ins.then_inc(xT_in_psum, 1)

            def bank_free(t, a):
                if t < 5:
                    before = done(t - 1) + a + 1 if t >= 1 else 0
                else:
                    before = done(5)
                if before:
                    pe.wait_ge(z_ready, before)

            def product(t, a, k):
                r = rows[t]
                rhs = w_in[:, k, a * ZC:(a + 1) * ZC] if t < 5 else w_mem[:, k, :]
                ins = nc.tensor.matmul(in_psum(t, a), xT[:, t % 2, k, 0:r], rhs, start=(k == 0), stop=(k == KD - 1))
                if k == KD - 1:
                    ins.then_inc(z_in_psum, 1)

            pe.wait_ge(consts_in, 16)
            turn(0)
            for t in range(n_items):
                if t + 1 < n_items:
                    turn(t + 1)
                pe.wait_ge(xT_ready, t + 1)
                if t == 5:
                    pe.wait_ge(wmem_in, 16)
                if t == 0 or t == TILES:
                    for a in range(4):
                        bank_free(t, a)
                    for k in range(KD):
                        if t == 0 and k % 2 == 0:
                            pe.wait_ge(win_in, 16 * (k // 2 + 1))
                        for a in range(4):
                            product(t, a, k)
                else:
                    for a in range(chunks[t]):
                        bank_free(t, a)
                        for k in range(KD):
                            product(t, a, k)

        self.close(st)

    def stream(self):
        nc, I, O = self.nc, self.ins, self.outs
        st = ExitStack()
        S = lambda n: self.sem(n, st)
        raw, w1 = self.raw, self.w1
        kvc = self.sb("kvc", [P, 4, 4, 2, 64], stack=st)
        winK = self.sb("winK", [P, 2, 4, 128], stack=st)
        memK = self.sb("memK", [P, 2, 2, 256], stack=st)
        XT = self.sb("XT", [P, 2, G, 512], stack=st)
        KsT = self.sb("KsT", [P, 1024], stack=st)
        KwT = self.sb("KwT", [P, 512], stack=st)
        KmT = self.sb("KmT", [P, 2, 256], stack=st)
        w2 = self.sb("w2", [P, 2, 64], stack=st)
        w2pad = self.sb("w2pad", [P, G, 128], stack=st)
        pe_pos = self.sb("pe_pos", [P, 2, 16], stack=st)
        hbias = self.sb("hbias", [P, 2], stack=st)
        hx = self.sb("hx", [P, 2, 256], stack=st)
        ht = self.sb("ht", [P, 256], stack=st)
        gel = self.sb("gel", [P, 2, 256], stack=st)
        Vs = self.sb("Vs", [P, NB, 4, 2, 128], stack=st)
        Vw = self.sb("Vw", [P, NB, 4, 128], stack=st)
        Vm = self.sb("Vm", [P, NB, 2, 256], stack=st)
        Q = self.sb("Q", [P, NB * 72], stack=st)
        Qm = self.sb("Qm", [P, 2, NB * 36], stack=st)
        kTn = self.sb("kTn", [P, 2, NB], stack=st)
        zb = self.sb("zb", [1, 512], BF16, stack=st)
        pages, kv_in = self.pages, self.kv_in
        gat = self.sb("gat", [NB, 24], stack=st)
        g64 = self.sb("g64", [64, 3], stack=st)
        wk_in, mk_in = ([S(f"{n}_in{j}") for j in range(2)] for n in ("wk", "mk"))
        v_in, w_in_, zeroed, steps_d, vs_ready = (S(n) for n in ("v_in", "cmp_w_in", "zeroed", "stream_dve", "vs_ready"))
        small_in_psum, q_ready, turned, out_a, out_d, kvc_ready = (S(n) for n in (
            "small_in_psum", "q_ready", "turned", "out_a", "out_d", "kvc_ready"))
        hid_in_psum, hx_ready, he_ready, gel_ready, cmp_in_psum, cmp_ready = (S(n) for n in (
            "hid_in_psum", "hx_ready", "he_ready", "gel_ready", "cmp_in_psum", "cmp_ready"))
        gate_out, gate_in, gclamp, gexp, gsig = (S(n) for n in ("gate_out", "gate_in", "gclamp", "gexp", "gsig"))
        cs_in_psum, ec, pc, imp_in_psum, es, ps_ready, pT_in_psum, pT_ready, o_in_psum, oT_ready, os_in_psum = (S(n) for n in (
            "cs_in_psum", "ec", "pc", "imp_in_psum", "es", "ps_ready", "pT_in_psum", "pT_ready", "o_in_psum", "oT_ready", "os_in_psum"))
        ps, z = self.ps, self.z
        sel0, win0, misc, hid, cmp_ = ps[:, 0:2, :], ps[:, 2, :], ps[:, 3, :], ps[:, 6, :], ps[:, 7, :]
        kcT, vc = self.kcT, self.vc
        smp = TILES
        blocks = [NC_S] * NB + [NC_P]
        ntile = [4] * NB + [2]
        units = [8] * NB + [4]
        first = [8 * s for s in range(NSEQ)]
        kind = lambda s, u: u if s < NB else u + 4
        hidv = hid.rearrange("p (q n) -> p q n", q=4)

        late = raw[:, 1, :, :, :].rearrange("p a b c -> p (a b c)")
        ssb, swb, smb = late[0:64, 0:1040], late[0:64, 1040:1568], late[0:32, 2400:2656]
        pTw = late[:, 1568:1824].rearrange("p (a b) -> p a b", a=4)
        pTm = late[:, 1824:1888].rearrange("p (a b) -> p a b", a=2)
        pTs = late[:, 1888:2400].rearrange("p (a b) -> p a b", a=8)
        dgn = late[0:64, 2656:2784].rearrange("p (a b) -> p a b", a=2)
        nw = late[0:NB, 2784:2912].rearrange("p (a b) -> p a b", a=2)
        oa, om = late[:, 2912:3168], late[:, 3168:3680]
        scb = self.sb("scb", [64, 64], stack=st)
        sst = self.sb("sst", [64, 4, 4], stack=st)
        imp = self.sb("imp", [64, 6, 16], stack=st)
        pTc = self.sb("pTc", [64, 64], stack=st)

        block = st.enter_context(nc.Block("stream"))

        marks = {}

        @block.vector
        def _(dve):
            ch = Chain(dve, steps_d)
            dve.wait_ge(zeroed, 6)
            def out(s):
                for u in range(1, units[s], 2):
                    dve.wait_ge(turned, first[s] + u + 1)
                    k = kind(s, u)
                    dst = (XT[:, (k - 4) // 2, 1, :] if k >= 4 else KsT[:, 512:1024] if k == 1
                           else KmT[:, :, :].rearrange("p a n -> p (a n)"))
                    w = 128 * ntile[s]
                    nc.vector.tensor_copy(dst[:, 0:w], ps[:, 5, 0:w]).then_inc(out_d, 1)

            def gelu(s):
                n = blocks[s]
                dve.wait_ge(hid_in_psum, s + 1)
                x = hx[:, s % 2, :].rearrange("p (q n) -> p q n", q=4)[:, :, 0:n]
                t = ht[:, :].rearrange("p (q n) -> p q n", q=4)[:, :, 0:n]
                for q in range(2):
                    ins = nc.vector.tensor_scalar(x[:, 2 * q:2 * q + 2, :], hidv[:, 2 * q:2 * q + 2, 0:n], hbias[:, q:q + 1], None, ALU.add)
                ch.then(ins)
                ch.then(nc.vector.tensor_tensor(t, x, x, ALU.mult))
                ch.then(nc.vector.tensor_scalar(t, t, 0.044715, 1.0, ALU.mult, ALU.add))
                ch.then(nc.vector.tensor_tensor(t, t, x, ALU.mult))
                nc.vector.tensor_scalar(t, t, -50.0, None, ALU.max).then_inc(hx_ready, 1)
                dve.wait_ge(he_ready, s + 1)
                ch.then(nc.vector.tensor_scalar(t, t, 1.0, None, ALU.add))
                ch.then(nc.vector.reciprocal(t, t))
                if s >= 2:
                    dve.wait_ge(cmp_in_psum, s - 1)
                nc.vector.tensor_tensor(gel[:, s % 2, :].rearrange("p (q n) -> p q n", q=4)[:, :, 0:n], t, x, ALU.mult).then_inc(gel_ready, 1)

            def keep(s):
                n = blocks[s]
                dve.wait_ge(cmp_in_psum, s + 1)
                nc.vector.tensor_copy(kcT[:, s, 0:n], cmp_[:, 0:n])
                nc.vector.tensor_copy(vc[0:n, s, :], cmp_[0:n, 128:256]).then_inc(cmp_ready, 1)

            nc.vector.tensor_scalar(gat[:, :], z[0:NB, smp, G0:G0 + 24], -80.0, None, ALU.max).then_inc(gclamp, 1)
            out(0)
            dve.wait_ge(small_in_psum, 1)
            nc.vector.tensor_copy(hbias[:, :], hid[:, 0:2])
            nc.vector.tensor_copy(w2pad[:, 0, 0:64], w2[:, 0, :])
            nc.vector.tensor_copy(w2pad[:, 1, 64:128], w2[:, 0, :])
            nc.vector.tensor_copy(kTn[:, :, :], cmp_[:, 48:64].rearrange("p (a b) -> p a b", a=2))
            for g in range(G):
                half = slice(64 * g, 64 * g + 64)
                nc.vector.tensor_copy(Q[half, :].rearrange("p (b x) -> p b x", x=72)[:, :, g:g + 2 * R:2],
                                      cmp_[half, 0:32].rearrange("p (r b) -> p b r", r=R))
                for hp in range(2):
                    h = 2 * hp + g
                    ins = nc.vector.tensor_copy(Qm[half, hp, :].rearrange("p (b x) -> p b x", x=36)[:, :, h:h + 1],
                                                cmp_[half, 32 + 8 * hp:40 + 8 * hp].unsqueeze(2))
            ins.then_inc(q_ready, 1)
            dve.wait_ge(gexp, 1)
            ch.then(nc.vector.tensor_scalar(gat[:, :], gat[:, :], 1.0, None, ALU.add))
            nc.vector.reciprocal(gat[:, :], gat[:, :]).then_inc(gsig, 1)
            def peak(j, rows, src, mark):
                ch.then(nc.vector.tensor_reduce(sst[0:rows, j, 0:1], src, AX.X, ALU.max))
                ch.then(nc.vector.tensor_scalar(sst[0:rows, j, 1:2], sst[0:rows, j, 0:1], -SCALE, None, ALU.mult))
                marks[mark] = ch.n

            def weights(j, rows, probs, gate, mark):
                ch.then(nc.vector.reciprocal(sst[0:rows, j, 3:4], sst[0:rows, j, 2:3]))
                if gate is None:
                    ch.then(nc.vector.tensor_scalar(probs, probs, sst[0:rows, j, 3:4], None, ALU.mult))
                else:
                    ch.then(nc.vector.tensor_scalar(probs, probs, sst[0:rows, j, 3:4], gate, ALU.mult, ALU.mult))
                if mark:
                    marks[mark] = ch.n

            for s in range(NSEQ):
                if s + 1 < NSEQ:
                    out(s + 1)
                if s == NB:
                    dve.wait_ge(vs_ready, NB)
                    ch.then(nc.vector.tensor_copy(smb[:, :], misc[64:96, 128:384]))
                    peak(1, 32, smb[:, :], "mmax")
                    nc.vector.memset(swb[:, 0:1], 0.0)
                    nc.vector.tensor_copy(swb[:, 1:512], win0[64:128, 1:512])
                    ch.then(nc.vector.tensor_copy(swb[:, 512:513], misc[0:64, 65:66]))
                    peak(2, 64, swb[:, 1:513], "wmax")
                gelu(s)
                if s >= 1:
                    keep(s - 1)
            keep(NSEQ - 1)

            dve.wait_ge(es, 1)
            weights(1, 32, smb[:, :], None, None)
            dve.wait_ge(gate_in, 16 * NB)
            dve.wait_ge(es, 2)
            weights(2, 64, swb[:, 1:513], g64[:, 2:3], None)
            ch.then(nc.vector.tensor_scalar(dgn[:, 1, :], self.c(C_ID, 64, 64), swb[:, 512:513], None, ALU.mult))
            marks["wp"] = ch.n
            dve.wait_ge(cs_in_psum, 1)
            ch.then(nc.vector.tensor_copy(scb[:, 0:NC_S], misc[0:64, 0:NC_S]))
            peak(0, 64, scb[:, 0:NC_S], "cmax")
            dve.wait_ge(es, 3)
            weights(0, 64, scb[:, 0:NC_S], None, "pc")
            dve.wait_ge(imp_in_psum, 1)
            ch.then(nc.vector.tensor_scalar(scb[:, 0:NC_S], scb[:, 0:NC_S], g64[:, 0:1], None, ALU.mult))
            marks["cg"] = ch.n
            ch.then(nc.vector.tensor_reduce(imp[:, 0, :], hid[0:64, 0:64].rearrange("p (n k) -> p n k", k=4), AX.X, ALU.add))
            ch.then(nc.vector.tensor_reduce(sst[:, 0, 0:1], imp[:, 0, 1:15], AX.X, ALU.min))
            ch.then(nc.vector.scalar_tensor_tensor(imp[:, 1, 1:15], imp[:, 0, 1:15], sst[:, 0, 0:1], self.c(C_BLK, 14, 64), ALU.is_equal, ALU.mult))
            ch.then(nc.vector.tensor_reduce(sst[:, 0, 1:2], imp[:, 1, 1:15], AX.X, ALU.max))
            ch.then(nc.vector.tensor_scalar(imp[:, 2, 1:15], self.c(C_BLK, 14, 64), sst[:, 0, 1:2], NEG, ALU.is_equal, ALU.mult))
            for par in range(2):
                v = lambda a: a.rearrange("p (c t k j) -> p c t k j", c=4, t=2, k=4)[:, :, par, :, :]
                out4 = ssb[:, 0:1024].rearrange("p (c t k j) -> p c t k j", c=4, t=2, k=4)
                in4 = sel0[0:64, :, :].rearrange("p a (c t k j) -> p (a c) t k j", c=2, t=2, k=4)
                mask = imp[:, 2, :].rearrange("p (c k) -> p c k", c=4).unsqueeze(3).broadcast_to([64, 4, 4, 32])
                nc.vector.tensor_tensor(out4[:, :, par, :, :], in4[:, :, par, :, :], mask, ALU.add)
            ch.then(nc.vector.tensor_copy(ssb[:, 1024:1025], misc[0:64, 64:65]))
            peak(3, 64, ssb[:, 0:1025], "smax")
            dve.wait_ge(pT_in_psum, 1)
            nc.vector.tensor_copy(late[:, 1568:1824], ps[:, 5, 0:256])
            nc.vector.tensor_copy(pTc[0:NC_S, :], ps[0:NC_S, 5, 256:320])
            nc.vector.tensor_copy(late[:, 1824:1888], ps[:, 5, 448:512])
            nc.vector.tensor_copy(nw[:, 1, :], ps[0:NB, 5, 384:448]).then_inc(pT_ready, 1)
            dve.wait_ge(es, 4)
            weights(3, 64, ssb[:, 0:1025], g64[:, 1:2], None)
            ch.then(nc.vector.tensor_scalar(dgn[:, 0, :], self.c(C_ID, 64, 64), ssb[:, 1024:1025], None, ALU.mult))
            marks["sp"] = ch.n
            dve.wait_ge(pT_in_psum, 2)
            nc.vector.tensor_copy(late[:, 1888:2400], ps[:, 4, :])
            nc.vector.tensor_copy(nw[:, 0, :], hid[0:NB, 256:320]).then_inc(pT_ready, 1)
            dve.wait_ge(o_in_psum, 4)
            nc.vector.tensor_copy(oa, cmp_[:, 0:256])
            nc.vector.tensor_copy(om, ps[:, 0, :]).then_inc(oT_ready, 1)
            dve.wait_ge(os_in_psum, 1)
            nc.vector.tensor_copy(self.o_s[:, 0:512], ps[0:NB, 4, :])
            nc.vector.tensor_copy(self.o_s[:, 512:768], ps[0:NB, 5, 0:256])

        @block.sync
        def _(sp):
            sp.dma_start(w2[:, :, :], I["w_cmp2"].rearrange("q p n -> p q n")).then_inc(w_in_, 16)
            sp.dma_start(pe_pos[:, :, :], I["pe"]).then_inc(w_in_, 16)
            self.load_pages(sp, 1, 1)
            with sp.Fori(1, NB // 2) as i:
                for slot in range(2):
                    sp.wait_ge(turned, i * 16 + (slot * 8 - 8))
                    sp.wait_ge(vs_ready, i * 2 + (slot - 1))
                    self.load_pages(sp, i * 2 + slot, slot)
            sp.wait_ge(turned, 8 * (NB - 1))
            sp.wait_ge(vs_ready, NB - 1)
            for c in range(2):
                sp.dma_start(raw[:, 0, c, :, 0:256], O["kv_p"][256 * c:256 * c + 256, 0:256].rearrange("(p t) c -> p t c", t=2)).then_inc(kv_in[0], 16)

        @block.gpsimd
        def _(pool):
            nc.gpsimd.memset(Q[:, :], 0.0).then_inc(zeroed, 1)
            nc.gpsimd.memset(Qm[:, :, :], 0.0).then_inc(zeroed, 1)
            nc.gpsimd.memset(w2pad[:, :, :], 0.0).then_inc(zeroed, 1)
            nc.gpsimd.memset(zb[:, :], 0.0).then_inc(zeroed, 1)
            nc.gpsimd.memset(scb[:, :], 0.0).then_inc(zeroed, 1)
            nc.gpsimd.memset(imp[:, :, :], 0.0).then_inc(zeroed, 1)

            def sort(s):
                pool.wait_ge(kv_in[s % 2], 128 * (s // 2 + 1) if s < NB else 128 * (NB // 2) + 32)
                if s >= 1:
                    pool.wait_ge(turned, first[s - 1] + 8)
                for c in range(ntile[s]):
                    ins = nc.gpsimd.tensor_copy(kvc[:, c, :, :, :], raw[:, s % 2, c, :, 0:256].rearrange("p t (a d) -> p a t d", a=4))
                ins.then_inc(kvc_ready, 1)

            sort(0)
            pool.wait_ge(gsig, 1)
            pool.dma_start(self.gate_dram, gat[:, :]).then_inc(gate_out, 16)
            pool.wait_ge(gate_out, 16)
            with nc.allow_non_contiguous_dma("192 gates"):
                for b in range(NB):
                    pool.dma_start(g64[H * b:H * b + H, :], self.gate_dram[b].rearrange("(q c) -> c q", q=3)).then_inc(gate_in, 16)
            for s in range(1, NSEQ):
                sort(s)

        @block.scalar
        def _(act):
            srcw = I["cache_win"].rearrange("(b p j) c -> b p j c", b=NB, j=4)
            srcm = I["cache_mem"].rearrange("(b p j) c -> b p j c", b=NB, j=2)

            def load(b):
                act.dma_start(winK[:, b % 2, :, :], srcw[b, :, :, 0:128]).then_inc(wk_in[b % 2], 16)
                act.dma_start(memK[:, b % 2, :, :], srcm[b, :, :, 0:256]).then_inc(mk_in[b % 2], 16)

            load(0)
            load(1)
            act.wait_ge(gclamp, 1)
            nc.scalar.activation(gat[:, :], gat[:, :], ACT.Exp, scale=-1.0).then_inc(gexp, 1)

            def out(s):
                for u in range(0, units[s], 2):
                    act.wait_ge(turned, first[s] + u + 1)
                    src, k = ps[:, 4, :], kind(s, u)
                    dst = XT[:, (k - 4) // 2, 0, :] if k >= 4 else KsT[:, 0:512] if k == 0 else KwT[:, :]
                    w = 128 * ntile[s]
                    nc.scalar.copy(dst[:, 0:w], src[:, 0:w]).then_inc(out_a, 1)
                if s < NB:
                    act.wait_ge(kv_in[s % 2], 128 * (s // 2 + 1))
                    nc.scalar.copy(Vs[:, s, :, :, :].rearrange("p c t d -> p (c t) d"),
                                   raw[:, s % 2, :, :, 384:512].rearrange("p c t d -> p (c t) d")).then_inc(vs_ready, 1)
                    act.dma_start(Vw[:, s, :, :], srcw[s, :, :, 128:256]).then_inc(v_in, 16)
                    act.dma_start(Vm[:, s, :, :], srcm[s, :, :, 256:512]).then_inc(v_in, 16)
                if s + 2 < NB:
                    act.wait_ge(turned, first[s] + 4)
                    load(s + 2)

            out(0)
            for s in range(NSEQ):
                if s + 1 < NSEQ:
                    out(s + 1)
                if s == NB:
                    act.wait_ge(steps_d, marks["mmax"])
                    nc.scalar.activation(smb[:, :], smb[:, :], ACT.Exp, bias=sst[0:32, 1, 1:2], scale=SCALE,
                                         accum_out=sst[0:32, 1, 2:3]).then_inc(es, 1)
                    act.wait_ge(steps_d, marks["wmax"])
                    nc.scalar.activation(swb[:, 1:513], swb[:, 1:513], ACT.Exp, bias=sst[:, 2, 1:2], scale=SCALE,
                                         accum_out=sst[:, 2, 2:3]).then_inc(es, 1)
                n = blocks[s]
                act.wait_ge(hx_ready, s + 1)
                v = ht[:, :].rearrange("p (q n) -> p q n", q=4)[:, :, 0:n]
                nc.scalar.activation(v, v, ACT.Exp, scale=-2.0 * 0.7978845608028654).then_inc(he_ready, 1)
            act.wait_ge(steps_d, marks["cmax"])
            nc.scalar.activation(scb[:, 0:NC_S], scb[:, 0:NC_S], ACT.Exp, bias=sst[:, 0, 1:2], scale=SCALE,
                                 accum_out=sst[:, 0, 2:3]).then_inc(es, 1)
            act.wait_ge(steps_d, marks["smax"])
            nc.scalar.activation(ssb[:, 0:1025], ssb[:, 0:1025], ACT.Exp, bias=sst[:, 3, 1:2], scale=SCALE,
                                 accum_out=sst[:, 3, 2:3]).then_inc(es, 1)

        @block.tensor
        def _(pe):
            ident = lambda n, at=0: self.consts[at:at + n, C_ID + at:C_ID + at + n]
            pe.wait_ge(zeroed, 6)
            for a in range(4):
                nc.tensor.matmul(ps[:, a, :], zb[0:1, 0:128], zb[0:1, :], start=True, stop=False, skip_group_check=True)
            def turn(s):
                k, w, m = kvc[:, :, :, :, :], winK[:, s % 2, :, :], memK[:, s % 2, :, :]
                for u in range(units[s]):
                    n, a = first[s] + u, kind(s, u)
                    if a == 0:
                        pe.wait_ge(kv_in[s % 2], 128 * (s // 2 + 1))
                    if a == 2:
                        pe.wait_ge(wk_in[s % 2], 16 * (s // 2 + 1))
                    if a == 3:
                        pe.wait_ge(mk_in[s % 2], 16 * (s // 2 + 1))
                    if a == 4:
                        pe.wait_ge(kvc_ready, s + 1)
                    if n >= 2:
                        pe.wait_ge(out_d if n % 2 else out_a, n // 2)
                    dst = ps[:, 4 + n % 2, :]
                    for c in range(ntile[s]):
                        if a < 2:
                            src = raw[:, s % 2, 2 * a + c // 2, c % 2, 256:384]
                        elif a == 2:
                            src = w[:, c, :]
                        elif a == 3:
                            src = m[:, c % 2, 128 * (c // 2):128 * (c // 2) + 128]
                        else:
                            src = k[:, c, a - 4, :, :].rearrange("p t d -> p (t d)")
                        ins = nc.tensor.transpose(dst[:, 128 * c:128 * c + 128], src, ident(P))
                    ins.then_inc(turned, 1)

            def small():
                for r in range(R):
                    nc.tensor.transpose(cmp_[:, 8 * r:8 * r + 8], z[0:NB, smp, Q0 + 128 * r:Q0 + 128 * r + 128], ident(NB))
                for j in range(2):
                    nc.tensor.transpose(cmp_[:, 32 + 8 * j:40 + 8 * j], z[0:NB, smp, M0 + 128 * j:M0 + 128 * j + 128], ident(NB))
                for j in range(2):
                    ins = nc.tensor.transpose(cmp_[:, 48 + 8 * j:56 + 8 * j], z[0:NB, smp, K0 + 128 * (j + 1):K0 + 128 * (j + 2)], ident(NB))
                pe.wait_ge(self.w1_in, 16)
                pe.wait_ge(w_in_, 32)
                for q in range(2):
                    for l in range(16):
                        ins = nc.tensor.matmul(hid[:, q:q + 1], w1[:, q, l, :], pe_pos[:, q, l:l + 1], start=(l == 0), stop=(l == 15))
                ins.then_inc(small_in_psum, 1)

            def compress(s):
                n = blocks[s]
                pe.wait_ge(out_a, (first[s] + units[s]) // 2)
                pe.wait_ge(out_d, (first[s] + units[s]) // 2)
                if s == 0:
                    pe.wait_ge(q_ready, 1)
                else:
                    pe.wait_ge(hx_ready, s)
                for q in range(2):
                    for l in range(16):
                        ins = nc.tensor.matmul(hidv[:, 2 * q:2 * q + 2, 0:n], w1[:, q, l, :],
                                               XT[:, q, :, l:l + 8 * (n - 1) + 1:8], start=(l == 0), stop=(l == 15))
                ins.then_inc(hid_in_psum, 1)

            def score(s):
                if s == NB:
                    return
                if s == 0:
                    pe.wait_ge(q_ready, 1)
                pe.wait_ge(out_a, first[s] // 2 + 2)
                pe.wait_ge(out_d, first[s] // 2 + 2)
                add = dict(start=False, stop=False, skip_group_check=True)
                q = Q[:, 64 * s:64 * s + 64]
                nc.tensor.matmul(sel0[0:64, 0, :], q, KsT[:, 0:512], **add)
                nc.tensor.matmul(win0[64:128, :], q, KwT[:, :], **add)
                nc.tensor.matmul(sel0[0:64, 1, :], q, KsT[:, 512:1024], **add)
                for a in range(2):
                    nc.tensor.matmul(misc[64:96, 128:384], Qm[:, a, 32 * s:32 * s + 32], KmT[:, a, :], **add)
                for a in range(2):
                    nc.tensor.matmul(misc[0:64, 64 + a:65 + a], q, kTn[:, a, s:s + 1], **add)

            def project_blocks(s):
                n = blocks[s]
                pe.wait_ge(gel_ready, s + 1)
                if s >= 1:
                    pe.wait_ge(cmp_ready, s)
                gk = gel[:, s % 2, :].rearrange("p (q n) -> p q n", q=4)
                for g in range(G):
                    nc.tensor.matmul(cmp_[:, 0:n], w2pad[:, g, :], gk[:, g, 0:n], start=(g == 0), stop=(g == 1))
                for g in range(G):
                    ins = nc.tensor.matmul(cmp_[0:n, 128 + 64 * g:192 + 64 * g], gk[:, 2 + g, 0:n], w2[:, 1, :], start=True, stop=True)
                ins.then_inc(cmp_in_psum, 1)

            for s in range(NSEQ):
                turn(s)
                if s == 0:
                    small()
                score(s)
                compress(s)
                if s >= 1:
                    project_blocks(s - 1)
            project_blocks(NSEQ - 1)
            pe.wait_ge(cmp_ready, NSEQ)
            for b in range(NB):
                ins = nc.tensor.matmul(misc[0:64, 0:NC_S], Q[:, 64 * b:64 * b + 64], kcT[:, b, 0:NC_S], start=False, stop=False, skip_group_check=True)
            ins.then_inc(cs_in_psum, 1)
            pe.wait_ge(steps_d, marks["pc"])
            nc.tensor.matmul(hid[0:64, 0:64], self.c(C_RG, 64, 64), scb[:, :], start=True, stop=True).then_inc(imp_in_psum, 1)
            pe.wait_ge(steps_d, marks["wp"])
            for j in range(2):
                nc.tensor.transpose(ps[:, 5, 448 + 32 * j:480 + 32 * j], smb[:, 128 * j:128 * j + 128], ident(32))
            for j in range(4):
                nc.tensor.transpose(ps[:, 5, 64 * j:64 * j + 64], swb[:, 128 * j:128 * j + 128], ident(64))
            nc.tensor.matmul(ps[0:NB, 5, 384:448], self.c(C_S8, NB, 64), dgn[:, 1, :], start=True, stop=True)
            pe.wait_ge(steps_d, marks["cg"])
            nc.tensor.transpose(ps[0:NC_S, 5, 256:320], scb[:, 0:NC_S], ident(64)).then_inc(pT_in_psum, 1)
            nc.tensor.matmul(cmp_, zb[0:1, 0:128], zb[0:1, :], start=True, stop=False, skip_group_check=True)
            add = dict(start=False, stop=False, skip_group_check=True)
            at = lambda b, n: slice(32 * (b % 4), 32 * (b % 4) + n)
            heads = lambda b: slice(8 * b, 8 * b + 8)
            o = lambda b: cmp_[at(b, 8), 128 * (b // 4):128 * (b // 4) + 128]
            pe.wait_ge(v_in, 16 * 2 * NB)
            pe.wait_ge(vs_ready, NB)
            pe.wait_ge(pT_ready, 1)
            nc.tensor.matmul(ps[:, 0, :], zb[0:1, 0:128], zb[0:1, :], start=True, stop=False, skip_group_check=True)
            for b in range(NB):
                nc.tensor.matmul(o(b), nw[:, 1, heads(b)], z[0:NB, smp, V0 + 256:V0 + 384], **add)
            for j in range(4):
                for b in range(NB):
                    nc.tensor.matmul(o(b), pTw[:, j, heads(b)], Vw[:, b, j, :], **add)
            for b in range(NB):
                nc.tensor.matmul(o(b), pTc[0:NC_S, heads(b)], vc[0:NC_S, b, :], **add)
            for j in range(2):
                for b in range(NB):
                    nc.tensor.matmul(ps[at(b, 4), 0, 256 * (b // 4):256 * (b // 4) + 256], pTm[:, j, 4 * b:4 * b + 4], Vm[:, b, j, :], **add)
            pe.wait_ge(steps_d, marks["sp"])
            for j in range(8):
                nc.tensor.transpose(ps[:, 4, 64 * j:64 * j + 64], ssb[:, 128 * j:128 * j + 128], ident(64))
            nc.tensor.matmul(hid[0:NB, 256:320], self.c(C_S8, NB, 64), dgn[:, 0, :], start=True, stop=True).then_inc(pT_in_psum, 1)
            pe.wait_ge(pT_ready, 2)
            for b in range(NB):
                nc.tensor.matmul(o(b), nw[:, 0, heads(b)], z[0:NB, smp, V0 + 128:V0 + 256], **add)
            for j in range(8):
                for b in range(NB):
                    ins = nc.tensor.matmul(o(b), pTs[:, j, heads(b)], Vs[:, b, j // 2, j % 2, :], **add)
                    if j == 7 and b >= NB - 4:
                        ins.then_inc(o_in_psum, 1)
            pe.wait_ge(oT_ready, 1)
            for n, (src, bank, wide) in enumerate(((oa, 4, 128), (om, 5, 256))):
                for c in range(H if n == 0 else MH):
                    for u in range(2):
                        v = src[:, wide * u + (64 * (c % 2) if n == 0 else 64 * c):][:, 0:64]
                        ins = nc.tensor.matmul(ps[0:NB, bank, 64 * c:64 * c + 64], self.c(C_SEL + NB * (8 * u + c), NB), v, start=(u == 0), stop=(u == 1))
            ins.then_inc(os_in_psum, 1)

        self.close(st)

    def alloc_mix(self, stack):
        sb = lambda *a: self.sb(*a, stack=stack)
        self.mix_in = (
            sb("bands", [P, BW]), sb("state", [P, 256]), sb("w_pool", [64, 4, 64]), sb("w_out", [P, KD, D]),
            sb("rows_g", [P, 2 * D + 256 + 36]),
            sb("w_router", [P, KD, 36]), sb("xin4", [P, 2, D]))
        self.mix_consts_in, self.wout_in = self.sem("mix_consts_in", self.stack), self.sem("wout_in", self.stack)
        self.x4_in = [self.sem(f"x4_in{j}", self.stack) for j in range(2)]

    def load_mix(self, sp):
        I, consts_in, wout_in, x_in = self.ins, self.mix_consts_in, self.wout_in, self.x4_in
        bands, state, w_pool, w_out, rows_g, w_router, xin = self.mix_in
        sp.dma_start(bands[:, :], I["bands"]).then_inc(consts_in, 16)
        sp.dma_start(state[0:NB * STATE, :], I["state_pool"]).then_inc(consts_in, 16)
        sp.dma_start(w_pool[:, :, :], I["w_pool"].rearrange("(w c) d -> c w d", w=4)).then_inc(consts_in, 16)
        sp.dma_start(rows_g[:, :], I["mix_rows"].partition_broadcast(P)).then_inc(consts_in, 16)
        for t in range(2):
            sp.dma_start(xin[0:ROWS[t], t, :], I["x"][t * P:t * P + ROWS[t], :]).then_inc(x_in[t], 16)
        for j in range(2):
            sp.dma_start(w_out[:, 4 * j:4 * j + 4, :], I["w_out"].rearrange("(p k) n -> p k n", k=KD)[:, 4 * j:4 * j + 4, :]).then_inc(wout_in, 16)
        sp.dma_start(w_router[:, :, :], I["w_router"].rearrange("(p k) n -> p k n", k=KD)).then_inc(wout_in, 16)

    def attend(self):
        nc, I, O = self.nc, self.ins, self.outs
        st = ExitStack()
        S = lambda n: self.sem(n, st)
        ps, z, o = self.ps, self.z, self.o
        qT = self.sb("qT", [P, R, T], stack=st)
        kT = self.sb("kT", [P, 2, T], stack=st)
        qmT = self.sb("qmT", [P, 2, T], stack=st)
        mz = self.sb("mz", [P, 2, 512], stack=st)
        mkT = self.sb("mkT", [P, 2, MEM], stack=st)
        gate = self.sb("gate", [P, TILES, 24], stack=st)
        prob = self.sb("prob", [P, 2, 2, 512], stack=st)
        pT = self.sb("pT", [P, 2, 512], stack=st)
        stt = self.sb("stt", [P, 2, 4, 8], stack=st)
        zb = self.sb("zb2", [1, 512], BF16, stack=st)
        mz_in, gclamp, gexp, steps, zeroed, turned, out_a, out_d = (S(n) for n in (
            "mz_in", "gate_clamped", "gate_exp", "attend_dve", "zb_zeroed", "qk_turned", "qk_out_a", "qk_out_d"))
        scores, peaks, exps, probs, p_turned, pT_a, pT_d, pv, o_in_psum, o_out = (S(n) for n in (
            "scores", "peaks", "exps", "probs", "p_turned", "pT_a", "pT_d", "pv", "o_in_psum", "o_out"))

        pre = []
        for r in range(R):
            pre.append(([z[:, t, Q0 + 128 * r:Q0 + 128 * r + 128] for t in range(TILES)], qT[:, r, :]))
        for a in range(2):
            pre.append(([z[:, t, K0 + 128 * (a + 1):K0 + 128 * (a + 2)] for t in range(TILES)], kT[:, a, :]))
        for a in range(2):
            pre.append(([z[:, t, M0 + 128 * a:M0 + 128 * a + 128] for t in range(TILES)], qmT[:, a, :]))
        pre.append(([mz[:, j, 128 * a:128 * a + 128] for a in range(2) for j in range(2)], mkT[:, :, :].rearrange("p a n -> p (a n)")))
        fit = [4, 2, 1, 1]
        units = [(t, kind, rs) for t in range(TILES)
                 for kind, rs in [("cmp", range(R)), ("mem", range(R))] + [(br, range(r, r + fit[t])) for br in ("sel", "win") for r in range(0, R, fit[t])]]
        NU = len(units)
        opens = lambda u: u == 0 or units[u][0] != units[u - 1][0]
        ends = lambda u: u == NU - 1 or opens(u + 1)

        block = st.enter_context(nc.Block("attend"))

        @block.sync
        def _(sp):
            for j in range(2):
                sp.dma_start(mz[:, j, :], O["mem_p"][j * P:(j + 1) * P, :]).then_inc(mz_in, 16)
            self.load_mix(sp)

        @block.gpsimd
        def _(pool):
            nc.gpsimd.memset(zb[:, :], 0.0).then_inc(zeroed, 1)

        @block.tensor
        def _(pe):
            ident = self.consts[:, C_ID:C_ID + P]
            pe.wait_ge(zeroed, 1)
            for n, (srcs, _) in enumerate(pre):
                if n == len(pre) - 1:
                    pe.wait_ge(mz_in, 32)
                if n >= 2:
                    pe.wait_ge(out_d if n % 2 else out_a, n // 2)
                for c, src in enumerate(srcs):
                    ins = nc.tensor.transpose(ps[:, 4 + n % 2, 128 * c:128 * c + 128], src, ident)
                ins.then_inc(turned, 1)

            def score(u):
                t, kind, rs = units[u]
                q = slice(t * P, (t + 1) * P)
                if u >= 2:
                    pe.wait_ge(exps, u - 1)
                b = 2 * (u % 2)
                last = {}
                if kind == "cmp":
                    for r in range(R):
                        for g in range(G):
                            hs = slice(64 * g, 64 * g + 64)
                            ins = nc.tensor.matmul(ps[:, b + g, 32 * r:32 * r + NC_P], qT[hs, r, q], self.kcT[hs, NB, 0:NC_P], start=True, stop=True)
                            last[g] = ins
                elif kind == "mem":
                    for h in range(MH):
                        hs = slice(64 * (h % 2), 64 * (h % 2) + 64)
                        hp = h // 2
                        ins = nc.tensor.matmul(ps[:, b + h % 2, MEM * hp:MEM * hp + MEM], qmT[hs, hp, q], mkT[hs, hp, :], start=True, stop=True)
                        last[h % 2] = ins
                else:
                    w = (t + 1) * P
                    for i, r in enumerate(rs):
                        for g in range(G):
                            hs = slice(64 * g, 64 * g + 64)
                            ins = nc.tensor.matmul(ps[:, b + g, w * i:w * i + w], qT[hs, r, q], kT[hs, int(kind == "win"), 0:w], start=True, stop=True)
                            last[g] = ins
                last[0].then_inc(scores, 1)
                ins.then_inc(scores, 1)

            def turn(u):
                t, kind, rs = units[u]
                pe.wait_ge(probs, u + 1)
                if u >= 1:
                    pe.wait_ge(pT_a, u)
                    pe.wait_ge(pT_d, u)
                p = prob[:, u % 2, :, :]
                for j in range(2):
                    for c in range(len(rs) * (t + 1) if kind in ("sel", "win") else 4):
                        if kind == "cmp":
                            ins = nc.tensor.transpose(ps[0:NC_P, 4 + j, 128 * c:128 * c + 128], p[:, j, 32 * c:32 * c + NC_P], ident)
                        else:
                            ins = nc.tensor.transpose(ps[:, 4 + j, 128 * c:128 * c + 128], p[:, j, 128 * c:128 * c + 128], ident)
                ins.then_inc(p_turned, 1)

            def value(u):
                t, kind, rs = units[u]
                add = dict(start=False, stop=False, skip_group_check=True)
                if opens(u):
                    if t >= 1:
                        pe.wait_ge(o_out, t)
                    for a in range(2):
                        nc.tensor.matmul(ps[:, 6 + a, :], zb[0:1, 0:P], zb[0:1, :], start=True, stop=False, skip_group_check=True)
                pe.wait_ge(pT_a, u + 1)
                pe.wait_ge(pT_d, u + 1)
                for j in range(2):
                    if kind == "cmp":
                        for r in range(R):
                            c = 2 * r + j
                            ins = nc.tensor.matmul(ps[:, 6, 64 * c:64 * c + 64], pT[0:NC_P, j, 128 * r:128 * r + 128], self.vc[0:NC_P, NB, 64 * j:64 * j + 64], **add)
                    elif kind == "mem":
                        for hp in range(2):
                            h = 2 * hp + j
                            for k in range(2):
                                ins = nc.tensor.matmul(ps[:, 7, 64 * h:64 * h + 64], pT[:, j, 128 * (2 * hp + k):128 * (2 * hp + k) + 128],
                                                       mz[:, k, 256 + 64 * h:320 + 64 * h], **add)
                    else:
                        v = V0 + 128 * (1 if kind == "sel" else 2) + 64 * j
                        for i, r in enumerate(rs):
                            c = 2 * r + j
                            for k in range(t + 1):
                                at = 128 * ((t + 1) * i + k)
                                ins = nc.tensor.matmul(ps[:, 6, 64 * c:64 * c + 64], pT[:, j, at:at + 128], z[:, k, v:v + 64], **add)
                if ends(u):
                    ins.then_inc(o_in_psum, 1)

            pe.wait_ge(out_a, (len(pre) + 1) // 2)
            pe.wait_ge(out_d, len(pre) // 2)
            score(0)
            score(1)
            for u in range(NU):
                if u + 2 < NU:
                    score(u + 2)
                if u >= 1:
                    value(u - 1)
                turn(u)
            value(NU - 1)

        def shape(u):
            t, kind, rs = units[u]
            return {"cmp": (4, NC_P, 32), "mem": (2, MEM, MEM)}.get(kind, (len(rs), (t + 1) * P, (t + 1) * P))

        def view(a, u):
            n, w, s = shape(u)
            return a[:, :, 0:n * s].rearrange("p j (n s) -> p j n s", n=n)[:, :, :, 0:w]

        @block.vector
        def _(dve):
            ch = Chain(dve, steps)
            nc.vector.tensor_scalar(gate[:, :, :], z[:, 0:TILES, G0:G0 + 24], -80.0, None, ALU.max).then_inc(gclamp, 1)
            dve.wait_ge(gexp, 1)
            ch.then(nc.vector.tensor_scalar(gate[:, :, :], gate[:, :, :], 1.0, None, ALU.add))
            ch.then(nc.vector.reciprocal(gate[:, :, :], gate[:, :, :]))
            for n in range(1, len(pre), 2):
                dve.wait_ge(turned, n + 1)
                nc.vector.tensor_copy(pre[n][1], ps[:, 5, :]).then_inc(out_d, 1)

            def peak(u):
                t, kind = units[u][0:2]
                n, w, s = shape(u)
                b = 2 * (u % 2)
                dve.wait_ge(scores, 2 * u + 2)
                sc = view(ps[:, b:b + 2, :], u)
                st_ = stt[:, u % 2, 0:2, :]
                if kind == "cmp":
                    mask = self.c(C_CADD + 32 * t, NC_P).unsqueeze(1).broadcast_to([P, R, NC_P])
                    for j in range(2):
                        ins = nc.vector.tensor_tensor(sc[:, j, :, :], sc[:, j, :, :], mask, ALU.add)
                    ch.then(ins)
                elif kind != "mem":
                    d = sc[:, :, :, t * P:(t + 1) * P]
                    ch.then(nc.vector.tensor_tensor(d, d, self.c(C_CAUS, P).unsqueeze(1).unsqueeze(1).broadcast_to([P, 2, n, P]), ALU.add))
                top = stt[:, u % 2, 0, 0:2 * n]
                ch.then(nc.vector.tensor_reduce(top.rearrange("p (j n) -> p j n", j=2), sc, AX.X, ALU.max))
                if kind == "cmp":
                    pr = view(prob[:, u % 2, :, :], u)
                    if u >= 2:
                        dve.wait_ge(p_turned, u - 1)
                    for j in range(2):
                        ins = nc.vector.tensor_tensor(pr[:, j, :, :], sc[:, j, :, :], top[:, 4 * j:4 * j + 4].unsqueeze(2).broadcast_to([P, 4, NC_P]), ALU.subtract)
                    ins.then_inc(peaks, 1)
                else:
                    nc.vector.tensor_scalar(stt[:, u % 2, 1, 0:2 * n], top, -SCALE, None, ALU.mult).then_inc(peaks, 1)

            def weigh(u):
                t, kind, rs = units[u]
                n, w, s = shape(u)
                dve.wait_ge(exps, u + 1)
                pr = view(prob[:, u % 2, :, :], u)
                total, f = stt[:, u % 2, 2, 0:2 * n], stt[:, u % 2, 3, 0:2 * n]
                if kind == "cmp":
                    mask = self.c(C_CMUL + 32 * t, NC_P).unsqueeze(1).broadcast_to([P, R, NC_P])
                    for j in range(2):
                        ins = nc.vector.tensor_tensor(pr[:, j, :, :], pr[:, j, :, :], mask, ALU.mult)
                    ch.then(ins)
                    ch.then(nc.vector.tensor_reduce(total.rearrange("p (j n) -> p j n", j=2), pr, AX.X, ALU.add))
                    ch.then(nc.vector.tensor_scalar(total, total, 1e-30, None, ALU.max))
                ch.then(nc.vector.reciprocal(f, total))
                if kind == "cmp":
                    ch.then(nc.vector.tensor_tensor(f.rearrange("p (j r) -> p j r", j=2), f.rearrange("p (j r) -> p j r", j=2),
                                                    gate[:, t, 0:8].rearrange("p (r j) -> p j r", j=2), ALU.mult))
                    for j in range(2):
                        ins = nc.vector.tensor_tensor(pr[:, j, :, :], pr[:, j, :, :], f[:, 4 * j:4 * j + 4].unsqueeze(2).broadcast_to([P, 4, NC_P]), ALU.mult)
                elif kind == "mem":
                    for i in range(4):
                        ins = nc.vector.tensor_scalar(pr[:, i // 2, i % 2, :], pr[:, i // 2, i % 2, :], f[:, i:i + 1], None, ALU.mult)
                else:
                    c = 8 * (1 if kind == "sel" else 2) + 2 * rs[0]
                    if n == 1:
                        for j in range(2):
                            ins = nc.vector.tensor_scalar(pr[:, j, 0, :], pr[:, j, 0, :], f[:, j:j + 1], gate[:, t, c + j:c + j + 1], ALU.mult, ALU.mult)
                    else:
                        fj = f.rearrange("p (j n) -> p j n", j=2)
                        ch.then(nc.vector.tensor_tensor(fj, fj, gate[:, t, c:c + 2 * n].rearrange("p (n j) -> p j n", j=2), ALU.mult))
                        ins = nc.vector.tensor_tensor(pr, pr, fj.unsqueeze(3).broadcast_to([P, 2, n, w]), ALU.mult)
                ins.then_inc(probs, 1)

            peak(0)
            peak(1)
            for u in range(NU):
                t, kind = units[u][0:2]
                weigh(u)
                if u + 2 < NU:
                    peak(u + 2)
                dve.wait_ge(p_turned, u + 1)
                rows = NC_P if kind == "cmp" else P
                w = 512 if kind in ("cmp", "mem") else len(units[u][2]) * (t + 1) * P
                nc.vector.tensor_copy(pT[0:rows, 1, 0:w], ps[0:rows, 5, 0:w]).then_inc(pT_d, 1)

        @block.scalar
        def _(act):
            act.wait_ge(gclamp, 1)
            nc.scalar.activation(gate[:, :, :], gate[:, :, :], ACT.Exp, scale=-1.0).then_inc(gexp, 1)
            for n in range(0, len(pre), 2):
                act.wait_ge(turned, n + 1)
                nc.scalar.copy(pre[n][1], ps[:, 4, :]).then_inc(out_a, 1)

            def exp(u):
                t, kind = units[u][0:2]
                b = 2 * (u % 2)
                act.wait_ge(peaks, u + 1)
                if u >= 2:
                    act.wait_ge(p_turned, u - 1)
                pr, sc = view(prob[:, u % 2, :, :], u), view(ps[:, b:b + 2, :], u)
                if kind == "cmp":
                    for j in range(2):
                        ins = nc.scalar.activation(pr[:, j, :, :], pr[:, j, :, :], ACT.Exp, scale=SCALE)
                else:
                    n = shape(u)[0]
                    for i in range(2 * n):
                        ins = nc.scalar.activation(pr[:, i // n, i % n, :], sc[:, i // n, i % n, :], ACT.Exp, bias=stt[:, u % 2, 1, i:i + 1],
                                                   scale=SCALE, accum_out=stt[:, u % 2, 2, i:i + 1])
                ins.then_inc(exps, 1)

            exp(0)
            exp(1)
            for u in range(NU):
                t, kind = units[u][0:2]
                act.wait_ge(p_turned, u + 1)
                rows = NC_P if kind == "cmp" else P
                w = 512 if kind in ("cmp", "mem") else len(units[u][2]) * (t + 1) * P
                nc.scalar.copy(pT[0:rows, 0, 0:w], ps[0:rows, 4, 0:w]).then_inc(pT_a, 1)
                if u + 2 < NU:
                    exp(u + 2)
                if u >= 1 and opens(u):
                    act.wait_ge(o_in_psum, t)
                    nc.scalar.copy(o[:, t - 1, 0:512], ps[:, 6, :])
                    nc.scalar.copy(o[:, t - 1, 512:768], ps[:, 7, 0:256]).then_inc(o_out, 1)
            act.wait_ge(o_in_psum, TILES)
            nc.scalar.copy(o[:, TILES - 1, 0:512], ps[:, 6, :])
            nc.scalar.copy(o[:, TILES - 1, 512:768], ps[:, 7, 0:256]).then_inc(o_out, 1)

        self.close(st)

    def mix(self):
        nc, I, O = self.nc, self.ins, self.outs
        st = ExitStack()
        S = lambda n: self.sem(n, st)
        ps, z, o = self.ps, self.z, self.o
        NT = TILES + 1
        bands, state, w_pool, w_out, rows_g, w_router, xin = self.mix_in
        consts_in, wout_in, x_in = self.mix_consts_in, self.wout_in, self.x4_in
        rT = self.sb("rT", [64, 4, P], stack=st)
        mixed = self.sb("mixed", [P, 2, D], stack=st)
        mT = self.sb("mT", [P, KD, P], stack=st)
        h = xin
        hn = self.sb("hn", [P, 2, D], stack=st)
        hT = self.sb("hT", [P, KD, P], stack=st)
        junk = self.sb("junk4", [P, 512], stack=st)
        sq = self.sb("sq", [P, 2, 8], stack=st)
        lg = self.sb("lg", [P, NT, 36], stack=st)
        ro = self.sb("ro", [P, NT, 72], stack=st)
        one = self.sb("one", [P, NT, 2, NEXP], stack=st)
        both = self.sb("both", [P, NT, NEXP], stack=st)
        cnt = self.sb("cnt", [P, NT + 1, NEXP], stack=st)
        scan = self.sb("scan", [P, 3, NEXP], stack=st)
        prod = self.sb("prod", [P, NT, 2, NEXP], stack=st)
        place = self.sb("place", [P, 6, NT * 2], stack=st)
        last = self.sb("last", [1, NOVER, NEXP], stack=st)
        stored = [S(f"h_stored{j}") for j in range(2)]
        names = ("mix_dve", "cleared", "r_in_psum", "r_ready", "y_in_psum", "y_out", "ms_ready4", "root_ready", "mixed_ready",
                 "mT_in_psum", "mT_ready", "h_in_psum", "hms", "hroot", "hn_ready", "hT_in_psum", "hT_ready", "l_in_psum",
                 "l_out", "lclear", "lexp", "pair_ready", "cnt_in_psum", "h_read", "h_copied", "hot_ready", "table_in_psum")
        (steps, cleared, r_in_psum, r_ready, y_in_psum, y_out, ms_ready, root_ready, mixed_ready,
         mT_in_psum, mT_ready, h_in_psum, hms, hroot, hn_ready, hT_in_psum, hT_ready, l_in_psum,
         l_out, lclear, lexp, pair_ready, cnt_in_psum, h_read, h_copied, hot_ready, table_in_psum) = (S(n) for n in names)
        gm, gf, sp_, br = rows_g[:, 0:D], rows_g[:, D:2 * D], rows_g[:, 2 * D:2 * D + 256], rows_g[:, 2 * D + 256:]

        slot_hot = mixed[:, 1, 0:2 * NT * CAP].rearrange("p (n s) -> p n s", s=CAP)
        tile_tok = mixed[:, 0, 0:2 * NT * NTILE].rearrange("p (n s) -> p n s", s=NTILE)

        block = st.enter_context(nc.Block("mix"))

        @block.sync
        def _(sp):
            wg, wu, wd = self.expert_slot(self.w0)
            self.load_gate_up(sp, 0, 0, (wg, wu))
            self.load_down(sp, 0, 0, wd)
            for t in range(NT):
                r = ROWS[t]
                sp.wait_ge(hn_ready, t + 1)
                sp.dma_start(self.hn_dram[t * P:t * P + r, :], hn[0:r, t % 2, :]).then_inc(stored[t % 2], 16)
                sp.dma_start(self.h_dram[t * P:t * P + r, :], h[0:r, t % 2, :]).then_inc(stored[t % 2], 16)
                if t + 2 < NT:
                    sp.wait_ge(stored[t % 2], 32 * (t // 2 + 1))
                    sp.dma_start(xin[0:ROWS[t + 2], t % 2, :], I["x"][(t + 2) * P:(t + 2) * P + ROWS[t + 2], :]).then_inc(x_in[t % 2], 16)
            sp.wait_ge(stored[0], 32 * ((NT + 1) // 2))
            sp.wait_ge(stored[1], 32 * (NT // 2))

        @block.gpsimd
        def _(pool):
            nc.gpsimd.memset(one[:, :, :, :], 0.0).then_inc(cleared, 1)
            nc.gpsimd.memset(cnt[:, :, :], 0.0).then_inc(cleared, 1)
            nc.gpsimd.memset(self.pair_w[:, :, :], 0.0).then_inc(cleared, 1)
            nc.gpsimd.memset(lg[:, :, :], 0.0).then_inc(cleared, 1)

        @block.tensor
        def _(pe):
            ident = lambda n: self.consts[0:n, C_ID:C_ID + n]
            pe.wait_ge(consts_in, 64)

            def windows(t):
                r = ROWS[t]
                if t >= 1:
                    pe.wait_ge(r_ready, t)
                band = lambda w, j: bands[:, C_BAND + (3 * w + j) * P:C_BAND + (3 * w + j + 1) * P]
                for w in range(4):
                    u = z[0:r, t, U0 + 64 * w:U0 + 64 * w + 64]
                    out = ps[0:64, 0, 128 * w:128 * w + r]
                    if t == 0:
                        ins = nc.tensor.matmul(out, u, band(w, 2), start=True, stop=True)
                    elif t < TILES:
                        nc.tensor.matmul(out, u, band(w, 0), start=True, stop=False)
                        ins = nc.tensor.matmul(out, z[:, t - 1, U0 + 64 * w:U0 + 64 * w + 64], band(w, 1), start=False, stop=True)
                    else:
                        n = NB * STATE
                        nc.tensor.matmul(out, state[0:n, 64 * w:64 * w + 64], bands[0:n, C_PST + NB * w:C_PST + NB * w + NB], start=True, stop=False)
                        ins = nc.tensor.matmul(out, z[0:NB, t, U0 + 64 * w:U0 + 64 * w + 64], bands[0:NB, C_PDG + NB * w:C_PDG + NB * w + NB], start=False, stop=True)
                ins.then_inc(r_in_psum, 1)

            def pool_proj(t):
                r = ROWS[t]
                pe.wait_ge(r_ready, t + 1)
                if t >= 1:
                    pe.wait_ge(y_out, t)
                for w in range(4):
                    ins = nc.tensor.matmul(ps[0:r, 1, 64 * w:64 * w + 64], rT[:, w, 0:r], w_pool[:, w, :], start=True, stop=True)
                ins.then_inc(y_in_psum, 1)

            def turn_mixed(t):
                r = ROWS[t]
                pe.wait_ge(mixed_ready, t + 1)
                if t >= 1:
                    pe.wait_ge(mT_ready, t)
                for k in range(KD):
                    ins = nc.tensor.transpose(ps[:, 2 + k // 4, 128 * (k % 4):128 * (k % 4) + r], mixed[0:r, t % 2, k:D:KD], ident(r))
                ins.then_inc(mT_in_psum, 1)

            def out_proj(t):
                r = ROWS[t]
                pe.wait_ge(mT_ready, t + 1)
                if t == 0:
                    pe.wait_ge(wout_in, 48)
                else:
                    pe.wait_ge(h_read, t)
                if t < TILES:
                    for a in range(2):
                        for k in range(KD):
                            ins = nc.tensor.matmul(ps[0:r, 4 + a, :], mT[:, k, 0:r], w_out[:, k, 512 * a:512 * a + 512], start=(k == 0), stop=(k == KD - 1))
                    ins.then_inc(h_in_psum, 1)
                else:
                    for k in range(KD):
                        for a in range(4):
                            ins = nc.tensor.matmul(ps[32 * a:32 * a + r, 4, 0:256], mT[:, k, 0:r], w_out[:, k, 256 * a:256 * a + 256], start=(k == 0), stop=(k == KD - 1))
                            if k == KD - 1:
                                ins.then_inc(h_in_psum, 1)

            def turn_hn(t):
                r = ROWS[t]
                pe.wait_ge(hn_ready, t + 1)
                for k in range(KD):
                    ins = nc.tensor.transpose(ps[:, k // 4, 128 * (k % 4):128 * (k % 4) + r], hn[0:r, t % 2, k:D:KD], ident(r))
                ins.then_inc(hT_in_psum, 1)

            def router(t):
                r = ROWS[t]
                pe.wait_ge(hT_ready, t + 1)
                if t >= 1:
                    pe.wait_ge(l_out, t)
                for k in range(KD):
                    ins = nc.tensor.matmul(ps[0:r, 6, 0:36], hT[:, k, 0:r], w_router[:, k, :], start=(k == 0), stop=(k == KD - 1))
                ins.then_inc(l_in_psum, 1)

            windows(0)
            for t in range(NT):
                pool_proj(t)
                if t + 1 < NT:
                    windows(t + 1)
                if t == 1:
                    turn_mixed(0)
            for t in range(NT):
                out_proj(t)
                if t + 1 < NT:
                    turn_mixed(t + 1)
                if t >= 2:
                    router(t - 2)
                if t == 1:
                    pe.wait_ge(y_out, NT)
                if t >= 1:
                    turn_hn(t - 1)
            router(NT - 2)
            turn_hn(NT - 1)
            router(NT - 1)
            pe.wait_ge(pair_ready, 1)
            for t in range(NT + 1):
                r = ROWS[t] if t < NT else P
                out = ps[0:r, 7, NEXP * t:NEXP * t + NEXP]
                for s in range(min(t, NT)):
                    ins = nc.tensor.matmul(out, self.c(C_ONE, r, ROWS[s]), both[0:ROWS[s], s, :], start=(s == 0), stop=(t == NT and s == NT - 1))
                if t < NT:
                    ins = nc.tensor.matmul(out, self.c(C_UP, r, r), both[0:r, t, :], start=(t == 0), stop=True)
            ins.then_inc(cnt_in_psum, 1)
            pe.wait_ge(hot_ready, 1)
            for t in range(NT):
                for k in range(2):
                    r, n = ROWS[t], 2 * t + k
                    ins = nc.tensor.matmul(ps[0:CAP, 0, 0:NTILE], slot_hot[0:r, n, :], tile_tok[0:r, n, :], start=(n == 0), stop=(n == 2 * NT - 1))
            ins.then_inc(table_in_psum, 1)

        @block.scalar
        def _(act):
            def mixed_T(t):
                r = ROWS[t]
                act.wait_ge(mT_in_psum, t + 1)
                nc.scalar.copy(mT[:, :, 0:r], ps[:, 2:4, :].rearrange("p a (k t) -> p (a k) t", t=P)[:, :, 0:r]).then_inc(mT_ready, 1)

            def root(t):
                act.wait_ge(ms_ready, t + 1)
                nc.scalar.activation(sq[0:ROWS[t], 0, 3:6], sq[0:ROWS[t], 0, 0:3], ACT.Sqrt).then_inc(root_ready, 1)

            def route(t):
                r = ROWS[t]
                act.wait_ge(hT_in_psum, t + 1)
                nc.scalar.copy(hT[:, :, 0:r], ps[:, 0:2, :].rearrange("p a (k t) -> p (a k) t", t=P)[:, :, 0:r]).then_inc(hT_ready, 1)

            root(0)
            mixed_T(0)
            root(1)
            for t in range(NT):
                r = ROWS[t]
                if t + 1 < NT:
                    mixed_T(t + 1)
                if t == TILES:
                    act.wait_ge(h_in_psum, TILES + 4)
                    for a in range(4):
                        ins = nc.scalar.copy(mixed[0:r, t % 2, 256 * a:256 * a + 256], ps[32 * a:32 * a + r, 4, 0:256])
                    ins.then_inc(h_copied, 1)
                act.wait_ge(hms, t + 1)
                nc.scalar.activation(sq[0:r, 1, 1:2], sq[0:r, 1, 0:1], ACT.Sqrt).then_inc(hroot, 1)
                if t + 2 < NT:
                    root(t + 2)
                if t >= 1:
                    route(t - 1)
            route(NT - 1)
            act.wait_ge(lclear, 1)
            nc.scalar.activation(ro[:, :, 0:5], ro[:, :, 0:5], ACT.Exp).then_inc(lexp, 1)

        @block.vector
        def _(dve):
            ch = Chain(dve, steps)
            dve.wait_ge(consts_in, 64)
            dve.wait_ge(cleared, 4)

            def first_top(dst, src, order, n, tmp):
                wide = lambda a: a.broadcast_to([P, NT, n])
                ranks = wide(self.c(order, n).unsqueeze(1))
                ch.then(nc.vector.tensor_reduce(tmp[:, :, 0:1], src, AX.X, ALU.max))
                ch.then(nc.vector.tensor_tensor(dst, src, wide(tmp[:, :, 0:1]), ALU.is_equal))
                ch.then(nc.vector.tensor_tensor(dst, dst, ranks, ALU.mult))
                ch.then(nc.vector.tensor_reduce(tmp[:, :, 1:2], dst, AX.X, ALU.max))
                ch.then(nc.vector.tensor_tensor(dst, ranks, wide(tmp[:, :, 1:2]), ALU.is_equal))

            def pooled(t):
                r = ROWS[t]
                dve.wait_ge(r_in_psum, t + 1)
                nc.vector.tensor_copy(rT[:, :, 0:r], ps[0:64, 0, :].rearrange("p (w t) -> p w t", w=4)[:, :, 0:r]).then_inc(r_ready, 1)

            def pool_out(t):
                r = ROWS[t]
                dve.wait_ge(r_in_psum, min(t + 2, NT))
                dve.wait_ge(y_in_psum, t + 1)
                nc.vector.tensor_tensor(z[0:r, t, U0:U0 + 256], ps[0:r, 1, 0:256], sp_[0:r, :], ALU.mult).then_inc(y_out, 1)

            def norm_mix(t):
                r = ROWS[t]
                ot = o[:, t, :] if t < TILES else self.o_s[:, :]
                if t >= 2:
                    dve.wait_ge(mT_in_psum, t - 1)
                dve.wait_ge(y_out, t + 1)
                s = sq[0:r, 0, :]
                parts = ((z[0:r, t, U0:U0 + 256], 0, 256), (ot[0:r, 0:512], 256, 512), (ot[0:r, 512:768], 768, 256))
                for j, (a, at, n) in enumerate(parts):
                    ch.then(nc.vector.tensor_tensor_reduce(junk[0:r, 0:n], a, a, 1.0, 0.0, ALU.mult, ALU.add, s[:, j:j + 1]))
                for j, (a, at, n) in enumerate(parts):
                    ins = nc.vector.tensor_scalar(s[:, j:j + 1], s[:, j:j + 1], 1.0 / n, EPS, ALU.mult, ALU.add)
                ins.then_inc(ms_ready, 1)
                dve.wait_ge(root_ready, t + 1)
                ch.then(nc.vector.reciprocal(s[:, 3:6], s[:, 3:6]))
                for j, (a, at, n) in enumerate(parts):
                    ins = nc.vector.scalar_tensor_tensor(mixed[0:r, t % 2, at:at + n], a, s[:, 3 + j:4 + j], gm[0:r, at:at + n], ALU.mult, ALU.mult)
                ins.then_inc(mixed_ready, 1)

            def norm_h(t):
                r = ROWS[t]
                dve.wait_ge(h_in_psum, t + 1 if t < TILES else TILES + 4)
                dve.wait_ge(x_in[t % 2], 16 * (t // 2 + 1))
                if t >= 2:
                    dve.wait_ge(stored[t % 2], 32 * (t // 2))
                if t < TILES:
                    nc.vector.tensor_tensor(h[0:r, t % 2, :].rearrange("p (a n) -> p a n", a=2), ps[0:r, 4:6, :],
                                            xin[0:r, t % 2, :].rearrange("p (a n) -> p a n", a=2), ALU.add).then_inc(h_read, 1)
                else:
                    dve.wait_ge(h_copied, 1)
                    nc.vector.tensor_tensor(h[0:r, t % 2, :], mixed[0:r, t % 2, :], xin[0:r, t % 2, :], ALU.add).then_inc(h_read, 1)
                dve.wait_ge(h_read, t + 1)
                ch.then(nc.vector.tensor_tensor_reduce(hn[0:r, t % 2, :], h[0:r, t % 2, :], h[0:r, t % 2, :], 1.0, 0.0, ALU.mult, ALU.add, sq[0:r, 1, 2:3]))
                nc.vector.tensor_scalar(sq[0:r, 1, 0:1], sq[0:r, 1, 2:3], 1.0 / D, EPS, ALU.mult, ALU.add).then_inc(hms, 1)
                dve.wait_ge(hroot, t + 1)
                ch.then(nc.vector.reciprocal(sq[0:r, 1, 3:4], sq[0:r, 1, 1:2]))
                nc.vector.scalar_tensor_tensor(hn[0:r, t % 2, :], h[0:r, t % 2, :], sq[0:r, 1, 3:4], gf[0:r, :], ALU.mult, ALU.mult).then_inc(hn_ready, 1)

            def logits(t):
                dve.wait_ge(l_in_psum, t + 1)
                nc.vector.tensor_tensor(lg[0:ROWS[t], t, :], ps[0:ROWS[t], 6, 0:36], br[0:ROWS[t], :], ALU.add).then_inc(l_out, 1)

            pooled(0)
            for t in range(NT):
                if t + 1 < NT:
                    pooled(t + 1)
                pool_out(t)
                if t == 0:
                    norm_mix(0)
            norm_mix(1)
            for t in range(NT):
                norm_h(t)
                if t + 2 < NT:
                    norm_mix(t + 2)
                if t >= 1:
                    logits(t - 1)
            logits(NT - 1)

            dve.wait_ge(l_out, NT)
            f = lambda a, n: ro[:, :, a:a + n]
            L = lg[:, :, :]
            low = prod[:, :, 0, :].rearrange("p t (g e) -> p t g e", g=4)
            first_top(f(8, 4), L[:, :, 0:4], C_G4, 4, f(48, 2))
            ch.then(nc.vector.tensor_tensor(f(0, 4), L[:, :, 0:4], f(48, 1).broadcast_to([P, NT, 4]), ALU.subtract))
            ch.then(nc.vector.tensor_tensor(low, L[:, :, 4:36].rearrange("p t (g e) -> p t g e", g=4),
                                            f(8, 4).unsqueeze(3).broadcast_to([P, NT, 4, 8]), ALU.mult))
            ch.then(nc.vector.tensor_reduce(f(16, 8), low.rearrange("p t g e -> p t e g"), AX.X, ALU.add))
            first_top(f(24, 8), f(16, 8), C_E8, 8, f(50, 2))
            ch.then(nc.vector.scalar_tensor_tensor(f(40, 8), f(24, 8), NEG, f(16, 8), ALU.mult, ALU.add))
            first_top(f(32, 8), f(40, 8), C_E8, 8, f(52, 2))
            nc.vector.tensor_tensor(f(4, 1), f(52, 1), f(50, 1), ALU.subtract).then_inc(lclear, 1)
            for k in range(2):
                ins = nc.vector.tensor_tensor(one[:, :, k, :].rearrange("p t (g e) -> p t g e", g=4), f(8, 4).unsqueeze(3).broadcast_to([P, NT, 4, 8]),
                                              f(24 + 8 * k, 8).unsqueeze(2).broadcast_to([P, NT, 4, 8]), ALU.mult)
            ch.then(ins)
            nc.vector.tensor_tensor(both[:, :, :], one[:, :, 0, :], one[:, :, 1, :], ALU.add).then_inc(pair_ready, 1)
            pw = self.pair_w
            dve.wait_ge(lexp, 1)
            ch.then(nc.vector.tensor_reduce(f(54, 1), f(0, 4), AX.X, ALU.add))
            ch.then(nc.vector.tensor_scalar(f(55, 1), f(4, 1), 1.0, None, ALU.add))
            ch.then(nc.vector.tensor_tensor(f(54, 1), f(54, 1), f(55, 1), ALU.mult))
            ch.then(nc.vector.reciprocal(pw[:, :, 0:1], f(54, 1)))
            nc.vector.tensor_tensor(pw[:, :, 1:2], pw[:, :, 0:1], f(4, 1), ALU.mult)

            v = lambda j: place[:, j, :]
            one3 = one[:, :, :, :].rearrange("p t k e -> p (t k) e")
            prod3 = prod[:, :, :, :].rearrange("p t k e -> p (t k) e")
            RANK, EXP, BASE, QQ, SLOT, TILE = range(6)
            experts = self.c(C_EI, NEXP)
            ch.then(nc.vector.tensor_tensor(prod3, one3, experts.unsqueeze(1).broadcast_to([P, 2 * NT, NEXP]), ALU.mult))
            ch.then(nc.vector.tensor_reduce(v(EXP), prod3, AX.X, ALU.add))
            dve.wait_ge(cnt_in_psum, 1)
            nc.vector.tensor_copy(cnt[:, 0:TILES, :], ps[:, 7, 0:TILES * NEXP].rearrange("p (t e) -> p t e", t=TILES))
            nc.vector.tensor_copy(cnt[0:NB, TILES, :], ps[0:NB, 7, TILES * NEXP:NT * NEXP])
            ch.then(nc.vector.tensor_copy(cnt[:, NT, :], ps[:, 7, NT * NEXP:(NT + 1) * NEXP]))
            over, a, b = scan[:, 0, :], scan[:, 1, :], scan[:, 2, :]
            steps_of = self.c(C_CAP, QMAX)
            many = hn[:, 0, 0:NEXP * QMAX].rearrange("p (e q) -> p e q", q=QMAX)
            dve.wait_ge(hT_in_psum, NT)
            dve.wait_ge(stored[0], 32 * ((NT + 1) // 2))
            ch.then(nc.vector.tensor_tensor(many, cnt[:, NT, :].unsqueeze(2).broadcast_to([P, NEXP, QMAX]),
                                            steps_of.unsqueeze(1).broadcast_to([P, NEXP, QMAX]), ALU.is_gt))
            ch.then(nc.vector.tensor_reduce(over, many, AX.X, ALU.add))
            ch.then(nc.vector.tensor_copy(a, over))
            d = 1
            while d < NEXP:
                nc.vector.tensor_copy(b[:, 0:d], a[:, 0:d])
                ch.then(nc.vector.tensor_tensor(b[:, d:NEXP], a[:, d:NEXP], a[:, 0:NEXP - d], ALU.add))
                a, b = b, a
                d *= 2
            ch.then(nc.vector.tensor_tensor(b, a, over, ALU.subtract))
            ch.then(nc.vector.tensor_tensor(b, b, experts, ALU.subtract))
            for k in range(2):
                ins = nc.vector.tensor_tensor(prod[:, :, k, :], one[:, :, k, :], cnt[:, 0:NT, :], ALU.mult)
            ch.then(ins)
            ch.then(nc.vector.tensor_reduce(v(RANK), prod3, AX.X, ALU.add))
            ch.then(nc.vector.tensor_tensor(prod3, one3, b.unsqueeze(1).broadcast_to([P, 2 * NT, NEXP]), ALU.mult))
            ch.then(nc.vector.tensor_reduce(v(BASE), prod3, AX.X, ALU.add))
            many = hn[:, 0, 0:2 * NT * QMAX].rearrange("p (n q) -> p n q", q=QMAX)
            ch.then(nc.vector.tensor_tensor(many, v(RANK).unsqueeze(2).broadcast_to([P, 2 * NT, QMAX]),
                                            steps_of.unsqueeze(1).broadcast_to([P, 2 * NT, QMAX]), ALU.is_ge))
            ch.then(nc.vector.tensor_reduce(v(QQ), many, AX.X, ALU.add))
            ch.then(nc.vector.scalar_tensor_tensor(v(SLOT), v(QQ), -float(CAP), v(RANK), ALU.mult, ALU.add))
            ch.then(nc.vector.scalar_tensor_tensor(v(TILE), v(QQ), float(NEXP - 1), v(BASE), ALU.add, ALU.add))
            ch.then(nc.vector.scalar_tensor_tensor(v(TILE), v(QQ), 1.0, v(TILE), ALU.min, ALU.mult))
            ch.then(nc.vector.tensor_tensor(v(TILE), v(TILE), v(EXP), ALU.add))
            dve.wait_ge(mT_in_psum, NT)
            nc.vector.tensor_tensor(slot_hot, v(SLOT).unsqueeze(2).broadcast_to([P, 2 * NT, CAP]),
                                    self.c(C_EI, CAP).unsqueeze(1).broadcast_to([P, 2 * NT, CAP]), ALU.is_equal)
            ch.then(nc.vector.tensor_tensor(tile_tok, v(TILE).unsqueeze(2).broadcast_to([P, 2 * NT, NTILE]),
                                            self.c(C_EI, NTILE).unsqueeze(1).broadcast_to([P, 2 * NT, NTILE]), ALU.is_equal))
            tok2 = self.c(C_TOK, NT).unsqueeze(2).broadcast_to([P, NT, 2 * NTILE])
            nc.vector.tensor_tensor(tile_tok.rearrange("p (t k) s -> p t (k s)", k=2), tile_tok.rearrange("p (t k) s -> p t (k s)", k=2),
                                    tok2, ALU.mult).then_inc(hot_ready, 1)
            ch.then(nc.vector.scalar_tensor_tensor(v(BASE), v(TILE), float(CAP), v(SLOT), ALU.mult, ALU.add))
            nc.vector.tensor_copy(self.pair_row[:, :], v(BASE))
            nc.vector.tensor_copy(self.n_over[:, :], a[0:1, NEXP - 1:NEXP])
            ch.then(nc.vector.tensor_tensor(last[:, :, :], a[0:1, :].unsqueeze(1).broadcast_to([1, NOVER, NEXP]),
                                            self.c(C_EI, NOVER, 1).unsqueeze(2).broadcast_to([1, NOVER, NEXP]), ALU.is_le))
            ch.then(nc.vector.tensor_reduce(prod[0:1, 0, 0, 0:NOVER], last[:, :, :], AX.X, ALU.add))
            ch.then(nc.vector.tensor_scalar(self.over_e[:, :], prod[0:1, 0, 0, 0:NOVER], float(NEXP - 1), None, ALU.min))
            dve.wait_ge(table_in_psum, 1)
            nc.vector.tensor_copy(self.table[:, :], ps[0:CAP, 0, 0:NTILE])

        self.close(st)

    def expert_slot(self, w):
        n = KD * FF
        return (w[:, 0:n].rearrange("p (k f) -> p k f", k=KD), w[:, n:2 * n].rearrange("p (k f) -> p k f", k=KD),
                w[:, 2 * n:3 * n].rearrange("p (h j d) -> p h j d", h=2, d=D))

    def load_gate_up(self, sp, n, slot, to):
        for name, w, sems in zip(("w_gate", "w_up"), to, self.weights_in):
            src = self.ins[name].rearrange("(e p k) f -> e p k f", p=P, k=KD)
            sp.dma_start(w, src[bass.ds(n, 1), :, :, :].rearrange("e p k f -> (e p) k f")).then_inc(sems[slot], 16)

    def load_down(self, sp, n, slot, w):
        src = self.ins["w_down"].rearrange("(e h p j) d -> e p h j d", h=2, p=P, j=KF // 2)
        sp.dma_start(w, src[bass.ds(n, 1), :, :, :, :].rearrange("e p h j d -> (e p) h j d")).then_inc(self.weights_in[2][slot], 16)

    def experts(self):
        nc, I = self.nc, self.ins
        st = ExitStack()
        S = lambda n: self.sem(n, st)
        ps = self.ps
        FH = FF // 2
        w1 = self.sb("we", [P, 12288], stack=st)
        wg, wu, wd = zip(self.expert_slot(self.w0), self.expert_slot(w1))
        xg = self.sb("xg", [CAP, 2, D], stack=st)
        xT = self.sb("xTe", [P, 2, KD, CAP], stack=st)
        gc = self.sb("gc", [2 * CAP, 2, FF // 2], stack=st)
        hh = self.sb("hh", [2 * CAP, 2, FF // 2], stack=st)
        hT = self.sb("hTe", [P, KF // 2, 2 * CAP], stack=st)
        yb = self.sb("yb", [2 * CAP, 2, D // 2], stack=st)
        g_in, u_in, d_in = self.weights_in
        xg_in, y_out = ([S(f"{n}{j}") for j in range(2)] for n in ("xg_in", "y_out"))
        (x_turned, xT_ready, gate_done, up_done, gc_ready, ge_ready, hh_ready, h_turned, hT_ready, y_in_psum, y_copied, steps) = (
            S(n) for n in ("x_turned", "xTe_ready", "gate_done", "up_done", "gc_ready", "ge_ready", "hh_ready",
                           "h_turned", "hTe_ready", "ye_in_psum", "y_copied", "experts_dve"))
        ys = self.ys_dram.rearrange("(n s) d -> n s d", s=CAP)
        block = st.enter_context(nc.Block("experts"))

        @block.sync
        def _(sp):
            self.load_gate_up(sp, 1, 1, (wg[1], wu[1]))
            self.load_down(sp, 1, 1, wd[1])
            with sp.Fori(1, NEXP // 2) as i:
                for slot in range(2):
                    sp.wait_ge(up_done, i * 4 + 2 * (slot - 1))
                    self.load_gate_up(sp, i * 2 + slot, slot, (wg[slot], wu[slot]))
                    sp.wait_ge(y_in_psum, i * 4 + 2 * (slot - 1))
                    self.load_down(sp, i * 2 + slot, slot, wd[slot])

        @block.gpsimd
        def _(pool):

            for n in range(NEXP):
                if n >= 2:
                    pool.wait_ge(x_turned, n - 1)
                pool.indirect_dma_start(out=xg[:, n % 2, :], out_offset=None, in_=self.hn_dram,
                                        in_offset=bass.IndirectOffsetOnAxis(ap=self.table[:, n:n + 1].bitcast(U32), axis=0)).then_inc(xg_in[n % 2], 16)

        @block.tensor
        def _(pe):
            def turn(out, rows, chunks):
                m, w = rows.shape
                ident = self.consts[0:m, C_ID:C_ID + m]
                for k in range(chunks):
                    dst, src = ps[:, out, m * k:m * k + m], rows[:, k:w:chunks]
                    if k == 0:
                        ins = nc.tensor.matmul(dst, src, ident, start=True, stop=True)
                    else:
                        ins = nc.tensor.transpose(dst, src, ident)
                return ins

            def gate_up(n, slot, half):
                pe.wait_ge(xT_ready, n + 1)
                for w, sem, bank, done in ((wg, g_in, slot, gate_done), (wu, u_in, 2 + slot, up_done)):
                    pe.wait_ge(sem[slot], half * 16)
                    for k in range(KD):
                        for h in range(2):
                            ins = nc.tensor.matmul(ps[h * CAP:h * CAP + CAP, bank, 0:FH], xT[:, slot, k, :], w[slot][:, k, h * FH:h * FH + FH],
                                                   start=(k == 0), stop=(k == KD - 1))
                            if k == KD - 1:
                                ins.then_inc(done, 1)

            def turn_x(n, slot, half, first=False):
                pe.wait_ge(xg_in[slot], half * 16)
                if not first:
                    pe.wait_ge(xT_ready, n)
                turn(4, xg[:, slot, :], KD).then_inc(x_turned, 1)

            def down(n, slot, half, first=False):
                pe.wait_ge(hT_ready, n + 1)
                pe.wait_ge(d_in[slot], half * 16)
                if not first:
                    pe.wait_ge(y_copied, n)
                for k in range(KF):
                    h, j = k // (KF // 2), k % (KF // 2)
                    for a in range(2):
                        ins = nc.tensor.matmul(ps[a * CAP:a * CAP + CAP, 6 + slot, :], hT[:, j, h * CAP:h * CAP + CAP], wd[slot][:, h, j, 512 * a:512 * a + 512],
                                               start=(k == 0), stop=(k == KF - 1))
                        if k == KF - 1:
                            ins.then_inc(y_in_psum, 1)

            def turn_h(n, slot):
                pe.wait_ge(hh_ready, n + 1)
                turn(5, hh[:, slot, :], KF // 2).then_inc(h_turned, 1)

            turn_x(0, 0, 1, first=True)
            gate_up(0, 0, 1)
            turn_x(1, 1, 1)
            turn_h(0, 0)
            gate_up(1, 1, 1)
            turn_x(2, 0, 2)
            down(0, 0, 1, first=True)
            turn_h(1, 1)
            with pe.Fori(1, NEXP // 2 - 1) as i:
                for slot in range(2):
                    n = i * 2 + slot
                    gate_up(n, slot, i + 1)
                    turn_x(n + 1, 1 - slot, i + 1 + slot)
                    down(n + (-1), 1 - slot, i + slot)
                    turn_h(n, slot)
            n, half = NEXP - 2, NEXP // 2
            gate_up(n, 0, half)
            turn_x(n + 1, 1, half)
            down(n - 1, 1, half - 1)
            turn_h(n, 0)
            gate_up(n + 1, 1, half)
            down(n, 0, half)
            turn_h(n + 1, 1)
            down(n + 1, 1, half)

        @block.vector
        def _(dve):
            def link(ins, count):
                ins.then_inc(steps, 1)
                dve.wait_ge(steps, count)

            def take_x(n, slot):
                dve.wait_ge(x_turned, n + 1)
                nc.vector.tensor_copy(xT[:, slot, :, :].rearrange("p k s -> p (k s)"), ps[:, 4, 0:KD * CAP]).then_inc(xT_ready, 1)

            def act_fn(n, slot):
                g, u = ps[0:2 * CAP, slot, 0:FH], ps[0:2 * CAP, 2 + slot, 0:FH]
                dve.wait_ge(gate_done, n * 2 + 2)
                nc.vector.tensor_scalar(gc[:, slot, :], g, -80.0, None, ALU.max).then_inc(gc_ready, 1)
                dve.wait_ge(ge_ready, n + 1)
                link(nc.vector.tensor_scalar(gc[:, slot, :], gc[:, slot, :], 1.0, None, ALU.add), n * 3 + 1)
                link(nc.vector.reciprocal(gc[:, slot, :], gc[:, slot, :]), n * 3 + 2)
                link(nc.vector.tensor_tensor(gc[:, slot, :], gc[:, slot, :], g, ALU.mult), n * 3 + 3)
                dve.wait_ge(up_done, n * 2 + 2)
                nc.vector.tensor_tensor(hh[:, slot, :], gc[:, slot, :], u, ALU.mult).then_inc(hh_ready, 1)

            def take_h(n):
                dve.wait_ge(h_turned, n + 1)
                nc.vector.tensor_copy(hT[:, :, :].rearrange("p k s -> p (k s)"), ps[:, 5, 0:KF * CAP]).then_inc(hT_ready, 1)

            take_x(0, 0)
            take_x(1, 1)
            act_fn(0, 0)
            take_h(0)
            take_x(2, 0)
            act_fn(1, 1)
            take_h(1)
            take_x(3, 1)
            act_fn(2, 0)
            take_h(2)
            with dve.Fori(1, NEXP // 2 - 1) as i:
                for s in range(2):
                    n = i * 2 + (1 + s)
                    slot = (1 + s) % 2
                    take_x(n + 1, 1 - slot)
                    act_fn(n, slot)
                    take_h(n)
            n = NEXP - 1
            act_fn(n, 1)
            take_h(n)

        @block.scalar
        def _(act):
            def exp(n, slot):
                act.wait_ge(gc_ready, n + 1)
                nc.scalar.activation(gc[:, slot, :], gc[:, slot, :], ACT.Exp, scale=-1.0).then_inc(ge_ready, 1)

            def take_y(n, slot, uses):
                act.wait_ge(y_in_psum, n * 2 + 2)
                if uses is not None:
                    act.wait_ge(y_out[slot], uses * 32)
                nc.scalar.copy(yb[:, slot, :], ps[0:2 * CAP, 6 + slot, :]).then_inc(y_copied, 1)
                act.wait_ge(y_copied, n + 1)
                for h in range(2):
                    act.dma_start(ys[bass.ds(n, 1), :, 512 * h:512 * h + 512].rearrange("o s d -> (o s) d"), yb[h * CAP:h * CAP + CAP, slot, :]).then_inc(y_out[slot], 16)

            exp(0, 0)
            exp(1, 1)
            take_y(0, 0, None)
            exp(2, 0)
            take_y(1, 1, None)
            with act.Fori(1, NEXP // 2 - 1) as i:
                for s in range(2):
                    n = i * 2 + (1 + s)
                    slot = (1 + s) % 2
                    exp(n, slot)
                    take_y(n + (-1), 1 - slot, i)
            n = NEXP - 1
            exp(n, 1)
            take_y(n - 1, 0, NEXP // 2 - 1)
            take_y(n, 1, NEXP // 2 - 1)
            for slot in range(2):
                act.wait_ge(y_out[slot], 32 * (NEXP // 2))

        self.close(st)

    def overflow(self):
        nc, I = self.nc, self.ins
        st = ExitStack()
        S = lambda n: self.sem(n, st)
        ps = self.ps
        wg = self.sb("wgo", [P, KD, FF], stack=st)
        wu = self.sb("wuo", [P, KD, FF], stack=st)
        wd = self.sb("wdo", [P, KF, D], stack=st)
        xg = self.sb("xgo", [CAP, D], stack=st)
        xT = self.sb("xTo", [P, KD, CAP], stack=st)
        gc = self.sb("gco", [CAP, FF], stack=st)
        hh = self.sb("hho", [CAP, FF], stack=st)
        hT = self.sb("hTo", [P, KF, CAP], stack=st)
        yb = self.sb("ybo", [CAP, D], stack=st)
        (tile_free, w_in, xg_in, x_turned, xT_ready, gate_up, gc_ready, ge_ready, a1, a2, a3, hh_ready, h_turned, hT_ready,
         y_in_psum, y_ready, y_out) = (S(n) for n in (
             "tile_free", "o_w_in", "o_xg_in", "o_x_turned", "o_xT", "o_gate_up", "o_gc", "o_ge", "o_a1", "o_a2", "o_a3",
             "o_hh", "o_h_turned", "o_hT", "o_y_psum", "o_y_ready", "o_y_out"))
        vg = I["w_gate"].rearrange("(e p k) f -> e p k f", p=P, k=KD)
        vu = I["w_up"].rearrange("(e p k) f -> e p k f", p=P, k=KD)
        vd = I["w_down"].rearrange("(e p k) f -> e p k f", p=P, k=KF)
        ys = self.ys_dram.rearrange("(n s) d -> n s d", s=CAP)
        at = lambda v, n: v[bass.ds(n, 1), :, :, :].rearrange("e p k f -> (e p) k f")

        def needed(eng):
            return eng.If(eng.value_load(self.n_over[0:1, 0:1], min_val=0, max_val=NOVER) > 0)

        block = st.enter_context(nc.Block("overflow"))

        @block.sync
        def _(sp):
            with needed(sp):
                with sp.Fori(0, NOVER) as j:
                    sp.wait_ge(tile_free, j + 1)
                    e = sp.value_load(self.over_e[0:1, bass.ds(j, 1)], min_val=0, max_val=NEXP - 1)
                    sp.dma_start(wg[:, :, :], at(vg, e)).then_inc(w_in, 16)
                    sp.dma_start(wu[:, :, :], at(vu, e)).then_inc(w_in, 16)
                    sp.dma_start(wd[:, :, :], at(vd, e)).then_inc(w_in, 16)

        @block.gpsimd
        def _(pool):
            with needed(pool):
                pool.sem_inc(tile_free, 1)
                for j in range(NOVER):
                    pool.indirect_dma_start(out=xg[:, :], out_offset=None, in_=self.hn_dram,
                                            in_offset=bass.IndirectOffsetOnAxis(ap=self.table[:, NEXP + j:NEXP + j + 1].bitcast(U32), axis=0)).then_inc(xg_in, 16)
                    pool.wait_ge(y_out, 16 * (j + 1))
                    pool.sem_inc(tile_free, 1)

        @block.tensor
        def _(pe):
            ident = self.consts[0:CAP, C_ID:C_ID + CAP]

            def turn(out, rows, chunks):
                w = rows.shape[-1]
                for k in range(chunks):
                    dst, src = ps[:, out, CAP * k:CAP * k + CAP], rows[:, k:w:chunks]
                    if k == 0:
                        ins = nc.tensor.matmul(dst, src, ident, start=True, stop=True)
                    else:
                        ins = nc.tensor.transpose(dst, src, ident)
                return ins

            with needed(pe):
                with pe.Fori(0, NOVER) as j:
                    pe.wait_ge(xg_in, j * 16 + 16)
                    turn(4, xg[:, :], KD).then_inc(x_turned, 1)
                    pe.wait_ge(xT_ready, j + 1)
                    pe.wait_ge(w_in, j * 48 + 48)
                    for a, w in enumerate((wg, wu)):
                        for k in range(KD):
                            ins = nc.tensor.matmul(ps[0:CAP, a, :], xT[:, k, :], w[:, k, :], start=(k == 0), stop=(k == KD - 1))
                    ins.then_inc(gate_up, 1)
                    pe.wait_ge(hh_ready, j + 1)
                    turn(5, hh[:, :], KF).then_inc(h_turned, 1)
                    pe.wait_ge(hT_ready, j + 1)
                    for a in range(2):
                        for k in range(KF):
                            ins = nc.tensor.matmul(ps[0:CAP, 6 + a, :], hT[:, k, :], wd[:, k, 512 * a:512 * a + 512], start=(k == 0), stop=(k == KF - 1))
                    ins.then_inc(y_in_psum, 1)

        @block.vector
        def _(dve):
            with needed(dve):
                with dve.Fori(0, NOVER) as j:
                    dve.wait_ge(x_turned, j + 1)
                    nc.vector.tensor_copy(xT[:, :, :].rearrange("p k s -> p (k s)"), ps[:, 4, 0:KD * CAP]).then_inc(xT_ready, 1)
                    dve.wait_ge(gate_up, j + 1)
                    nc.vector.tensor_scalar(gc[:, :], ps[0:CAP, 0, :], -80.0, None, ALU.max).then_inc(gc_ready, 1)
                    dve.wait_ge(ge_ready, j + 1)
                    nc.vector.tensor_scalar(gc[:, :], gc[:, :], 1.0, None, ALU.add).then_inc(a1, 1)
                    dve.wait_ge(a1, j + 1)
                    nc.vector.reciprocal(gc[:, :], gc[:, :]).then_inc(a2, 1)
                    dve.wait_ge(a2, j + 1)
                    nc.vector.tensor_tensor(gc[:, :], gc[:, :], ps[0:CAP, 0, :], ALU.mult).then_inc(a3, 1)
                    dve.wait_ge(a3, j + 1)
                    nc.vector.tensor_tensor(hh[:, :], gc[:, :], ps[0:CAP, 1, :], ALU.mult).then_inc(hh_ready, 1)
                    dve.wait_ge(h_turned, j + 1)
                    nc.vector.tensor_copy(hT[:, :, :].rearrange("p k s -> p (k s)"), ps[:, 5, 0:KF * CAP]).then_inc(hT_ready, 1)
                    dve.wait_ge(y_in_psum, j + 1)
                    nc.vector.tensor_copy(yb[:, :].rearrange("p (a n) -> p a n", a=2), ps[0:CAP, 6:8, :]).then_inc(y_ready, 1)

        @block.scalar
        def _(act):
            with needed(act):
                with act.Fori(0, NOVER) as j:
                    act.wait_ge(gc_ready, j + 1)
                    nc.scalar.activation(gc[:, :], gc[:, :], ACT.Exp, scale=-1.0).then_inc(ge_ready, 1)
                    act.wait_ge(y_ready, j + 1)
                    act.dma_start(ys[bass.ds(j + NEXP, 1), :, :].rearrange("o s d -> (o s) d"), yb[:, :]).then_inc(y_out, 16)

        self.close(st)

    def combine(self):
        nc, O = self.nc, self.outs
        st = ExitStack()
        S = lambda n: self.sem(n, st)
        NT = TILES + 1
        rows = self.sb("rows", [P, NT, 2, D], stack=st)
        h = self.sb("h7", [P, NT, D], stack=st)
        rows_in = [S(f"rows_in{t}") for t in range(NT)]
        h_in = S("h_in")
        steps, y_ready, stored = S("combine_dve"), S("y_ready"), S("y_stored")
        block = st.enter_context(nc.Block("combine"))

        @block.gpsimd
        def _(pool):
            for t in range(NT):
                for k in range(2):
                    pool.indirect_dma_start(out=rows[0:ROWS[t], t, k, :], out_offset=None, in_=self.ys_dram,
                                            in_offset=bass.IndirectOffsetOnAxis(ap=self.pair_row[0:ROWS[t], 2 * t + k:2 * t + k + 1].bitcast(U32), axis=0)).then_inc(rows_in[t], 16)
            pool.wait_ge(self.moved, 32)
            pool.wait_ge(self.blanked, 16)

        @block.vector
        def _(dve):
            ch = Chain(dve, steps)
            dve.wait_ge(h_in, 16 * NT)
            for t in range(NT):
                r = ROWS[t]
                dve.wait_ge(rows_in[t], 32)
                ch.then(nc.vector.scalar_tensor_tensor(h[0:r, t, :], rows[0:r, t, 0, :], self.pair_w[0:r, t, 0:1], h[0:r, t, :], ALU.mult, ALU.add))
                nc.vector.scalar_tensor_tensor(h[0:r, t, :], rows[0:r, t, 1, :], self.pair_w[0:r, t, 1:2], h[0:r, t, :], ALU.mult, ALU.add).then_inc(y_ready, 1)

        @block.sync
        def _(sp):
            for t in range(NT):
                sp.dma_start(h[0:ROWS[t], t, :], self.h_dram[t * P:t * P + ROWS[t], :]).then_inc(h_in, 16)
            for t in range(NT):
                sp.wait_ge(y_ready, t + 1)
                sp.dma_start(O["y"][t * P:t * P + ROWS[t], :], h[0:ROWS[t], t, :]).then_inc(stored, 16)
            sp.wait_ge(stored, 16 * NT)

        self.close(st)

    def run(self):
        nc = self.nc
        sb = self.sb
        with self.stack:
            self.moved = self.sem("moved", self.stack)
            self.blanked = self.sem("blanked", self.stack)
            self.pages = sb("pages", [1, NB * NB], I32)
            self.w0 = sb("w0", [P, 12288])
            self.raw = self.w0[:, 0:8192].rearrange("p (s a b c) -> p s a b c", s=2, a=4, b=2)
            self.w1 = self.w0[:, 8192:12288].rearrange("p (q l n) -> p q l n", q=2, l=16)
            self.kv_in = [self.sem(f"kv_in{j}", self.stack) for j in range(2)]
            self.weights_in = [[self.sem(f"{n}_in{j}", self.stack) for j in range(2)] for n in ("wg", "wu", "wd")]
            self.pages_in, self.w1_in = self.sem("pages_in", self.stack), self.sem("w1_in", self.stack)
            self.ps = self.stack.enter_context(nc.psum_tensor("ps", [P, 8, 512], F32))
            self.pz = self.ps[:, 0:4, :]
            self.pt = self.ps[:, 4:6, :].rearrange("p a (k t) -> p (a k) t", t=P)
            self.gate_dram = nc.dram_tensor("gate_dram", [NB, 24], F32).ap()
            self.h_dram = nc.dram_tensor("h_dram", [NTOK, D], F32).ap()
            self.hn_dram = nc.dram_tensor("hn_dram", [NTOK, D], F32).ap()
            self.ys_dram = nc.dram_tensor("ys_dram", [CAP * NTILE, D], F32).ap()
            self.consts = sb("consts", [P, CW])
            self.table = sb("table", [CAP, NTILE], I32)
            self.pair_w = sb("pair_w", [P, TILES + 1, 2])
            self.pair_row = sb("pair_row", [P, 2 * (TILES + 1)], I32)
            self.over_e = sb("over_e", [1, NOVER], I32)
            self.n_over = sb("n_over", [1, 1], I32)
            with ExitStack() as front:
                self.z = sb("z", [P, TILES + 1, ZW], stack=front)
                self.o_s = sb("o_s", [NB, 768], stack=front)
                with ExitStack() as blocks:
                    self.kcT = sb("kcT", [P, NSEQ, 64], stack=blocks)
                    self.vc = sb("vc", [64, NSEQ, 128], stack=blocks)
                    self.project()
                    self.stream()
                    self.o = sb("o", [P, TILES, 768], stack=blocks)
                    self.alloc_mix(blocks)
                    self.attend()
                    self.mix()
            self.experts()
            self.overflow()
            self.combine()


def kernel(**inputs):
    import numpy as np
    import concourse.bacc as bacc
    from concourse.bass_utils import run_bass_kernel_spmd

    f = {k: np.asarray(v) for k, v in inputs.items()}
    heads = [g * R + r for r in range(R) for g in range(G)]
    col = lambda base, unit, order: [base + o * unit + j for o in order for j in range(unit)]
    kv = 768
    order = (list(range(256)) + col(256, HD, heads)
             + [kv + ((br * 2 + 0) * G + g) * HD + j for br in range(3) for g in range(G) for j in range(HD)]
             + list(range(1560, 1816))
             + [kv + ((br * 2 + 1) * G + g) * HD + j for br in range(3) for g in range(G) for j in range(HD)]
             + [1536 + h * 3 + br for br in range(3) for h in heads])
    mixed = list(range(256)) + col(256, HD, heads) + list(range(768, 1024))
    arrays = {
        "consts": constants()[0], "bands": constants()[1],
        "x": np.concatenate([f["x_prompt"][0], f["x_sample"][:, 0]], 0),
        "mem": f["mem_prompt"][0],
        "w_in": f["w_in"][0][:, order],
        "w_mem": f["w_mem_kv"][0],
        "g_rows": np.concatenate([f["g_attn"], f["g_mem"]], 0),
        "g_head": np.concatenate([np.tile(f["g_q"][0], H), np.repeat(f["g_k"][0][:, None], G, 1).reshape(-1),
                                  np.tile(f["g_mq"][0], MH), np.tile(f["g_mk"][0], MH)]),
        "cache_kv": f["cache_kv"][0].reshape(-1, 512),
        "cache_win": f["cache_win"][0].reshape(-1, 256),
        "cache_mem": f["cache_mem_kv"][0].reshape(-1, 512),
        "state_pool": f["state_pool"][0].reshape(-1, 256),
        "page_table": f["page_table"].reshape(1, -1).astype(np.int32),
        "pe": np.ascontiguousarray(f["pe_cmp"][0].reshape(2, 16, 128).transpose(2, 0, 1)),
        "w_cmp1": f["w_cmp1"][0], "w_cmp2": f["w_cmp2"][0],
        "w_pool": f["w_pool"][0].reshape(-1, 64),
        "w_out": f["w_out"][0][mixed],
        "mix_rows": np.concatenate([f["g_mix"][0][mixed], f["g_ffn"][0], f["s_pool"][0], f["b_router1"][0], f["b_router2"][0].reshape(-1)]),
        "w_router": np.concatenate([f["w_router1"][0], f["w_router2"][0].reshape(D, -1)], 1),
        "w_gate": f["w_gate"][0].reshape(-1, FF), "w_up": f["w_up"][0].reshape(-1, FF),
        "w_down": f["w_down"][0].reshape(-1, D),
    }
    shapes = {
        "y": (NTOK, D), "kv_p": (T, 512), "kv_s": (NB, 512), "win_p": (T, 256), "win_s": (NB * T, 256),
        "pool_p": (STATE, 256), "pool_s": (NB * STATE, 256), "mem_p": (MEM, 512),
    }
    nc = bacc.Bacc("TRN2", target_bir_lowering=False, num_devices=1)
    arrays = {k: np.ascontiguousarray(v) for k, v in arrays.items()}
    ins = {k: nc.dram_tensor(f"in_{k}", v.shape, mybir.dt.from_np(v.dtype), kind="ExternalInput").ap() for k, v in arrays.items()}
    outs = {k: nc.dram_tensor(f"out_{k}", s, F32, kind="ExternalOutput").ap() for k, s in shapes.items()}
    Kernel(nc, ins, outs).run()
    r = run_bass_kernel_spmd(nc, [{f"in_{k}": v for k, v in arrays.items()}], core_ids=[0]).results[0]
    o = {k: r[f"out_{k}"] for k in shapes}
    return (o["y"][:T].reshape(1, T, D), o["y"][T:].reshape(NB, 1, D),
            o["kv_p"].reshape(1, 1, T, 4, 2, 64), o["kv_s"].reshape(1, NB, 1, 4, 2, 64),
            o["win_p"].reshape(1, 1, T, 2, 2, 64), o["win_s"].reshape(1, NB, T, 2, 2, 64),
            o["pool_p"].reshape(1, 1, STATE, 256), o["pool_s"].reshape(1, NB, STATE, 256),
            o["mem_p"].reshape(1, 1, MEM, 2, 4, 64))
```
